# Optimizing a Trainium2 kernel written in Bass

```python
import jax, jax.numpy as jnp
from jax import lax
import numpy as np
import math
import jax
import jax.numpy as jnp

D_MODEL = 1024
BATCH = 1
SEQ = 512
DEPTH = 2

N_EVEN = (DEPTH + 1) // 2
N_ODD = DEPTH // 2
D_PLE = 256
D_FF = 4 * D_MODEL
DN_ALPHA = (2.0 * DEPTH) ** 0.25
DN_BETA = (8.0 * DEPTH) ** -0.25
LN_EPS = 1e-5
NEG = -1e30

A_HEADS = 4
A_DH = D_MODEL // 8
A_W = A_HEADS * A_DH
A_CONV = 4
A_CHUNK = 64

B_HEADS = 8
B_DH = 64
B_W = B_HEADS * B_DH
B_KV = 2
B_HPG = B_HEADS // B_KV
B_KVW = B_KV * B_DH
B_CMP_LEN = 32
B_CMP_STRIDE = 16
B_CMP_HID = 128
B_SEL_BLK = 64
B_SEL_N = 16
B_WIN = 512
B_QBLK = 64

C_HEADS = 8
C_DN = 128
C_DR = 64
C_DV = 128
C_QL = 512
C_KVL = 256
C_IDX_HEADS = 8
C_IDX_DH = 64
C_IDX_DR = 32
C_TOPK = 256
C_QBLK = 128
ROPE_BASE = 10000.0

EVEN_SIZES = (A_W, A_W, A_W, A_W, A_HEADS, A_HEADS, B_W, B_KVW, B_KVW, B_KVW, B_KVW, B_KVW, B_KVW, 3 * B_HEADS)
ODD_SIZES = (C_QL, C_KVL, C_DR, C_IDX_DH, C_IDX_HEADS)


def _split(z, sizes):
    out, o = [], 0
    for s in sizes:
        out.append(z[..., o:o + s])
        o += s
    return out

def _layer_norm(x, g, b):
    xf = x.astype(jnp.float32)
    mu = xf.mean(-1, keepdims=True)
    var = jnp.square(xf - mu).mean(-1, keepdims=True)
    return ((xf - mu) * lax.rsqrt(var + LN_EPS) * g + b).astype(x.dtype)

def _rms_norm(x, g):
    xf = x.astype(jnp.float32)
    return (xf * lax.rsqrt(jnp.square(xf).mean(-1, keepdims=True) + LN_EPS) * g).astype(x.dtype)

def _masked_softmax(s, mask):
    s = jnp.where(mask, s.astype(jnp.float32), NEG)
    return jnp.where(mask, jax.nn.softmax(s, axis=-1), 0.0)

def _causal_dwconv(x, w):
    k = w.shape[0]
    return lax.conv_general_dilated(x, w[:, None, :].astype(x.dtype), window_strides=(1,), padding=[(k - 1, 0)],
                                    dimension_numbers=('NWC', 'WIO', 'NWC'), feature_group_count=x.shape[-1])

def _rope_tables(pos, d):
    inv = ROPE_BASE ** (-jnp.arange(0, d, 2, dtype=jnp.float32) / d)
    ang = pos.astype(jnp.float32)[..., None] * inv
    return jnp.cos(ang), jnp.sin(ang)

def _rope(x, cos, sin):
    h = x.shape[-1] // 2
    c, s = cos.astype(x.dtype), sin.astype(x.dtype)
    x1, x2 = x[..., :h], x[..., h:]
    return jnp.concatenate([x1 * c - x2 * s, x1 * s + x2 * c], -1)

def _mlstm(q, k, v, o, ig, fg, conv_w, norm_g):
    B, T, _ = q.shape
    dt = q.dtype
    qk = jax.nn.silu(_causal_dwconv(jnp.concatenate([q, k], -1), conv_w))
    q, k = qk[..., :A_W], qk[..., A_W:]
    N = T // A_CHUNK

    def heads(u):
        return u.astype(jnp.float32).reshape(B, N, A_CHUNK, A_HEADS, A_DH).transpose(1, 0, 3, 2, 4)

    def gate(u):
        return u.astype(jnp.float32).reshape(B, N, A_CHUNK, A_HEADS).transpose(1, 0, 3, 2)

    xs = (heads(q) * A_DH ** -0.5, heads(k), heads(v), gate(ig), jax.nn.log_sigmoid(gate(fg)))
    causal = jnp.tril(jnp.ones((A_CHUNK, A_CHUNK), bool))

    def step(carry, inp):
        C, n, m = carry
        qc, kc, vc, ic, lf = inp
        b = jnp.cumsum(lf, axis=-1)
        D = jnp.where(causal, b[..., :, None] - b[..., None, :] + ic[..., None, :], NEG)
        m_inter = b + m[..., None]
        m_t = jnp.maximum(m_inter, D.max(-1))
        e_inter = jnp.exp(m_inter - m_t)
        S = jnp.einsum('bhld,bhsd->bhls', qc, kc) * jnp.exp(D - m_t[..., None])
        num = e_inter[..., None] * jnp.einsum('bhld,bhvd->bhlv', qc, C) + jnp.einsum('bhls,bhsv->bhlv', S, vc)
        den = e_inter * jnp.einsum('bhld,bhd->bhl', qc, n) + S.sum(-1)
        hc = num / jnp.maximum(jnp.abs(den), jnp.exp(-m_t))[..., None]
        bL = b[..., -1]
        dec = bL[..., None] - b + ic
        m_new = jnp.maximum(bL + m, dec.max(-1))
        w = jnp.exp(dec - m_new[..., None])
        e_st = jnp.exp(bL + m - m_new)
        C_new = e_st[..., None, None] * C + jnp.einsum('bhs,bhsv,bhsd->bhvd', w, vc, kc)
        n_new = e_st[..., None] * n + jnp.einsum('bhs,bhsd->bhd', w, kc)
        return (C_new, n_new, m_new), hc

    init = (jnp.zeros((B, A_HEADS, A_DH, A_DH), jnp.float32), jnp.zeros((B, A_HEADS, A_DH), jnp.float32),
            jnp.zeros((B, A_HEADS), jnp.float32))
    _, hs = lax.scan(step, init, xs)
    hs = hs.transpose(1, 0, 3, 2, 4).reshape(B, T, A_HEADS, A_DH)
    mu = hs.mean(-1, keepdims=True)
    var = jnp.square(hs - mu).mean(-1, keepdims=True)
    hn = ((hs - mu) * lax.rsqrt(var + LN_EPS)).reshape(B, T, A_W) * norm_g
    return (hn * jax.nn.sigmoid(o.astype(jnp.float32))).astype(dt)

def _nsa(q, kc_raw, vc_raw, ks, vs, kw, vw, g_pre, cmp_pos, cmp_w1, cmp_w2):
    B, T, _ = q.shape
    dt = q.dtype
    q = q.reshape(B, T, B_KV, B_HPG, B_DH) * B_DH ** -0.5
    r = lambda u: u.reshape(B, T, B_KV, B_DH)
    M = (T - B_CMP_LEN) // B_CMP_STRIDE + 1
    NSB = T // B_SEL_BLK
    n_sel = min(B_SEL_N, NSB)
    win = jnp.arange(M)[:, None] * B_CMP_STRIDE + jnp.arange(B_CMP_LEN)[None, :]

    def compress(u, j):
        blk = u[:, win] + cmp_pos[j][None, None, :, None, :].astype(dt)
        blk = blk.transpose(0, 1, 3, 2, 4).reshape(B, M, B_KV, B_CMP_LEN * B_DH)
        return jax.nn.gelu(blk @ cmp_w1[j]) @ cmp_w2[j]

    k_cmp = compress(r(kc_raw), 0)
    v_cmp = compress(r(vc_raw), 1)
    cmp_end = jnp.arange(M) * B_CMP_STRIDE + B_CMP_LEN - 1
    mi, jb = jnp.arange(M), jnp.arange(NSB)
    overlap = ((mi[:, None] * B_CMP_STRIDE < (jb[None, :] + 1) * B_SEL_BLK) &
               (mi[:, None] * B_CMP_STRIDE + B_CMP_LEN > jb[None, :] * B_SEL_BLK)).astype(jnp.float32)
    ks_blk = r(ks).reshape(B, NSB, B_SEL_BLK, B_KV, B_DH).transpose(0, 3, 1, 2, 4)
    vs_blk = r(vs).reshape(B, NSB, B_SEL_BLK, B_KV, B_DH).transpose(0, 3, 1, 2, 4)
    kw_pad = jnp.pad(r(kw), ((0, 0), (B_WIN, 0), (0, 0), (0, 0)))
    vw_pad = jnp.pad(r(vw), ((0, 0), (B_WIN, 0), (0, 0), (0, 0)))
    gates = jax.nn.sigmoid(g_pre.astype(jnp.float32)).reshape(B, T, B_KV, B_HPG, 3)
    bi = jnp.arange(B)[:, None, None, None]
    gi = jnp.arange(B_KV)[None, :, None, None]
    wlen = B_WIN + B_QBLK

    def block(c):
        s0 = c * B_QBLK
        tq = s0 + jnp.arange(B_QBLK)
        qb = lax.dynamic_slice_in_dim(q, s0, B_QBLK, 1)
        s = jnp.einsum('bqghd,bmgd->bqghm', qb, k_cmp)
        p_cmp = _masked_softmax(s, (cmp_end[None, :] <= tq[:, None])[None, :, None, None, :])
        o_cmp = jnp.einsum('bqghm,bmgd->bqghd', p_cmp.astype(dt), v_cmp)
        imp = p_cmp.sum(3) @ overlap
        cur = tq[:, None] // B_SEL_BLK
        forced = (jb[None, :] == 0) | (jb[None, :] == cur) | (jb[None, :] == cur - 1)
        valid = jb[None, :] * B_SEL_BLK <= tq[:, None]
        score = jnp.where(forced[None, :, None, :], 1e6, imp)
        score = jnp.where(valid[None, :, None, :], score, NEG)
        _, idx = lax.top_k(score, n_sel)
        idx = idx.transpose(0, 2, 1, 3)
        k_sel = ks_blk[bi, gi, idx].reshape(B, B_KV, B_QBLK, n_sel * B_SEL_BLK, B_DH)
        v_sel = vs_blk[bi, gi, idx].reshape(B, B_KV, B_QBLK, n_sel * B_SEL_BLK, B_DH)
        kpos = (idx[..., None] * B_SEL_BLK + jnp.arange(B_SEL_BLK)).reshape(B, B_KV, B_QBLK, n_sel * B_SEL_BLK)
        s = jnp.einsum('bgqhd,bgqkd->bgqhk', qb.transpose(0, 2, 1, 3, 4), k_sel)
        p = _masked_softmax(s, (kpos <= tq[None, None, :, None])[:, :, :, None, :])
        o_sel = jnp.einsum('bgqhk,bgqkd->bqghd', p.astype(dt), v_sel)
        kwb = lax.dynamic_slice_in_dim(kw_pad, s0, wlen, 1)
        vwb = lax.dynamic_slice_in_dim(vw_pad, s0, wlen, 1)
        wpos = s0 - B_WIN + jnp.arange(wlen)
        wmask = (wpos[None, :] <= tq[:, None]) & (wpos[None, :] > tq[:, None] - B_WIN) & (wpos[None, :] >= 0)
        s = jnp.einsum('bqghd,bkgd->bqghk', qb, kwb)
        p = _masked_softmax(s, wmask[None, :, None, None, :])
        o_win = jnp.einsum('bqghk,bkgd->bqghd', p.astype(dt), vwb)
        gb = lax.dynamic_slice_in_dim(gates, s0, B_QBLK, 1).astype(dt)
        o = gb[..., 0:1] * o_cmp + gb[..., 1:2] * o_sel + gb[..., 2:3] * o_win
        return o.reshape(B, B_QBLK, B_W)

    out = lax.map(block, jnp.arange(T // B_QBLK))
    return out.transpose(1, 0, 2, 3).reshape(B, T, B_W)

def _even_mixer(h, w_in, a_conv, a_i_b, a_f_b, a_norm, b_cmp_pos, b_cmp_w1, b_cmp_w2, b_g_b, w_out):
    aq, ak, av, ao, ai, af, bq, bkc, bvc, bks, bvs, bkw, bvw, bg = _split(h @ w_in, EVEN_SIZES)
    ya = _mlstm(aq, ak, av, ao, ai + a_i_b, af + a_f_b, a_conv, a_norm)
    yb = _nsa(bq, bkc, bvc, bks, bvs, bkw, bvw, bg + b_g_b, b_cmp_pos, b_cmp_w1, b_cmp_w2)
    return jnp.concatenate([ya, yb], -1) @ w_out

def _odd_mixer(h, pos, w_in, q_norm, kv_norm, w_qb, w_uk, w_uv, w_iq, ik_g, ik_b, w_out):
    B, T, _ = h.shape
    dt = h.dtype
    cq, ckv, kr, ik, iw = _split(h @ w_in, ODD_SIZES)
    cq = _rms_norm(cq, q_norm)
    ckv = _rms_norm(ckv, kv_norm)
    cos, sin = _rope_tables(pos, C_DR)
    qf = (cq @ w_qb).reshape(B, T, C_HEADS, C_DN + C_DR)
    q_rope = _rope(qf[..., C_DN:], cos[:, :, None], sin[:, :, None])
    k_rope = _rope(kr, cos, sin)
    q_abs = jnp.einsum('bthd,chd->bthc', qf[..., :C_DN], w_uk)
    qa = jnp.concatenate([q_abs, q_rope], -1) * (C_DN + C_DR) ** -0.5
    kv_cat = jnp.concatenate([ckv, k_rope], -1)
    icos, isin = _rope_tables(pos, C_IDX_DR)
    qi = (cq @ w_iq).reshape(B, T, C_IDX_HEADS, C_IDX_DH)
    qi = jnp.concatenate([_rope(qi[..., :C_IDX_DR], icos[:, :, None], isin[:, :, None]), qi[..., C_IDX_DR:]], -1)
    ki = _layer_norm(ik, ik_g, ik_b)
    ki = jnp.concatenate([_rope(ki[..., :C_IDX_DR], icos, isin), ki[..., C_IDX_DR:]], -1)
    wi = iw * (C_IDX_HEADS ** -0.5 * C_IDX_DH ** -0.5)
    k_sel = min(C_TOPK, T // 4)
    kpos = jnp.arange(T)
    bidx = jnp.arange(B)[:, None, None]

    def block(c):
        s0 = c * C_QBLK
        tq = s0 + jnp.arange(C_QBLK)
        qib = lax.dynamic_slice_in_dim(qi, s0, C_QBLK, 1)
        wib = lax.dynamic_slice_in_dim(wi, s0, C_QBLK, 1)
        isc = jnp.einsum('bqh,bqhs->bqs', wib, jax.nn.relu(jnp.einsum('bqhd,bsd->bqhs', qib, ki))).astype(jnp.float32)
        isc = jnp.where(kpos[None, None, :] <= tq[None, :, None], isc, NEG)
        _, idx = lax.top_k(isc, k_sel)
        g = kv_cat[bidx, idx]
        qab = lax.dynamic_slice_in_dim(qa, s0, C_QBLK, 1)
        s = jnp.einsum('bqhc,bqkc->bqhk', qab, g)
        pr = _masked_softmax(s, (idx <= tq[None, :, None])[:, :, None, :])
        return jnp.einsum('bqhk,bqkc->bqhc', pr.astype(dt), g[..., :C_KVL])

    o_lat = lax.map(block, jnp.arange(T // C_QBLK))
    o_lat = o_lat.transpose(1, 0, 2, 3, 4).reshape(B, T, C_HEADS, C_KVL)
    o = jnp.einsum('bthc,chv->bthv', o_lat, w_uv).reshape(B, T, C_HEADS * C_DV)
    return o @ w_out

def first_inputs(seed: int = 0) -> dict:
    key = jax.random.key(seed)
    keys = iter(jax.random.split(key, 64))

    def nrm(shape, scale):
        return jax.random.normal(next(keys), shape, jnp.float32) * scale

    E, O, L, D = N_EVEN, N_ODD, DEPTH, D_MODEL
    sD = D ** -0.5
    x = nrm((BATCH, SEQ, D), 1.0)
    p = nrm((DEPTH, BATCH, SEQ, D_PLE), 1.0)
    positions = jnp.broadcast_to(jnp.arange(SEQ, dtype=jnp.int32), (BATCH, SEQ))
    seg = lambda n, sc=1.0: nrm((E, D, n), sD * sc)
    e_w_in = jnp.concatenate([seg(A_W), seg(A_W), seg(A_W, DN_BETA), seg(A_W), seg(A_HEADS), seg(A_HEADS),
                              seg(B_W), seg(B_KVW), seg(B_KVW, DN_BETA), seg(B_KVW), seg(B_KVW, DN_BETA),
                              seg(B_KVW), seg(B_KVW, DN_BETA), seg(3 * B_HEADS)], axis=-1)
    e_a_conv = nrm((E, A_CONV, 2 * A_W), A_CONV ** -0.5)
    e_a_i_b = nrm((E, A_HEADS), 0.1)
    e_a_f_b = jnp.linspace(3.0, 6.0, A_HEADS, dtype=jnp.float32)[None] + nrm((E, A_HEADS), 0.1)
    e_a_norm = 1.0 + nrm((E, A_W), 0.02)
    e_b_cmp_pos = nrm((E, 2, B_CMP_LEN, B_DH), 0.1)
    e_b_cmp_w1 = nrm((E, 2, B_CMP_LEN * B_DH, B_CMP_HID), (B_CMP_LEN * B_DH) ** -0.5)
    e_b_cmp_w2 = nrm((E, 2, B_CMP_HID, B_DH), B_CMP_HID ** -0.5) * jnp.array([1.0, DN_BETA], jnp.float32)[None, :, None, None]
    e_b_g_b = nrm((E, 3 * B_HEADS), 0.1)
    e_w_out = nrm((E, A_W + B_W, D), (A_W + B_W) ** -0.5 * DN_BETA)
    o_w_in = jnp.concatenate([nrm((O, D, n), sD) for n in ODD_SIZES], axis=-1)
    o_q_norm = 1.0 + nrm((O, C_QL), 0.02)
    o_kv_norm = 1.0 + nrm((O, C_KVL), 0.02)
    o_w_qb = nrm((O, C_QL, C_HEADS * (C_DN + C_DR)), C_QL ** -0.5)
    o_w_uk = nrm((O, C_KVL, C_HEADS, C_DN), C_KVL ** -0.5)
    o_w_uv = nrm((O, C_KVL, C_HEADS, C_DV), C_KVL ** -0.5 * DN_BETA)
    o_w_iq = nrm((O, C_QL, C_IDX_HEADS * C_IDX_DH), C_QL ** -0.5)
    o_ik_g = 1.0 + nrm((O, C_IDX_DH), 0.02)
    o_ik_b = nrm((O, C_IDX_DH), 0.02)
    o_w_out = nrm((O, C_HEADS * C_DV, D), (C_HEADS * C_DV) ** -0.5 * DN_BETA)
    ln1_g = 1.0 + nrm((L, D), 0.02)
    ln1_b = nrm((L, D), 0.02)
    ln2_g = 1.0 + nrm((L, D), 0.02)
    ln2_b = nrm((L, D), 0.02)
    mlp_w1 = nrm((L, D, D_FF), sD * DN_BETA)
    mlp_w2 = nrm((L, D_FF, D), D_FF ** -0.5 * DN_BETA)
    ple_gate_w = nrm((L, D, D), sD)
    ple_w = nrm((L, D_PLE, D), D_PLE ** -0.5)
    return {'x': x, 'p': p, 'positions': positions,
            'e_w_in': e_w_in, 'e_a_conv': e_a_conv, 'e_a_i_b': e_a_i_b, 'e_a_f_b': e_a_f_b, 'e_a_norm': e_a_norm,
            'e_b_cmp_pos': e_b_cmp_pos, 'e_b_cmp_w1': e_b_cmp_w1, 'e_b_cmp_w2': e_b_cmp_w2, 'e_b_g_b': e_b_g_b,
            'e_w_out': e_w_out,
            'o_w_in': o_w_in, 'o_q_norm': o_q_norm, 'o_kv_norm': o_kv_norm, 'o_w_qb': o_w_qb, 'o_w_uk': o_w_uk,
            'o_w_uv': o_w_uv, 'o_w_iq': o_w_iq, 'o_ik_g': o_ik_g, 'o_ik_b': o_ik_b, 'o_w_out': o_w_out,
            'ln1_g': ln1_g, 'ln1_b': ln1_b, 'ln2_g': ln2_g, 'ln2_b': ln2_b, 'mlp_w1': mlp_w1, 'mlp_w2': mlp_w2,
            'ple_gate_w': ple_gate_w, 'ple_w': ple_w}

def first_block(x, p, positions,
              e_w_in, e_a_conv, e_a_i_b, e_a_f_b, e_a_norm, e_b_cmp_pos, e_b_cmp_w1, e_b_cmp_w2, e_b_g_b, e_w_out,
              o_w_in, o_q_norm, o_kv_norm, o_w_qb, o_w_uk, o_w_uv, o_w_iq, o_ik_g, o_ik_b, o_w_out,
              ln1_g, ln1_b, ln2_g, ln2_b, mlp_w1, mlp_w2, ple_gate_w, ple_w):
    h = x
    for i in range(DEPTH):
        j = i // 2
        if i % 2 == 0:
            y = _even_mixer(h, e_w_in[j], e_a_conv[j], e_a_i_b[j], e_a_f_b[j], e_a_norm[j], e_b_cmp_pos[j],
                            e_b_cmp_w1[j], e_b_cmp_w2[j], e_b_g_b[j], e_w_out[j])
        else:
            y = _odd_mixer(h, positions, o_w_in[j], o_q_norm[j], o_kv_norm[j], o_w_qb[j], o_w_uk[j], o_w_uv[j],
                           o_w_iq[j], o_ik_g[j], o_ik_b[j], o_w_out[j])
        h = _layer_norm(DN_ALPHA * h + y, ln1_g[i], ln1_b[i])
        u = jnp.square(jax.nn.relu(h @ mlp_w1[i])) @ mlp_w2[i]
        h = _layer_norm(DN_ALPHA * h + u, ln2_g[i], ln2_b[i])
        h = h + jax.nn.sigmoid(h @ ple_gate_w[i]) * (p[i] @ ple_w[i])
    return h


D_MIX = D_MODEL
HG_HEADS = 4
HG_DK = 64
HG_DV = 64
HG_QK = HG_HEADS * HG_DK
HG_W = HG_HEADS * HG_DV
GD_HEADS = 4
GD_DK = 128
GD_DV = 128
GD_QK = GD_HEADS * GD_DK
GD_W = GD_HEADS * GD_DV
RG_W = D_MIX - HG_W - GD_W
RG_BLOCKS = 4
RG_BD = RG_W // RG_BLOCKS
RG_C = 8.0
CONV_W = 4
D_FF_2 = 2816
CHUNK = 64
EPS = 1e-6
SPLIT_SIZES = (HG_QK, HG_QK, HG_W, HG_W, GD_QK, GD_QK, GD_W, GD_W, GD_HEADS, GD_HEADS, RG_W, RG_W)
SPLIT_POINTS = tuple(int(p) for p in np.cumsum(SPLIT_SIZES)[:-1])
N_IN = int(sum(SPLIT_SIZES))


def rmsnorm(x, w):
    xf = x.astype(jnp.float32)
    y = xf * lax.rsqrt(jnp.mean(xf * xf, axis=-1, keepdims=True) + EPS)
    return (y * w.astype(jnp.float32)).astype(x.dtype)

def head_rmsnorm(o, w):
    return o * lax.rsqrt(jnp.mean(o * o, axis=-1, keepdims=True) + EPS) * w.astype(jnp.float32)

def l2norm(t):
    return t * lax.rsqrt(jnp.sum(t * t, axis=-1, keepdims=True) + EPS)

def causal_depthwise_conv(x, w):
    return lax.conv_general_dilated(
        x, w[:, None, :].astype(x.dtype), window_strides=(1,), padding=[(CONV_W - 1, 0)],
        dimension_numbers=('NWC', 'WIO', 'NWC'), feature_group_count=x.shape[-1])

def to_chunks(t):
    b, l, h, d = t.shape
    return t.reshape(b, l // CHUNK, CHUNK, h, d).transpose(1, 0, 3, 2, 4)

def from_chunks(t):
    n, b, h, c, d = t.shape
    return t.transpose(1, 0, 3, 2, 4).reshape(b, n * c, h, d)

def swiglu(h, w_gate, w_up, w_down):
    return (jax.nn.silu(h @ w_gate) * (h @ w_up)) @ w_down

def hgrn2_chunked(q, k, v, logf):
    qc, kc, vc, gc = to_chunks(q), to_chunks(k), to_chunks(v), to_chunks(logf)
    _, b, h, _, dk = qc.shape
    dv = vc.shape[-1]
    causal = jnp.tril(jnp.ones((CHUNK, CHUNK), dtype=bool))[:, :, None]

    def step(state, inp):
        qi, ki, vi, gi = inp
        cum = jnp.cumsum(gi, axis=2)
        diff = cum[:, :, :, None, :] - cum[:, :, None, :, :]
        decay = jnp.exp(jnp.where(causal, diff, -jnp.inf))
        scores = jnp.einsum('bhtd,bhsd,bhtsd->bhts', qi, ki, decay)
        o = (jnp.einsum('bhts,bhsv->bhtv', scores, vi)
             + jnp.einsum('bhtd,bhdv->bhtv', qi * jnp.exp(cum), state))
        last = cum[:, :, -1:, :]
        state = (state * jnp.exp(last[:, :, 0, :, None])
                 + jnp.einsum('bhsd,bhsv->bhdv', ki * jnp.exp(last - cum), vi))
        return state, o

    s0 = jnp.zeros((b, h, dk, dv), jnp.float32)
    _, o = lax.scan(step, s0, (qc, kc, vc, gc))
    return from_chunks(o)

def gated_delta_chunked(q, k, v, g, beta):
    qc, kc, vc = to_chunks(q), to_chunks(k), to_chunks(v)
    gc = to_chunks(g[..., None])[..., 0]
    bc = to_chunks(beta[..., None])[..., 0]
    _, b, h, _, dk = qc.shape
    dv = vc.shape[-1]
    incl = jnp.tril(jnp.ones((CHUNK, CHUNK), dtype=bool))
    strict = jnp.tril(jnp.ones((CHUNK, CHUNK), dtype=bool), k=-1)
    eye = jnp.eye(CHUNK, dtype=jnp.float32)

    def step(state, inp):
        qi, ki, vi, gi, bi = inp
        cum = jnp.cumsum(gi, axis=-1)
        decay = jnp.exp(jnp.where(incl, cum[..., :, None] - cum[..., None, :], -jnp.inf))
        kb = ki * bi[..., None]
        lower = jnp.where(strict, jnp.einsum('bhtd,bhsd->bhts', kb, ki) * decay, 0.0)
        rhs = jnp.concatenate([vi * bi[..., None], kb * jnp.exp(cum)[..., None]], axis=-1)
        sol = lax.linalg.triangular_solve(eye + lower, rhs, left_side=True, lower=True,
                                          unit_diagonal=True)
        u, w = sol[..., :dv], sol[..., dv:]
        v_new = u - jnp.einsum('bhtd,bhdv->bhtv', w, state)
        scores = jnp.einsum('bhtd,bhsd->bhts', qi, ki) * decay
        o = (jnp.einsum('bhtd,bhdv->bhtv', qi * jnp.exp(cum)[..., None], state)
             + jnp.einsum('bhts,bhsv->bhtv', scores, v_new))
        last = cum[..., -1:]
        state = (state * jnp.exp(last)[..., None]
                 + jnp.einsum('bhsd,bhsv->bhdv', ki * jnp.exp(last - cum)[..., None], v_new))
        return state, o

    s0 = jnp.zeros((b, h, dk, dv), jnp.float32)
    _, o = lax.scan(step, s0, (qc, kc, vc, gc, bc))
    return from_chunks(o)

def rg_lru(xc, wr, br, wi, bi, lam):
    b, l, _ = xc.shape
    xb = xc.reshape(b, l, RG_BLOCKS, RG_BD)
    r = jax.nn.sigmoid(jnp.einsum('blni,nio->blno', xb, wr.astype(jnp.float32)).reshape(b, l, RG_W)
                       + br.astype(jnp.float32))
    ig = jax.nn.sigmoid(jnp.einsum('blni,nio->blno', xb, wi.astype(jnp.float32)).reshape(b, l, RG_W)
                        + bi.astype(jnp.float32))
    log_a = -RG_C * r * jax.nn.softplus(-lam.astype(jnp.float32))
    a = jnp.exp(log_a)
    bx = jnp.sqrt(-jnp.expm1(2.0 * log_a)) * (ig * xc)

    def combine(c1, c2):
        a1, b1 = c1
        a2, b2 = c2
        return a1 * a2, a2 * b1 + b2

    _, hs = lax.associative_scan(combine, (a, bx), axis=1)
    return hs

def hybrid_mixer(h, lb, w_in, hg_norm_w, gd_conv_w, gd_a_log, gd_dt_bias, gd_norm_w,
                 rg_conv_w, rg_conv_b, rg_wr, rg_br, rg_wi, rg_bi, rg_lambda, w_out):
    b, l, _ = h.shape
    f32 = jnp.float32
    proj = (h @ w_in).astype(f32)
    (hg_q, hg_f, hg_i, hg_g, gd_q, gd_k, gd_v, gd_z, gd_b, gd_a,
     rg_x, rg_gate) = jnp.split(proj, SPLIT_POINTS, axis=-1)

    lbf = lb.reshape(HG_HEADS, HG_DK)
    q = jax.nn.silu(hg_q).reshape(b, l, HG_HEADS, HG_DK) * (HG_DK ** -0.5)
    f = lbf + (1.0 - lbf) * jax.nn.sigmoid(hg_f.reshape(b, l, HG_HEADS, HG_DK))
    o_hg = hgrn2_chunked(q, 1.0 - f, hg_i.reshape(b, l, HG_HEADS, HG_DV), jnp.log(f))
    o_hg = head_rmsnorm(o_hg, hg_norm_w) * jax.nn.silu(hg_g.reshape(b, l, HG_HEADS, HG_DV))

    qkv = jax.nn.silu(causal_depthwise_conv(jnp.concatenate([gd_q, gd_k, gd_v], axis=-1), gd_conv_w))
    cq, ck, cv = jnp.split(qkv, (GD_QK, 2 * GD_QK), axis=-1)
    cq = l2norm(cq.reshape(b, l, GD_HEADS, GD_DK)) * (GD_DK ** -0.5)
    ck = l2norm(ck.reshape(b, l, GD_HEADS, GD_DK))
    beta = jax.nn.sigmoid(gd_b)
    g = -jnp.exp(gd_a_log.astype(f32)) * jax.nn.softplus(gd_a + gd_dt_bias.astype(f32))
    o_gd = gated_delta_chunked(cq, ck, cv.reshape(b, l, GD_HEADS, GD_DV), g, beta)
    o_gd = head_rmsnorm(o_gd, gd_norm_w) * jax.nn.silu(gd_z.reshape(b, l, GD_HEADS, GD_DV))

    xc = causal_depthwise_conv(rg_x, rg_conv_w) + rg_conv_b.astype(f32)
    o_rg = rg_lru(xc, rg_wr, rg_br, rg_wi, rg_bi, rg_lambda) * jax.nn.gelu(rg_gate, approximate=True)

    y = jnp.concatenate([o_hg.reshape(b, l, HG_W), o_gd.reshape(b, l, GD_W), o_rg], axis=-1)
    return y.astype(h.dtype) @ w_out

def second_inputs(seed: int = 0) -> dict:
    key = jax.random.key(seed)
    ks = jax.random.split(key, 32)
    f32 = jnp.float32

    def nrm(k, shape, scale):
        return jax.random.normal(k, shape, f32) * scale

    def gain(k, shape):
        return 1.0 + 0.02 * jax.random.normal(k, shape, f32)

    dt = jnp.exp(jax.random.uniform(ks[12], (DEPTH, GD_HEADS), f32, math.log(1e-3), math.log(1e-1)))
    a0 = jax.random.uniform(ks[19], (DEPTH, RG_W), f32, 0.9, 0.999) ** (1.0 / RG_C)
    return {
        'x': nrm(ks[0], (BATCH, SEQ, D_MODEL), 1.0),
        'norm_ffn1': gain(ks[1], (DEPTH, D_MODEL)),
        'ffn1_gate': nrm(ks[2], (DEPTH, D_MODEL, D_FF_2), D_MODEL ** -0.5),
        'ffn1_up': nrm(ks[3], (DEPTH, D_MODEL, D_FF_2), D_MODEL ** -0.5),
        'ffn1_down': nrm(ks[4], (DEPTH, D_FF_2, D_MODEL), D_FF_2 ** -0.5),
        'norm_mix': gain(ks[5], (DEPTH, D_MODEL)),
        'w_in': nrm(ks[6], (DEPTH, D_MODEL, N_IN), D_MODEL ** -0.5),
        'hg_lb': nrm(ks[7], (DEPTH, HG_QK), 1.0),
        'hg_norm_w': gain(ks[8], (DEPTH, HG_DV)),
        'gd_conv_w': nrm(ks[9], (DEPTH, CONV_W, 2 * GD_QK + GD_W), CONV_W ** -0.5),
        'gd_a_log': jnp.log(jax.random.uniform(ks[10], (DEPTH, GD_HEADS), f32, 1.0, 16.0)),
        'gd_dt_bias': dt + jnp.log(-jnp.expm1(-dt)),
        'gd_norm_w': gain(ks[11], (DEPTH, GD_DV)),
        'rg_conv_w': nrm(ks[13], (DEPTH, CONV_W, RG_W), CONV_W ** -0.5),
        'rg_conv_b': nrm(ks[14], (DEPTH, RG_W), 0.02),
        'rg_wr': nrm(ks[15], (DEPTH, RG_BLOCKS, RG_BD, RG_BD), RG_BD ** -0.5),
        'rg_br': nrm(ks[16], (DEPTH, RG_W), 0.1),
        'rg_wi': nrm(ks[17], (DEPTH, RG_BLOCKS, RG_BD, RG_BD), RG_BD ** -0.5),
        'rg_bi': nrm(ks[18], (DEPTH, RG_W), 0.1),
        'rg_lambda': jnp.log(a0) - jnp.log1p(-a0),
        'w_out': nrm(ks[20], (DEPTH, D_MIX, D_MODEL), D_MIX ** -0.5),
        'norm_ffn2': gain(ks[21], (DEPTH, D_MODEL)),
        'ffn2_gate': nrm(ks[22], (DEPTH, D_MODEL, D_FF_2), D_MODEL ** -0.5),
        'ffn2_up': nrm(ks[23], (DEPTH, D_MODEL, D_FF_2), D_MODEL ** -0.5),
        'ffn2_down': nrm(ks[24], (DEPTH, D_FF_2, D_MODEL), D_FF_2 ** -0.5),
        'norm_final': gain(ks[25], (D_MODEL,)),
    }

def second_block(x, norm_ffn1, ffn1_gate, ffn1_up, ffn1_down, norm_mix, w_in, hg_lb, hg_norm_w,
              gd_conv_w, gd_a_log, gd_dt_bias, gd_norm_w, rg_conv_w, rg_conv_b, rg_wr, rg_br,
              rg_wi, rg_bi, rg_lambda, w_out, norm_ffn2, ffn2_gate, ffn2_up, ffn2_down, norm_final):
    lb_all = jnp.cumsum(jax.nn.softmax(hg_lb.astype(jnp.float32), axis=0), axis=0)
    lb_all = lb_all - lb_all[0]
    for layer in range(DEPTH):
        x = x + 0.5 * swiglu(rmsnorm(x, norm_ffn1[layer]), ffn1_gate[layer], ffn1_up[layer],
                             ffn1_down[layer])
        x = x + hybrid_mixer(rmsnorm(x, norm_mix[layer]), lb_all[layer], w_in[layer], hg_norm_w[layer],
                             gd_conv_w[layer], gd_a_log[layer], gd_dt_bias[layer], gd_norm_w[layer],
                             rg_conv_w[layer], rg_conv_b[layer], rg_wr[layer], rg_br[layer],
                             rg_wi[layer], rg_bi[layer], rg_lambda[layer], w_out[layer])
        x = x + 0.5 * swiglu(rmsnorm(x, norm_ffn2[layer]), ffn2_gate[layer], ffn2_up[layer],
                             ffn2_down[layer])
    return rmsnorm(x, norm_final)


def setup_inputs(seed=0):
    out = dict(first_inputs(seed))
    for name, value in second_inputs(seed + 1).items():
        if name != "x":
            out[name + "_2"] = value
    return out


def reference(
    x, p, positions, e_w_in, e_a_conv, e_a_i_b, e_a_f_b, e_a_norm, e_b_cmp_pos, e_b_cmp_w1,
    e_b_cmp_w2, e_b_g_b, e_w_out, o_w_in, o_q_norm, o_kv_norm, o_w_qb, o_w_uk, o_w_uv, o_w_iq,
    o_ik_g, o_ik_b, o_w_out, ln1_g, ln1_b, ln2_g, ln2_b, mlp_w1, mlp_w2, ple_gate_w, ple_w,
    norm_ffn1_2, ffn1_gate_2, ffn1_up_2, ffn1_down_2, norm_mix_2, w_in_2, hg_lb_2, hg_norm_w_2,
    gd_conv_w_2, gd_a_log_2, gd_dt_bias_2, gd_norm_w_2, rg_conv_w_2, rg_conv_b_2, rg_wr_2,
    rg_br_2, rg_wi_2, rg_bi_2, rg_lambda_2, w_out_2, norm_ffn2_2, ffn2_gate_2, ffn2_up_2,
    ffn2_down_2, norm_final_2,
):
    x = first_block(
        x, p, positions, e_w_in, e_a_conv, e_a_i_b, e_a_f_b, e_a_norm, e_b_cmp_pos, e_b_cmp_w1,
        e_b_cmp_w2, e_b_g_b, e_w_out, o_w_in, o_q_norm, o_kv_norm, o_w_qb, o_w_uk, o_w_uv,
        o_w_iq, o_ik_g, o_ik_b, o_w_out, ln1_g, ln1_b, ln2_g, ln2_b, mlp_w1, mlp_w2, ple_gate_w,
        ple_w,
    )
    return second_block(
        x, norm_ffn1_2, ffn1_gate_2, ffn1_up_2, ffn1_down_2, norm_mix_2, w_in_2, hg_lb_2,
        hg_norm_w_2, gd_conv_w_2, gd_a_log_2, gd_dt_bias_2, gd_norm_w_2, rg_conv_w_2,
        rg_conv_b_2, rg_wr_2, rg_br_2, rg_wi_2, rg_bi_2, rg_lambda_2, w_out_2, norm_ffn2_2,
        ffn2_gate_2, ffn2_up_2, ffn2_down_2, norm_final_2,
    )


_drawn_inputs = setup_inputs


def setup_inputs(seed=0):
    import zlib

    import numpy as np

    out = dict(_drawn_inputs(seed))
    spreads = {}
    factors = {'e_a_i_b': 8.0,
     'e_a_norm': 8.0,
     'e_b_cmp_pos': 8.0,
     'e_b_cmp_w1': 4.584,
     'e_b_g_b': 8.0,
     'o_q_norm': 8.0,
     'o_kv_norm': 8.0,
     'o_w_iq': 3.028,
     'o_ik_g': 8.0,
     'o_ik_b': 8.0,
     'norm_ffn1_2': 4.694,
     'norm_mix_2': 2.804,
     'hg_norm_w_2': 8.0,
     'gd_norm_w_2': 5.548,
     'rg_br_2': 8.0,
     'rg_bi_2': 5.247,
     'norm_ffn2_2': 6.059,
     'norm_final_2': 2.823}
    for name, (base, spread) in spreads.items():
        noise = np.random.default_rng([zlib.crc32(name.encode()), seed]).standard_normal(out[name].shape)
        drawn = base * np.exp(spread * noise) if base else spread * noise
        out[name] = jnp.asarray(drawn.astype(out[name].dtype))
    for name, factor in factors.items():
        out[name] = (out[name] * factor).astype(out[name].dtype)
    return out
```

```python
import numpy as np
import concourse.bass as bass
import concourse.mybir as mybir
from concourse.alu_op_type import AluOpType as ALU
from contextlib import ExitStack

F32 = mybir.dt.float32
I32 = mybir.dt.int32
ACT = mybir.ActivationFunctionType
AX = mybir.AxisListType
T = 512
NS = 3
SLOT = 4096
NA = 24100
ALPHA = float((2.0 * 2) ** 0.25)
NEG = -1e30

CONSTS = [
    ("ident", 128), ("lev", 8 * 128), ("cmask", 128), ("tmask", 128), ("ones", 128), ("sel", 512),
    ("cmpadd", 124), ("cmp01", 124), ("invf", 48), ("zero", 1),
    ("aconv", 32), ("aib", 1), ("afb", 1), ("anorm", 512), ("cpos", 64), ("cw2", 128), ("gb", 24),
    ("qnorm", 4), ("kvnorm", 256), ("ikg", 64), ("ikb", 64),
    ("nf1", 16), ("nmix", 16), ("nf2", 16), ("hlb", 4), ("hnw", 128), ("gconv", 96), ("galog", 2), ("gdt", 2),
    ("gnw", 256), ("rconv", 16), ("rconvb", 4), ("rbr", 4), ("rbi", 4), ("rlam", 4),
]
COFF = {}
NCB = 0
for _n, _w in CONSTS:
    COFF[_n] = (NCB, _w)
    NCB += _w


class Prog:

    ENG = ("pe", "act", "dve", "pool", "sp")

    def __init__(self):
        self.ops = {e: [] for e in self.ENG}
        self.cnt = {e: 0 for e in self.ENG}
        self.seen = {e: {} for e in self.ENG}
        self.need = {e: [] for e in self.ENG}

    def last(self, e):
        if not self.ops[e]:
            return (e, 0)
        o = self.ops[e][-1]
        if not o[2]:
            o[2] = True
            self.cnt[e] += 1
        return (e, self.cnt[e])

    def op(self, e, fn, after=(), chain=True):
        waits = []
        after = [a for a in after if a is not None] + self.need[e]
        self.need[e] = []
        if chain and e in ("act", "dve", "pool"):
            after.append(self.last(e))
        for s, v in after:
            if v and self.seen[e].get(s, 0) < v and not (e == "pe" and s == "pe"):
                self.seen[e][s] = v
                waits.append((s, v))
        self.ops[e].append([fn, waits, False])


class Bank:
    def __init__(self, t):
        self.t = t
        self.free = []


def bc(ap, shape):
    return ap.broadcast_to(shape)


def record(nc, ctx, dbg=None):
    P = Prog()
    sb = lambda n, s, d=F32: ctx.enter_context(nc.sbuf_tensor(n, s, d))
    RING = sb("ring", [128, NS, SLOT])
    X = sb("X", [128, 4, 1024])
    H = sb("H", [128, 8, 512])
    C = sb("C", [128, NCB])
    ARENA = sb("arena", [128, NA])
    POS = sb("pos", [128, 4], I32)
    SM = sb("small", [128, 256])
    banks = [Bank(ctx.enter_context(nc.psum_tensor(f"ps{i}", [128, 512], F32))) for i in range(8)]
    st = {"bank": 0, "ev": 0}
    stream = []
    slotfree = [[] for _ in range(NS)]
    misc = []

    def cst(name):
        o, w = COFF[name]
        return C[:, o:o + w]

    def bank():
        b = banks[st["bank"] % 8]
        st["bank"] += 1
        return b

    E = lambda: P.last("pe")
    A = lambda: P.last("act")
    D = lambda: P.last("dve")
    G = lambda: P.last("pool")
    AD = lambda: [A(), D()]

    class Arena:
        def __init__(self):
            self.o = 0

        def take(self, *dims):
            n = int(np.prod(dims))
            v = ARENA[:, self.o:self.o + n]
            self.o += n
            assert self.o <= NA, self.o
            if len(dims) == 2:
                v = v.rearrange("p (a b) -> p a b", a=dims[0])
            if len(dims) == 3:
                v = v.rearrange("p (a b c) -> p a b c", a=dims[0], b=dims[1])
            return v

        def at(self, o):
            self.o = o
            return self

    def mm(out, l, r, start, stop, after=()):
        P.op("pe", lambda e: e.matmul(out, l, r, start=start, stop=stop, skip_group_check=True), after)

    def tr(out, i, after=()):
        k = i.shape[0]
        o, _ = COFF["ident"]
        s0 = i.base_partition() if callable(i.base_partition) else i.base_partition
        idn = C[s0:s0 + k, o + s0:o + s0 + k]
        P.op("pe", lambda e: e.transpose(out, i, idn), after)

    def act(out, i, f, bias=None, scale=None, accum=None, after=()):
        kw = {}
        if bias is not None:
            kw["bias"] = bias
        if scale is not None:
            kw["scale"] = scale
        if accum is not None:
            kw["accum_out"] = accum
        P.op("act", lambda e: e.activation(out, i, f, **kw), after)

    def ts(out, i, s1, s2, o0, o1=None, after=(), accum=None, eng="dve"):
        if o1 is None:
            P.op(eng, lambda e: e.tensor_scalar(out, i, s1, None, o0), after)
        elif accum is not None:
            P.op(eng, lambda e: e.tensor_scalar(out, i, s1, s2, o0, o1, accum_out=accum), after)
        else:
            P.op(eng, lambda e: e.tensor_scalar(out, i, s1, s2, o0, o1), after)

    def tt(out, a, b, o, after=(), eng="dve"):
        P.op(eng, lambda e: e.tensor_tensor(out, a, b, o), after)

    def stt(out, a, s, b, o0, o1, after=()):
        P.op("dve", lambda e: e.scalar_tensor_tensor(out, a, s, b, o0, o1), after)

    def vcp(out, i, after=()):
        P.op("dve", lambda e: e.tensor_copy(out, i), after)

    def bns(out, i, after=()):
        P.op("dve", lambda e: e.bn_stats(out, i), after)

    def bna(out, i):
        P.op("dve", lambda e: e.bn_aggr(out, i))

    def top8(m8, a):
        P.op("dve", lambda e: e.max(m8, a))
        P.op("dve", lambda e: e.match_replace(a, m8, a, -3.0e38))

    def recip(out, i, after=()):
        P.op("dve", lambda e: e.reciprocal(out, i), after)

    def scan(out, a, b, init, o0, o1, after=()):
        P.op("dve", lambda e: e.tensor_tensor_scan(out, a, b, init, o0, o1), after)

    def red(out, i, o, neg=False, after=()):
        P.op("dve", lambda e: e.tensor_reduce(out, i, AX.X, o, negate=neg), after)

    def evc(out, i, after=(), scale=None):
        st["ev"] += 1
        if st["ev"] % 2:
            act(out, i, ACT.Copy, scale=scale, after=after)
        elif scale is None:
            vcp(out, i, after)
        else:
            ts(out, i, scale, None, ALU.mult, after=after)

    def load(key, k0, nk, c0, ncol):
        i = len(stream)
        slot = i % NS
        assert nk * ncol <= SLOT
        stream.append((key, k0, nk, c0, ncol))
        v = RING[:, slot, 0:nk * ncol]
        P.op("sp", lambda e, W, S: e.dma_start(v, W[i]).then_inc(S[f"w{slot}"], 16), slotfree[slot])
        slotfree[slot] = None
        return v.rearrange("p (k n) -> p k n", k=nk), (f"w{slot}", 16 * (i // NS + 1)), slot

    def release(slot, toks):
        slotfree[slot] = list(toks)

    def lin(src, nk, key, c0, ncol, fm, evict, after=()):
        nm = ncol // 128 if fm else 4
        bs = [bank() for _ in range(nm)]
        for kc in range(0, nk, 8):
            n = min(8, nk - kc)
            w, tok, slot = load(key, kc, n, c0, ncol)
            for m in range(nm):
                for k in range(n):
                    kk = kc + k
                    if fm:
                        l, r = w[:, k, m * 128:(m + 1) * 128], src[:, kk, :]
                    else:
                        l, r = src[:, kk, m * 128:(m + 1) * 128], w[:, k, :]
                    nn = 512 if fm else ncol
                    mm(bs[m].t[:, 0:nn], l, r, kk == 0, kk == nk - 1, [tok] + list(after) + bs[m].free)
                if kc + n == nk:
                    evict(m, bs[m].t)
                    bs[m].free = AD()
            release(slot, [E()])

    def to_fm(src, dst, nf, gain=None, after=()):
        for f in range(nf):
            b = bank()
            for j in range(4):
                tr(b.t[:, j * 128:(j + 1) * 128], src[:, j, f * 128:(f + 1) * 128], list(after) + b.free)
            if gain is None:
                evc(dst[:, f, :], b.t[:, :], [E()])
            else:
                st["ev"] += 1
                if st["ev"] % 2:
                    act(dst[:, f, :], b.t[:, :], ACT.Copy, scale=gain[:, f:f + 1], after=[E()])
                else:
                    ts(dst[:, f, :], b.t[:, :], gain[:, f:f + 1], None, ALU.mult, after=[E()])
            b.free = AD()

    def pw(x):
        act(x, x, ACT.Sqrt, after=[D()])
        recip(x, x, after=[A()])

    def rsq(out, i, mul, eps):
        ts(out, i, mul, eps, ALU.mult, ALU.add)
        pw(out)

    def layer_norm(key):
        w, tok, slot = load(key, 0, 1, 0, 2048)
        sc = SM[:, 0:16]
        for j in range(4):
            bns(sc[:, 0:6], X[:, j, 0:512], after=[A()])
            bns(sc[:, 6:12], X[:, j, 512:1024])
            bna(sc[:, 12:14], sc[:, 0:12])
            rsq(sc[:, 14:15], sc[:, 13:14], 1.0, 1e-5)
            ts(X[:, j, :], X[:, j, :], sc[:, 12:13], sc[:, 14:15], ALU.subtract, ALU.mult)
            tt(X[:, j, :], X[:, j, :], w[:, 0, 0:1024], ALU.mult, [tok])
            tt(X[:, j, :], X[:, j, :], w[:, 0, 1024:2048], ALU.add)
        release(slot, [D()])

    def rms_rows(src, tmp, dst, n, out_scale, eps):
        a = SM[:, 16:17]
        act(tmp, src, ACT.Square, accum=a, after=[D()])
        ts(SM[:, 17:18], a, 1.0 / n, eps, ALU.mult, ALU.add, after=[A()])
        pw(SM[:, 17:18])
        ts(dst, src, SM[:, 17:18], None, ALU.mult)

    def dump(name, ap, shape):
        if dbg is None:
            return
        dbg.append((name, shape))
        P.op("sp", lambda e, W, S: e.dma_start(W["dbg_" + name], ap).then_inc(S["out"], 16), [E(), A(), D(), G()])

    P.op("sp", lambda e, W, S: e.dma_start(C[:, :], W["cb"]).then_inc(S["c"], 16))
    P.op("sp", lambda e, W, S: e.dma_start(H[:, :, :], W["xT"]).then_inc(S["xt"], 16))
    P.op("sp", lambda e, W, S: e.dma_start(X[:, :, :], W["x"]).then_inc(S["x"], 16))
    P.op("sp", lambda e, W, S: e.dma_start(POS[:, :], W["pos"]).then_inc(S["pos"], 16))
    cb_tok, xt_tok, x_tok, pos_tok = ("c", 16), ("xt", 16), ("x", 16), ("pos", 16)
    P.op("dve", lambda e: e.memset(SM[:, :], 0.0), [cb_tok, x_tok])
    P.op("act", lambda e: e.activation(SM[:, 200:201], SM[:, 201:202], ACT.Copy), [cb_tok, D()])
    P.op("pool", lambda e: e.memset(SM[:, 202:203], 0.0), [cb_tok, D()])

    ident, ones, sel = cst("ident"), cst("ones"), cst("sel")

    def res_add(scale_x, scale_y, c0):
        def f(m, ps):
            xs = X[:, m, c0:c0 + 512]
            if scale_y is None:
                stt(xs, xs, scale_x, ps[:, :], ALU.mult, ALU.add, [E()])
            else:
                stt(xs, ps[:, :], scale_y, xs, ALU.mult, ALU.add, [E()])
        return f

    def even_mixer():
        ar = Arena()
        QK = ar.take(8, 512)
        AV = ar.take(4, 4, 129)
        BQ = ar.take(4, 512)
        KCV = ar.take(2, 512)
        KSW = ar.take(2, 512)
        VSW = ar.take(4, 256)
        GT = ar.take(4, 24)
        AO = ar.take(4, 512)
        YA = ar.take(4, 1024)
        base = ar.o
        raw = ar.take(2, 516)
        acc = ar.take(512)
        aconv = cst("aconv")
        P.op("pool", lambda e: e.memset(raw[:, :, 0:3], 0.0))
        P.op("pool", lambda e: e.memset(AV[:, :, :, 128:129], 1.0))
        g0 = G()

        def ev_qk(c):
            def f(m, ps):
                t = c * 4 + m
                r = raw[:, t % 2, :]
                act(r[:, 3:515], ps[:, :], ACT.Copy, after=[E(), D(), g0])
                ts(acc, r[:, 0:512], aconv[:, t * 4:t * 4 + 1], None, ALU.mult, after=[A()])
                for j in range(1, 4):
                    stt(acc, r[:, j:j + 512], aconv[:, t * 4 + j:t * 4 + j + 1], acc, ALU.mult, ALU.add)
                act(QK[:, t, :], acc, ACT.Silu, after=[D()])
            return f

        lin(H, 8, "e_in", 0, 512, True, ev_qk(0), [xt_tok])
        lin(H, 8, "e_in", 512, 512, True, ev_qk(1))

        def ev_k(m, ps):
            evc(KCV[:, m, :] if m < 2 else KSW[:, m - 2, :], ps[:, :], [E()])
        lin(H, 8, "e_in", 1024, 512, True, ev_k)
        lin(H, 8, "e_in", 1536, 512, True, lambda m, ps: evc(BQ[:, m, :], ps[:, :], [E()], scale=0.125))
        lin(H, 8, "e_in", 2048, 512, False,
            lambda m, ps: evc(AV[:, m, :, 0:128], ps[:, :].rearrange("p (h d) -> p h d", h=4), [E()]))
        lin(H, 8, "e_in", 2560, 512, False, lambda m, ps: act(AO[:, m, :], ps[:, :], ACT.Sigmoid, after=[E()]))

        w, tok, slot = load("e_in", 0, 8, 3072, 288)
        bs = [bank() for _ in range(4)]
        for m in range(4):
            for k in range(8):
                mm(bs[m].t[:, 0:280], H[:, k, m * 128:(m + 1) * 128], w[:, k, 0:280], k == 0, k == 7, [tok] + bs[m].free)
            vcp(VSW[:, m, :], bs[m].t[:, 0:256], [E()])
            tt(GT[:, m, :], bs[m].t[:, 256:280], cst("gb"), ALU.add)
            bs[m].free = AD()
        act(GT, GT, ACT.Sigmoid, after=[D()])
        rows = YA[0:4, :, :].rearrange("p a b -> p (a b)")
        R = [rows[:, i * 512:(i + 1) * 512] for i in range(8)]
        for i in range(2):
            b = bank()
            for k in range(8):
                mm(b.t[0:4, :], w[:, k, 280 + 4 * i:284 + 4 * i], H[:, k, :], k == 0, k == 7, b.free)
            ts(R[i], b.t[0:4, :], cst("aib" if i == 0 else "afb")[0:4, :], None, ALU.add, after=[E()])
            b.free = AD()
        release(slot, [E()])
        stt(R[2], R[1], -1.0, R[1], ALU.mult, ALU.max)
        act(R[2], R[2], ACT.Exp, scale=-1.0, after=[D()])
        act(R[2], R[2], ACT.Ln, bias=ones[0:4, 0:1])
        stt(R[1], R[1], 0.0, R[2], ALU.min, ALU.subtract, [A()])
        scan(R[3], bc(ones[0:4, 0:1], [4, 512]), R[1], 0.0, ALU.mult, ALU.add)
        tt(R[4], R[0], R[3], ALU.subtract)
        scan(R[5], R[4], R[4], 0.0, ALU.max, ALU.max)
        tt(R[6], R[3], R[5], ALU.add)
        act(R[6], R[6], ACT.Exp, scale=-1.0, after=[D()])
        cols = SM[:, 32:64].rearrange("p (a b c) -> p a b c", a=2, b=4)
        b = bank()
        for a_, r in ((0, R[4]), (1, R[6])):
            for j in range(4):
                tr(b.t[:, (a_ * 4 + j) * 4:(a_ * 4 + j) * 4 + 4], r[:, j * 128:(j + 1) * 128], AD() + b.free)
        vcp(SM[:, 32:64], b.t[:, 0:32], [E()])
        b.free = AD()
        ar.at(base)
        PT = ar.take(2, 4, 512)
        tmp = ar.take(512)
        hs = ar.take(128)
        for h in range(4):
            pt = PT[:, h % 2, :, :]
            mb = bank()
            mm(mb.t[:, :], sel[0:4, h * 128:(h + 1) * 128], R[5], True, True, AD() + mb.free)
            etok = E()
            for i in range(4):
                n = 512 - 128 * i
                s = bank()
                mm(s.t[:, 0:n], QK[:, 4 + h, i * 128:(i + 1) * 128], QK[:, h, i * 128:512], True, True, AD() + s.free)
                ts(tmp[:, 0:n], mb.t[:, i * 128:512], cols[:, 0, i, h:h + 1], 0.0, ALU.subtract, ALU.max,
                   after=[etok, A()])
                act(pt[:, i, i * 128:512], tmp[:, 0:n], ACT.Exp, scale=-1.0, after=[D(), E()])
                tt(pt[:, i, i * 128:(i + 1) * 128], pt[:, i, i * 128:(i + 1) * 128], cst("tmask"), ALU.mult, after=[A()])
                stt(pt[:, i, i * 128:512], s.t[:, 0:n], 128.0 ** -0.5, pt[:, i, i * 128:512], ALU.mult, ALU.mult,
                    [E(), A()])
                s.free = AD()
            mb.free = AD()
            for jp in range(2):
                b = bank()
                for jj in range(2):
                    j = jp * 2 + jj
                    for i in range(j + 1):
                        mm(b.t[:, jj * 129:(jj + 1) * 129], pt[:, i, j * 128:(j + 1) * 128], AV[:, i, h, :], i == 0,
                           i == j, AD() + b.free)
                for jj in range(2):
                    j = jp * 2 + jj
                    d = SM[:, 64:65]
                    vcp(SM[:, 65:66], b.t[:, jj * 129 + 128:jj * 129 + 129], [E()])
                    stt(d, SM[:, 65:66], -1.0, SM[:, 65:66], ALU.mult, ALU.max)
                    tt(d, d, cols[:, 1, j, h:h + 1], ALU.max)
                    recip(d, d)
                    ts(hs, b.t[:, jj * 129:jj * 129 + 128], d, None, ALU.mult)
                    bns(SM[:, 66:72], hs)
                    bna(SM[:, 72:74], SM[:, 66:72])
                    rsq(SM[:, 74:75], SM[:, 73:74], 1.0, 1e-5)
                    ya = QK[:, h, j * 128:(j + 1) * 128]
                    ts(ya, hs, SM[:, 72:73], SM[:, 74:75], ALU.subtract, ALU.mult, after=[E()])
                b.free = AD()
        for j in range(4):
            y = YA[:, j, 0:512]
            qv = QK[:, 0:4, j * 128:(j + 1) * 128]
            tt(y.rearrange("p (h d) -> p h d", h=4), qv, cst("anorm").rearrange("p (h d) -> p h d", h=4), ALU.mult,
               after=[E(), A()])
            tt(y, y, AO[:, j, :], ALU.mult)
        dump("ya", YA[:, :, 0:512], [128, 4, 512])

        ar.at(0)
        blk = ar.take(32, 31)
        PP = ar.take(2, 512)
        PT2 = ar.take(2, 512)
        hid = ar.take(2, 64)
        assert ar.o <= 4096
        ar.at(base)
        kc = ar.take(31)
        vc = ar.take(2, 64)
        PC = ar.take(8, 32)
        PCT = ar.take(8, 128)
        rc = ar.take(3, 8)
        cpos = cst("cpos")
        for jj in range(2):
            w, tok, slot = load("cw1", jj, 1, 0, 4096)
            u = KCV[:, jj, :].rearrange("p (m l) -> p l m", l=16)
            pb = cpos[:, jj * 32:(jj + 1) * 32].unsqueeze(2)
            tt(blk[:, 0:16, :], u[:, :, 0:31], bc(pb[:, 0:16, :], [128, 16, 31]), ALU.add, after=[E(), A()])
            tt(blk[:, 16:32, :], u[:, :, 1:32], bc(pb[:, 16:32, :], [128, 16, 31]), ALU.add)
            hb = [bank(), bank()]
            for g in range(2):
                for l in range(32):
                    mm(hb[g].t[:, 0:31], w[64 * g:64 * g + 64, 0, l * 128:(l + 1) * 128],
                       blk[64 * g:64 * g + 64, l, :], l == 0, l == 31, [tok, D()] + hb[g].free)
            release(slot, [E()])
            for g in range(2):
                act(hid[:, jj, g * 32:g * 32 + 31], hb[g].t[:, 0:31], ACT.Gelu_apprx_tanh, after=[E()])
                hb[g].free = AD()
            b = bank()
            cw2 = cst("cw2")[:, jj * 64:(jj + 1) * 64]
            for g in range(2):
                if jj == 0:
                    mm(b.t[64 * g:64 * g + 64, 0:31], cw2, hid[:, 0, g * 32:g * 32 + 31], True, True, [A()] + b.free)
                else:
                    mm(b.t[0:31, g * 64:(g + 1) * 64], hid[:, 1, g * 32:g * 32 + 31], cw2, True, True, [A()] + b.free)
            if jj == 0:
                vcp(kc, b.t[:, 0:31], [E()])
            else:
                vcp(vc[0:31, :, :].rearrange("p a b -> p (a b)"), b.t[0:31, 0:128], [E()])
            b.free = AD()
        dump("kc", kc, [128, 31])
        ca, c01 = cst("cmpadd"), cst("cmp01")
        for i in range(4):
            cb = [bank(), bank()]
            for h in range(8):
                g, j = h // 4, h % 4
                mm(cb[g].t[:, j * 32:j * 32 + 31], BQ[64 * g:64 * g + 64, j, i * 128:(i + 1) * 128], kc[64 * g:64 * g + 64, :], True,
                   True, AD() + cb[g].free)
            pc = PC[:, :, 0:31]
            for g in range(2):
                tt(PC[:, 4 * g:4 * g + 4, 0:31], cb[g].t[:, 0:128].rearrange("p (h m) -> p h m", h=4)[:, :, 0:31],
                   bc(ca[:, i * 31:(i + 1) * 31].unsqueeze(1), [128, 4, 31]), ALU.add, after=[E()])
                cb[g].free = AD()
            red(rc[:, 0, :], pc, ALU.max)
            tt(pc, pc, bc(rc[:, 0, :].unsqueeze(2), [128, 8, 31]), ALU.subtract)
            act(pc, pc, ACT.Exp, after=[D()])
            red(rc[:, 1, :], pc, ALU.add, after=[A()])
            tt(pc, pc, bc(c01[:, i * 31:(i + 1) * 31].unsqueeze(1), [128, 8, 31]), ALU.mult)
            recip(rc[:, 2, :], rc[:, 1, :])
            tt(rc[:, 2, :], rc[:, 2, :], GT[:, i, 0:24:3], ALU.mult)
            for hh in range(2):
                b = bank()
                for q in range(4):
                    tr(b.t[0:31, q * 128:(q + 1) * 128], PC[:, hh * 4 + q, 0:31], [D()] + b.free)
                evc(PCT[0:31, hh * 4:hh * 4 + 4, :].rearrange("p a b -> p (a b)"), b.t[0:31, :], [E()])
                b.free = AD()
            b = bank()
            for h in range(8):
                mm(b.t[:, h * 64:(h + 1) * 64], PCT[0:31, h, :], vc[0:31, h // 4, :], True, True, AD() + b.free)
            tt(YA[:, i, 512:1024].rearrange("p (h d) -> p h d", h=8), b.t[:, :].rearrange("p (h d) -> p h d", h=8),
               bc(rc[:, 2, :].unsqueeze(2), [128, 8, 64]), ALU.mult, after=[E()])
            b.free = AD()
            n = 128 * (i + 1)
            for h in range(8):
                g, j = h // 4, h % 4
                for br in range(2):
                    s = bank()
                    sl = slice(64 * g, 64 * g + 64)
                    mm(s.t[:, 0:n], BQ[sl, j, i * 128:(i + 1) * 128], KSW[sl, br, 0:n], True, False, AD() + s.free)
                    mm(s.t[:, n - 128:n], ident, cst("cmask"), False, True)
                    x = 80 + 4 * br
                    red(SM[:, x:x + 1], s.t[:, 0:n], ALU.max, neg=True, after=[E()])
                    pp = PP[:, br, 0:n]
                    act(pp, s.t[:, 0:n], ACT.Exp, bias=SM[:, x:x + 1], accum=SM[:, x + 1:x + 2], after=[D(), E()])
                    s.free = AD()
                    recip(SM[:, x + 2:x + 3], SM[:, x + 1:x + 2], after=[A()])
                    tt(SM[:, x + 2:x + 3], SM[:, x + 2:x + 3], GT[:, i, 3 * h + 1 + br:3 * h + 2 + br], ALU.mult)
                    b = bank()
                    for k in range(i + 1):
                        tr(b.t[:, k * 128:(k + 1) * 128], PP[:, br, k * 128:(k + 1) * 128], [A()] + b.free)
                    evc(PT2[:, br, 0:n], b.t[:, 0:n], [E()])
                    b.free = AD()
                    b = bank()
                    for k in range(i + 1):
                        mm(b.t[:, 0:64], PT2[:, br, k * 128:(k + 1) * 128], VSW[:, k, br * 128 + 64 * g:br * 128 + 64 * g + 64],
                           k == 0, k == i, AD() + b.free)
                    y = YA[:, i, 512 + 64 * h:576 + 64 * h]
                    stt(y, b.t[:, 0:64], SM[:, x + 2:x + 3], y, ALU.mult, ALU.add, [E()])
                    b.free = AD()
        dump("yb", YA[:, :, 512:1024], [128, 4, 512])
        to_fm(YA, H, 8, after=AD() + [E()])
        lin(H, 8, "e_out", 0, 512, False, res_add(ALPHA, None, 0), AD() + [x_tok])
        lin(H, 8, "e_out", 512, 512, False, res_add(ALPHA, None, 512))

    def mlp_ple(l):
        layer_norm(f"ln1_{l}")
        to_fm(X, H, 8, after=[D(), E()])
        dump(f"ln1_{l}", X[:, :, :], [128, 4, 1024])
        ar = Arena()
        U = ar.take(32, 512)
        tmp = ar.take(2, 512)
        for c in range(8):
            def ev(m, ps, c=c):
                u = U[:, c * 4 + m, :]
                act(u, ps[:, :], ACT.Relu, after=[E()])
                tt(u, u, u, ALU.mult, after=[A()])
            lin(H, 8, f"w1_{l}", c * 512, 512, True, ev, AD())
        for c in range(2):
            lin(U, 32, f"w2_{l}", c * 512, 512, False, res_add(ALPHA, None, c * 512), AD())
        layer_norm(f"ln2_{l}")
        to_fm(X, H, 8, after=[D(), E()])
        w, tok, slot = load(f"pT_{l}", 0, 2, 0, 512)
        pT = ar.take(2, 512)
        vcp(pT, w, [tok, E()])
        release(slot, [D()])
        for c in range(2):
            gb = [bank() for _ in range(4)]
            gw, gtok, gs = load(f"pgw_{l}", 0, 8, c * 512, 512)
            pw, ptok, pslot = load(f"pw_{l}", 0, 2, c * 512, 512)
            for m in range(4):
                for k in range(8):
                    mm(gb[m].t[:, :], H[:, k, m * 128:(m + 1) * 128], gw[:, k, :], k == 0, k == 7, [gtok] + AD() + gb[m].free)
                act(tmp[:, m % 2, :], gb[m].t[:, :], ACT.Sigmoid, after=[E(), D()])
                gb[m].free = AD()
                b = bank()
                for k in range(2):
                    mm(b.t[:, :], pT[:, k, m * 128:(m + 1) * 128], pw[:, k, :], k == 0, k == 1, [ptok, D()] + b.free)
                tt(tmp[:, m % 2, :], tmp[:, m % 2, :], b.t[:, :], ALU.mult, after=[E(), A()])
                tt(X[:, m, c * 512:(c + 1) * 512], X[:, m, c * 512:(c + 1) * 512], tmp[:, m % 2, :], ALU.add)
                b.free = AD()
            release(gs, [E()])
            release(pslot, [E()])
        dump(f"h_{l}", X[:, :, :], [128, 4, 1024])

    def odd_mixer():
        to_fm(X, H, 8, after=[D(), A(), E()])
        ar = Arena()
        CKV = ar.take(4, 256)
        CKT = ar.take(2, 512)
        KRT = ar.take(512)
        KIT = ar.take(512)
        WI = ar.take(4, 8)
        MADD = ar.take(3, 512)
        TAB = ar.take(4, 96)
        CQT = ar.take(4, 512)
        QRT = ar.take(4, 512)
        QN = ar.take(8, 512)
        base = ar.o
        CQ = ar.take(4, 512)
        KD = ar.take(4, 256)
        tmp = ar.take(512)
        ANG = ar.take(4, 48)
        KK = ar.take(4, 48)
        RR = ar.take(4, 48)
        pf = SM[:, 90:94]
        vcp(pf, POS[:, :], [pos_tok])
        tt(ANG, bc(pf.unsqueeze(2), [128, 4, 48]), bc(cst("invf").unsqueeze(1), [128, 4, 48]), ALU.mult)
        MAGIC = 12582912.0
        TWO_PI = (6.28125, 0.0019350051879882812, 3.0199160517e-07)
        for which in range(2):
            ts(KK, ANG, 1.0 / (2.0 * np.pi), 0.25 if which == 0 else 0.0, ALU.mult, ALU.add, after=[A()])
            ts(KK, KK, MAGIC, None, ALU.add)
            ts(KK, KK, MAGIC, None, ALU.subtract)
            stt(RR, KK, -TWO_PI[0], ANG, ALU.mult, ALU.add)
            stt(RR, KK, -TWO_PI[1], RR, ALU.mult, ALU.add)
            stt(RR, KK, -TWO_PI[2], RR, ALU.mult, ALU.add)
            if which == 0:
                ts(RR, RR, float(np.pi / 2), None, ALU.add)
            ts(RR, RR, 3.1415925, -3.1415925, ALU.min, ALU.max)
            act(TAB[:, :, 32 * which:32 * which + 32], RR[:, :, 0:32], ACT.Sin, after=[D()])
            act(TAB[:, :, 64 + 16 * which:80 + 16 * which], RR[:, :, 32:48], ACT.Sin)
        dump("tab", TAB, [128, 4, 96])

        def rope(dst, src, j, half, heads, t1, after=()):
            o = 0 if half == 32 else 64
            cs = bc(TAB[:, j, o:o + half].unsqueeze(1), [128, heads, half])
            sn = bc(TAB[:, j, o + half:o + 2 * half].unsqueeze(1), [128, heads, half])
            x1, x2 = src[:, :, 0:half], src[:, :, half:2 * half]
            tv = t1.rearrange("p (h d) -> p h d", h=heads)
            tt(tv, x2, sn, ALU.mult, after=after)
            tt(dst[:, :, 0:half], x1, cs, ALU.mult)
            tt(dst[:, :, 0:half], dst[:, :, 0:half], tv, ALU.subtract)
            tt(tv, x1, sn, ALU.mult)
            tt(dst[:, :, half:2 * half], x2, cs, ALU.mult)
            tt(dst[:, :, half:2 * half], dst[:, :, half:2 * half], tv, ALU.add)

        lin(H, 8, "o_in", 0, 512, False, lambda m, ps: evc(CQ[:, m, :], ps[:, :], [E()]), AD())
        for m in range(4):
            rms_rows(CQ[:, m, :], tmp, CQ[:, m, :], 512, None, 1e-5)
        to_fm(CQ, CQT, 4, gain=cst("qnorm"), after=[D()])

        def ev2(m, ps):
            kv = CKV[:, m, :]
            evc(tmp[:, 0:392], ps[:, 0:392], [E(), D(), A()])
            a0 = [A(), D()]
            act(kv, tmp[:, 0:256], ACT.Square, accum=SM[:, 95:96], after=a0)
            ts(SM[:, 96:97], SM[:, 95:96], 1.0 / 256, 1e-5, ALU.mult, ALU.add, after=[A()])
            pw(SM[:, 96:97])
            ts(kv, tmp[:, 0:256], SM[:, 96:97], None, ALU.mult)
            tt(kv, kv, cst("kvnorm"), ALU.mult)
            rope(KD[:, m, 0:64].unsqueeze(1), tmp[:, 256:320].unsqueeze(1), m, 32, 1, tmp[:, 400:432])
            vcp(KD[:, m, 64:128], KD[:, m, 0:64])
            bns(SM[:, 98:104], tmp[:, 320:384])
            bna(SM[:, 104:106], SM[:, 98:104])
            rsq(SM[:, 106:107], SM[:, 105:106], 1.0, 1e-5)
            ki = KD[:, m, 128:192]
            ts(ki, tmp[:, 320:384], SM[:, 104:105], SM[:, 106:107], ALU.subtract, ALU.mult)
            tt(ki, ki, cst("ikg"), ALU.mult)
            tt(ki, ki, cst("ikb"), ALU.add)
            rope(KD[:, m, 192:224].unsqueeze(1), KD[:, m, 128:160].unsqueeze(1), m, 16, 1, tmp[:, 400:416])
            vcp(KD[:, m, 128:160], KD[:, m, 192:224])
            vcp(KD[:, m, 192:256], KD[:, m, 128:192])
            ts(WI[:, m, :], tmp[:, 384:392], float(8 ** -0.5 * 64 ** -0.5), None, ALU.mult)
        lin(H, 8, "o_in", 512, 392, False, ev2, AD())
        to_fm(CKV, CKT, 2, after=[D()])
        for f, dst in ((0, KRT), (1, KIT)):
            b = bank()
            for j in range(4):
                tr(b.t[:, j * 128:(j + 1) * 128], KD[:, j, f * 128:(f + 1) * 128], [D()] + b.free)
            evc(dst, b.t[:, :], [E()])
            b.free = AD()
        dump("ckv", CKV, [128, 4, 256])
        dump("krt", KRT, [128, 512])
        dump("kit", KIT, [128, 512])
        QR = CQ
        def ev3(m, ps):
            evc(tmp, ps[:, :], [E(), D(), A()])
            rope(QR[:, m, :].rearrange("p (h d) -> p h d", h=8), tmp.rearrange("p (h d) -> p h d", h=8), m, 32, 8,
                 KD2, after=[A(), D(), E()])
        KD2 = ar.take(256)
        lin(CQT, 4, "o_qb", 1024, 512, False, ev3, AD())
        to_fm(QR, QRT, 4, after=[D()])
        dump("qrt", QRT, [128, 4, 512])
        for c in range(2):
            lin(CQT, 4, "o_qb", c * 512, 512, True,
                lambda m, ps, c=c: evc(QN[:, c * 4 + m, :], ps[:, :], [E()]), AD())
        w, tok, slot = load("o_iq", 0, 4, 0, 512)
        ar.at(base)
        QIT = ar.take(4, 384)
        QI = ar.take(3, 512)
        tmp = ar.take(512)
        t2 = ar.take(256)
        ISC = ar.take(3, 512)
        RL = ar.take(2, 512)
        m8 = ar.take(8)
        for q in range(3):
            m = 1 + q
            b = bank()
            for k in range(4):
                mm(b.t[:, :], CQT[:, k, m * 128:(m + 1) * 128], w[:, k, :], k == 0, k == 3, [tok] + AD() + b.free)
            act(tmp, b.t[:, :], ACT.Copy, after=[E(), D()])
            b.free = AD()
            qv = QI[:, q, :].rearrange("p (h d) -> p h d", h=8)
            tv = tmp.rearrange("p (h d) -> p h d", h=8)
            rope(qv[:, :, 0:32], tv[:, :, 0:32], m, 16, 8, t2[:, 0:128], after=[A(), E()])
            vcp(qv[:, :, 32:64], tv[:, :, 32:64])
        release(slot, [E()])
        for f in range(4):
            b = bank()
            for q in range(3):
                tr(b.t[:, q * 128:(q + 1) * 128], QI[:, q, f * 128:(f + 1) * 128], [D(), A()] + b.free)
            evc(QIT[:, f, :], b.t[:, 0:384], [E()])
            b.free = AD()
        for q in range(3):
            m = 1 + q
            n = 128 * (m + 1)
            isc = ISC[:, q, :]
            if n < 512:
                P.op("dve", lambda e, a=isc[:, n:512]: e.memset(a, NEG))
            for h in range(8):
                b = bank()
                sl = slice(64 * (h % 2), 64 * (h % 2) + 64)
                mm(b.t[:, 0:n], QIT[sl, h // 2, q * 128:(q + 1) * 128], KIT[sl, 0:n], True, True, AD() + b.free)
                act(RL[:, h % 2, 0:n], b.t[:, 0:n], ACT.Relu, after=[E(), D()])
                b.free = AD()
                if h == 0:
                    ts(isc[:, 0:n], RL[:, 0, 0:n], WI[:, m, 0:1], None, ALU.mult, after=[A()])
                else:
                    stt(isc[:, 0:n], RL[:, h % 2, 0:n], WI[:, m, h:h + 1], isc[:, 0:n], ALU.mult, ALU.add, [A()])
            tt(isc[:, n - 128:n], isc[:, n - 128:n], cst("cmask"), ALU.add)
            dump(f"isc{q}", isc, [128, 512])
            for it in range(16):
                top8(m8, isc)
            ts(MADD[:, q, :], isc, -2.0e38, NEG, ALU.is_gt, ALU.mult)
            dump(f"madd{q}", MADD[:, q, :], [128, 512])
        ar.at(base)
        QA = ar.take(2, 2, 512)
        PP = ar.take(2, 512)
        PT = ar.take(4, 512)
        OL = ar.take(2, 2, 512)
        assert ar.o <= NA
        uk, ktok, kslot = load("o_uk", 0, 1, 0, 2048)
        uv, vtok, vslot = load("o_uv", 0, 2, 0, 1024)
        SC = float((128 + 64) ** -0.5)
        for h in range(8):
            qa = QA[:, h % 2, :, :]
            for c in range(2):
                b = bank()
                mm(b.t[:, :], uk[:, 0, h * 256 + c * 128:h * 256 + (c + 1) * 128], QN[:, h, :], True, True,
                   [ktok] + AD() + b.free)
                evc(qa[:, c, :], b.t[:, :], [E()])
                b.free = AD()
            sl = slice(64 * (h % 2), 64 * (h % 2) + 64)
            for i in range(4):
                n = 128 * (i + 1)
                s = bank()
                mm(s.t[:, 0:n], qa[:, 0, i * 128:n], CKT[:, 0, 0:n], True, False, AD() + s.free)
                mm(s.t[:, 0:n], qa[:, 1, i * 128:n], CKT[:, 1, 0:n], False, False)
                mm(s.t[:, 0:n], QRT[sl, h // 2, i * 128:n], KRT[sl, 0:n], False, False)
                if i < 1:
                    mm(s.t[:, n - 128:n], ident, cst("cmask"), False, True)
                else:
                    mm(s.t[:, 0:n], ident, MADD[:, i - 1, 0:n], False, True)
                x = 110 + 4 * (i % 2)
                pp = PP[:, i % 2, 0:n]
                red(SM[:, x:x + 1], s.t[:, 0:n], ALU.max, neg=True, after=[E()])
                ts(SM[:, x:x + 1], SM[:, x:x + 1], SC, None, ALU.mult)
                act(pp, s.t[:, 0:n], ACT.Exp, bias=SM[:, x:x + 1], scale=SC, accum=SM[:, x + 1:x + 2], after=[D(), E()])
                s.free = AD()
                recip(SM[:, x + 2:x + 3], SM[:, x + 1:x + 2], after=[A()])
                ts(pp, pp, SM[:, x + 2:x + 3], None, ALU.mult)
                b = bank()
                for k in range(i + 1):
                    tr(b.t[:, k * 128:(k + 1) * 128], PP[:, i % 2, k * 128:(k + 1) * 128], [D()] + b.free)
                evc(PT[:, 0:i + 1, i * 128:n], b.t[:, 0:n].rearrange("p (k t) -> p k t", t=128), [E()])
                b.free = AD()
            ol = OL[:, h % 2, :, :]
            for c in range(2):
                b = bank()
                for k in range(4):
                    mm(b.t[:, 128 * k:512], CKV[:, k, c * 128:(c + 1) * 128], PT[:, k, 128 * k:512], k == 0, k == 3,
                       AD() + b.free)
                evc(ol[:, c, :], b.t[:, :], [E()])
                b.free = AD()
            b = bank()
            for c in range(2):
                mm(b.t[:, :], uv[:, c, h * 128:(h + 1) * 128], ol[:, c, :], c == 0, c == 1, [vtok] + AD() + b.free)
            evc(H[:, h, :], b.t[:, :], [E()])
            b.free = AD()
        release(kslot, [E()])
        release(vslot, [E()])
        lin(H, 8, "o_out", 0, 512, False, res_add(ALPHA, None, 0), AD())
        lin(H, 8, "o_out", 512, 512, False, res_add(ALPHA, None, 512))

    def rms_to_fm(gain):
        ar = Arena()
        tmp = ar.take(1024)
        xn = ar.take(4, 1024)
        P.op("act", lambda e: e.activation(SM[:, 200:201], SM[:, 201:202], ACT.Copy), [E(), D()])
        for j in range(4):
            rms_rows(X[:, j, :], tmp, xn[:, j, :], 1024, None, 1e-6)
        to_fm(xn, H, 8, gain=gain, after=[D(), E()])

    def ffn(l, which):
        rms_to_fm(cst("nf1" if which == 1 else "nf2")[:, 8 * l:8 * l + 8])
        ar = Arena()
        U = ar.take(22, 512)
        for c in range(6):
            nc_ = 512 if c < 5 else 256

            def evg(m, ps, c=c):
                act(U[:, c * 4 + m, :], ps[:, :], ACT.Silu, after=[E(), D()])

            def evu(m, ps, c=c):
                tt(U[:, c * 4 + m, :], U[:, c * 4 + m, :], ps[:, :], ALU.mult, after=[E(), A()])
            lin(H, 8, f"fg{which}_{l}", c * 512, nc_, True, evg, AD())
            lin(H, 8, f"fu{which}_{l}", c * 512, nc_, True, evu, AD())
        for c in range(2):
            lin(U, 22, f"fd{which}_{l}", c * 512, 512, False, res_add(None, 0.5, c * 512), AD())
        dump(f"f{which}_{l}", X[:, :, :], [128, 4, 1024])

    def hybrid(l):
        key = f"win_{l}"
        rms_to_fm(cst("nmix")[:, 8 * l:8 * l + 8])
        ar = Arena()
        GD = ar.take(12, 512)
        GZ = ar.take(4, 512)
        HQ = ar.take(2, 512)
        HK = ar.take(2, 512)
        CUM = ar.take(2, 512)
        HI = ar.take(4, 256)
        HG = ar.take(4, 256)
        XC = ar.take(2, 512)
        RG = ar.take(2, 512)
        GROW = ar.take(3, 512)
        base = ar.o
        raw = ar.take(2, 516)
        acc = ar.take(512)
        LB = SM[:, 120:124]
        start_act = [E(), D(), A()]
        P.op("pool", lambda e: e.memset(raw[:, :, 0:3], 0.0), [E(), D(), A()])
        g0 = G()
        if l == 0:
            P.op("dve", lambda e: e.memset(LB[:, 0:2], 0.0))
        else:
            hl = cst("hlb")
            s = SM[:, 124:140]
            tt(s[:, 0:2], hl[:, 0:2], hl[:, 2:4], ALU.max)
            tt(s[:, 2:4], hl[:, 0:2], s[:, 0:2], ALU.subtract)
            tt(s[:, 4:6], hl[:, 2:4], s[:, 0:2], ALU.subtract)
            act(s[:, 2:6], s[:, 2:6], ACT.Exp, after=[D()])
            tt(s[:, 6:8], s[:, 2:4], s[:, 4:6], ALU.add, after=[A()])
            recip(s[:, 6:8], s[:, 6:8])
            tt(s[:, 8:10], s[:, 2:4], s[:, 6:8], ALU.mult)
            tt(s[:, 10:12], s[:, 4:6], s[:, 6:8], ALU.mult)
            tt(s[:, 12:14], s[:, 8:10], s[:, 10:12], ALU.add)
            tt(LB[:, 0:2], s[:, 12:14], s[:, 8:10], ALU.subtract)
        ts(LB[:, 2:4], LB[:, 0:2], -1.0, 1.0, ALU.mult, ALU.add)

        def ev_hg(m, ps):
            if m < 2:
                act(HQ[:, m, :], ps[:, :], ACT.Silu, after=[E(), D()])
            else:
                m -= 2
                act(HK[:, m, :], ps[:, :], ACT.Sigmoid, after=[E(), D()])
                ts(CUM[:, m, :], HK[:, m, :], LB[:, 2 + m:3 + m], LB[:, m:m + 1], ALU.mult, ALU.add, after=[A()])
                ts(HK[:, m, :], CUM[:, m, :], -1.0, 1.0, ALU.mult, ALU.add)
                ts(CUM[:, m, :], CUM[:, m, :], 6.0e-20, None, ALU.max)
        lin(H, 8, key, 0, 512, True, ev_hg, AD())
        ts(HQ, HQ, 64.0 ** -0.5, None, ALU.mult, after=[A()])
        gconv = cst("gconv")[:, 48 * l:48 * l + 48]
        rconv = cst("rconv")[:, 8 * l:8 * l + 8]

        def conv_to(dst, ps, w, t, fin):
            r = raw[:, t % 2, :]
            act(r[:, 3:515], ps[:, :], ACT.Copy, after=[E(), D(), g0])
            ts(acc, r[:, 0:512], w[:, 0:1], None, ALU.mult, after=[A()])
            for j in range(1, 4):
                stt(acc, r[:, j:j + 512], w[:, j:j + 1], acc, ALU.mult, ALU.add)
            if fin is None:
                act(dst, acc, ACT.Silu, after=[D()])
            else:
                ts(dst, acc, fin, None, ALU.add)
        for c in range(3):
            lin(H, 8, key, 512 + c * 512, 512, True,
                lambda m, ps, c=c: conv_to(GD[:, c * 4 + m, :], ps, gconv[:, (c * 4 + m) * 4:(c * 4 + m) * 4 + 4], m, None),
                AD())

        def ev_rg(m, ps):
            if m < 2:
                conv_to(XC[:, m, :], ps, rconv[:, m * 4:m * 4 + 4], m, cst("rconvb")[:, 2 * l + m:2 * l + m + 1])
            else:
                act(RG[:, m - 2, :], ps[:, :], ACT.Gelu_apprx_tanh, after=[E(), D()])
        lin(H, 8, key, 2048, 512, True, ev_rg, AD())

        def ev_ig(m, ps):
            vcp(HI[:, m, :], ps[:, 0:256], [E()])
            act(HG[:, m, :], ps[:, 256:512], ACT.Silu, after=[E(), D()])
        lin(H, 8, key, 2560, 512, False, ev_ig, AD())
        lin(H, 8, key, 3072, 512, False, lambda m, ps: act(GZ[:, m, :], ps[:, :], ACT.Silu, after=[E()]), AD())
        w, tok, slot = load(key, 0, 8, 3584, 8)
        for i in range(2):
            b = bank()
            for k in range(8):
                mm(b.t[0:4, :], w[:, k, 4 * i:4 * i + 4], H[:, k, :], k == 0, k == 7, [tok] + b.free)
            r = GROW[0:4, i, :]
            if i == 0:
                act(r, b.t[0:4, :], ACT.Sigmoid, after=[E()])
            else:
                ts(r, b.t[0:4, :], cst("gdt")[0:4, l:l + 1], None, ALU.add, after=[E()])
                t3 = GROW[0:4, 2, :]
                stt(t3, r, -1.0, r, ALU.mult, ALU.max)
                act(t3, t3, ACT.Exp, scale=-1.0, after=[D()])
                act(t3, t3, ACT.Ln, bias=ones[0:4, 0:1])
                stt(t3, r, 0.0, t3, ALU.max, ALU.add, [A()])
                act(SM[0:4, 142:143], cst("galog")[0:4, l:l + 1], ACT.Exp)
                ts(t3, t3, SM[0:4, 142:143], -1.0, ALU.mult, ALU.mult, after=[A()])
                for j in range(4):
                    scan(r[:, j * 128:(j + 1) * 128], bc(ones[0:4, 0:1], [4, 128]), t3[:, j * 128:(j + 1) * 128], 0.0,
                         ALU.mult, ALU.add)
            b.free = AD()
        release(slot, [E()])

        ar.at(base)
        LA = ar.take(2, 512)
        IG = ar.take(2, 512)
        TA = ar.take(2, 512)
        TBf = ar.take(2, 512)
        w, tok, slot = load(f"rgw_{l}", 0, 1, 0, 512)
        lam = cst("rlam")[:, 2 * l:2 * l + 2]
        s = SM[:, 144:148]
        stt(s[:, 0:2], lam, -1.0, lam, ALU.mult, ALU.max)
        act(s[:, 0:2], s[:, 0:2], ACT.Exp, scale=-1.0, after=[D()])
        act(s[:, 0:2], s[:, 0:2], ACT.Ln, bias=ones[:, 0:1])
        ts(s[:, 2:4], lam, -1.0, 0.0, ALU.mult, ALU.max, after=[A()])
        tt(s[:, 0:2], s[:, 0:2], s[:, 2:4], ALU.add)
        ts(s[:, 0:2], s[:, 0:2], -8.0, None, ALU.mult)
        for m in range(2):
            for q, dst, bias in ((0, LA, "rbr"), (1, IG, "rbi")):
                b = bank()
                mm(b.t[:, :], w[:, 0, (2 * q + m) * 128:(2 * q + m + 1) * 128], XC[:, m, :], True, True,
                   [tok] + AD() + b.free)
                act(dst[:, m, :], b.t[:, :], ACT.Sigmoid, bias=cst(bias)[:, 2 * l + m:2 * l + m + 1], after=[E(), D()])
                b.free = AD()
            ts(LA[:, m, :], LA[:, m, :], s[:, m:m + 1], None, ALU.mult, after=[A()])
        release(slot, [E()])
        act(TA, LA, ACT.Tanh, scale=-1.0, after=[D()])
        act(LA, LA, ACT.Exp)
        ts(TBf, TA, 1.0, None, ALU.add, after=[A()])
        recip(TBf, TBf)
        stt(TA, TA, 2.0, TBf, ALU.mult, ALU.mult)
        act(TA, TA, ACT.Sqrt, after=[D()])
        tt(IG, IG, XC, ALU.mult)
        tt(IG, IG, TA, ALU.mult, after=[A()])
        for m in range(2):
            scan(TBf[:, m, :], LA[:, m, :], IG[:, m, :], 0.0, ALU.mult, ALU.add)
            tt(H[:, 6 + m, :], TBf[:, m, :], RG[:, m, :], ALU.mult, after=[E(), A()])
        dump(f"rg_{l}", H[:, 6:8, :], [128, 2, 512])

        ar.at(base)
        XL = ar.take(2, 512)
        DF = ar.take(2, 512)
        QD = XC
        KDc = RG
        act(CUM, CUM, ACT.Ln, after=[D()])
        vcp(DF, CUM, [A(), E()])
        for m in range(2):
            for j in range(4):
                scan(CUM[:, m, j * 128:(j + 1) * 128], bc(ones[:, 0:1], [128, 128]), DF[:, m, j * 128:(j + 1) * 128], 0.0,
                     ALU.mult, ALU.add)
        dump(f"cum_{l}", CUM, [128, 2, 512])
        ET = SM[:, 150:158].rearrange("p (m j) -> p m j", m=2)
        act(ET, CUM.rearrange("p m (j t) -> p m j t", t=128)[:, :, :, 127], ACT.Exp, after=[D()])
        ST = ar.take(4, 10, 128)
        P.op("pool", lambda e: e.memset(ST, 0.0), [E(), D(), A()])
        act(QD, CUM, ACT.Exp, after=[D(), E()])
        tt(QD, QD, HQ, ALU.mult, after=[A()])
        for m in range(2):
            for j in range(4):
                t0 = slice(j * 128, (j + 1) * 128)
                ts(KDc[:, m, t0], CUM[:, m, t0], CUM[:, m, j * 128 + 127:j * 128 + 128], None, ALU.subtract)
        act(KDc, KDc, ACT.Exp, scale=-1.0, after=[D()])
        tt(KDc, KDc, HK, ALU.mult, after=[A()])
        hsl = lambda h: slice(64 * (h % 2), 64 * (h % 2) + 64)
        for j in range(1, 4):
            for h in range(4):
                b = bank()
                for i in range(j):
                    mm(b.t[:, i * 128:(i + 1) * 128], KDc[hsl(h), h // 2, i * 128:(i + 1) * 128],
                       QD[hsl(h), h // 2, j * 128:(j + 1) * 128], True, True, AD() + b.free)
                evc(ST[:, h, j * (j + 1) // 2:j * (j + 1) // 2 + j, :], b.t[:, 0:j * 128].rearrange("p (k t) -> p k t", t=128),
                    [E(), G()])
                b.free = AD()
            if j < 3:
                for m in range(2):
                    ts(KDc[:, m, 0:j * 128], KDc[:, m, 0:j * 128], ET[:, m, j:j + 1], None, ALU.mult, after=[E(), A()])
        lev = cst("lev")
        for lv in range(8):
            if lv < 7:
                Bs = 1 << lv
                nb = 512 // (2 * Bs)
                xv = XL.rearrange("p m (n b) -> p (m n) b", b=2 * Bs)
                dv_ = DF.rearrange("p m (n b) -> p (m n) b", b=2 * Bs)
                cv = CUM.rearrange("p m (n b) -> p (m n) b", b=2 * Bs)
                qv = HQ.rearrange("p m (n b) -> p (m n) b", b=2 * Bs)
                kv = HK.rearrange("p m (n b) -> p (m n) b", b=2 * Bs)
                r = bc(cv[:, :, Bs - 1:Bs], [128, 2 * nb, Bs])
                tt(dv_[:, :, Bs:2 * Bs], cv[:, :, Bs:2 * Bs], r, ALU.subtract, after=[A()])
                tt(dv_[:, :, 0:Bs], r, cv[:, :, 0:Bs], ALU.subtract)
                act(DF, DF, ACT.Exp, after=[D()])
                tt(xv[:, :, Bs:2 * Bs], dv_[:, :, Bs:2 * Bs], qv[:, :, Bs:2 * Bs], ALU.mult, after=[A(), E()])
                tt(xv[:, :, 0:Bs], dv_[:, :, 0:Bs], kv[:, :, 0:Bs], ALU.mult)
                L_, R_ = XL, XL
            else:
                L_, R_ = HK, HQ
            for h in range(4):
                b = bank()
                for j in range(4):
                    t0 = slice(j * 128, (j + 1) * 128)
                    mm(b.t[:, t0], L_[hsl(h), h // 2, t0], R_[hsl(h), h // 2, t0], True, True, AD() + b.free)
                for j in range(4):
                    t0 = slice(j * 128, (j + 1) * 128)
                    P.op("dve", lambda e, o=ST[:, h, j * (j + 1) // 2 + j, :], mk=lev[:, lv * 128:(lv + 1) * 128].bitcast(I32),
                         d=b.t[:, t0]: e.copy_predicated(o, mk, d), [E(), G(), A()])
                b.free = AD()
        
        OT = DF.rearrange("p a b -> p (a b)")
        OH = OT.rearrange("p (j c) -> p j c", j=4)
        SQ = XL.rearrange("p a b -> p (a b)")[:, 0:256]
        hnw = cst("hnw")[:, 64 * l:64 * l + 64]
        for j in range(4):
            b = bank()
            for h in range(4):
                for i in range(j + 1):
                    mm(b.t[:, h * 64:(h + 1) * 64], ST[:, h, j * (j + 1) // 2 + i, :], HI[:, i, h * 64:(h + 1) * 64],
                       i == 0, i == j, AD() + b.free)
            act(SQ, b.t[:, 0:256], ACT.Square, after=[E(), D()])
            red(SM[:, 160:164], SQ.rearrange("p (h d) -> p h d", h=4), ALU.add, after=[A()])
            rsq(SM[:, 160:164], SM[:, 160:164], 1.0 / 64, 1e-6)
            o3 = OH[:, j, :].rearrange("p (h d) -> p h d", h=4)
            tt(o3, b.t[:, 0:256].rearrange("p (h d) -> p h d", h=4), bc(SM[:, 160:164].unsqueeze(2), [128, 4, 64]), ALU.mult)
            tt(o3, o3, bc(hnw.unsqueeze(1), [128, 4, 64]), ALU.mult)
            tt(OH[:, j, :], OH[:, j, :], HG[:, j, :], ALU.mult)
            b.free = AD()
        to_fm(OH, H, 2, after=[D(), E()])
        dump(f"hg_{l}", H[:, 0:2, :], [128, 2, 512])

        hq_off = 16 * 512
        ar.at(hq_off)
        KT_ = ar.take(4, 512)
        VT_ = ar.take(4, 512)
        SCT = ar.take(4, 512)
        CB = ar.take(512)
        BB = ar.take(512)
        assert ar.o <= base - 3 * 512
        ar.at(base)
        XI = ar.take(4, 512)
        XT = ar.take(4, 512)
        LT = ar.take(4, 512)
        TM = ar.take(512)
        RL_ = ar.take(512)
        scT = lambda h: SCT[:, h, :]
        gcol = SM[:, 164:196].rearrange("p (a j h) -> p a j h", a=2, j=4)
        b = bank()
        for a_ in range(2):
            for j in range(4):
                tr(b.t[:, (a_ * 4 + j) * 4:(a_ * 4 + j) * 4 + 4], GROW[0:4, a_, j * 128:(j + 1) * 128], AD() + b.free)
        vcp(SM[:, 164:196], b.t[:, 0:32], [E()])
        b.free = AD()
        elast = SM[:, 204:220].rearrange("p (h j) -> p h j", h=4)
        tmask = cst("tmask")
        for h in range(4):
            t0s = [slice(j * 128, (j + 1) * 128) for j in range(4)]
            for a_, dst in ((1, CB), (0, BB)):
                b = bank()
                mm(b.t[:, :], sel[0:4, h * 128:(h + 1) * 128], GROW[0:4, a_, :], True, True, AD() + b.free)
                evc(dst, b.t[:, :], [E(), A(), D()])
                b.free = AD()
            for c, sc_ in ((h, 128.0 ** -0.5), (4 + h, 1.0)):
                v = GD[:, c, :]
                act(TM, v, ACT.Square, after=[D(), E()])
                b = bank()
                mm(b.t[:, :], ones, TM, True, True, [A()] + b.free)
                ts(TM, b.t[:, :], 1e-6, None, ALU.add, after=[E()])
                act(TM, TM, ACT.Sqrt, after=[D()])
                recip(TM, TM, after=[A()])
                b.free = AD()
                stt(v, v, sc_, TM, ALU.mult, ALU.mult)
            for c, dst in ((4 + h, KT_), (8 + h, VT_)):
                b = bank()
                for j in range(4):
                    tr(b.t[:, t0s[j]], GD[:, c, t0s[j]], AD() + b.free)
                evc(dst[:, h, :], b.t[:, :], [E()])
                b.free = AD()
            for j in range(4):
                ts(RL_[:, t0s[j]], CB[:, t0s[j]], gcol[:, 1, j, h:h + 1], 0.0, ALU.subtract, ALU.min,
                   after=[A(), E()])
            act(RL_, RL_, ACT.Exp, after=[D()])
            tt(RL_.rearrange("p (j t) -> p j t", j=4), RL_.rearrange("p (j t) -> p j t", j=4),
               bc(tmask.unsqueeze(1), [128, 4, 128]), ALU.mult, after=[A()])
            b = bank()
            for j in range(4):
                mm(b.t[:, t0s[j]], GD[:, 4 + h, t0s[j]], GD[:, h, t0s[j]], True, True, AD() + b.free)
            tt(scT(h), b.t[:, :], RL_, ALU.mult, after=[E()])
            b.free = AD()
            b = bank()
            for j in range(4):
                mm(b.t[:, t0s[j]], GD[:, 4 + h, t0s[j]], GD[:, 4 + h, t0s[j]], True, True, AD() + b.free)
            tt(RL_, RL_, BB, ALU.mult)
            tt(LT[:, h, :], b.t[:, :], RL_, ALU.mult, after=[E()])
            b.free = AD()
            act(TM, CB, ACT.Exp, after=[D(), E()])
            act(elast[:, h, :], CB.rearrange("p (j t) -> p j t", j=4)[:, :, 127], ACT.Exp)
            tt(GD[:, h, :], GD[:, h, :], TM, ALU.mult, after=[A(), E()])
            for j in range(4):
                s = SM[:, 224 + 4 * (j % 2):228 + 4 * (j % 2)]
                act(s[:, 0:1], gcol[:, 1, j, h:h + 1], ACT.Exp, after=[D()])
                ts(s[:, 1:2], gcol[:, 1, j, h:h + 1], CB[:, j * 128 + 127:j * 128 + 128], None, ALU.subtract)
                act(s[:, 1:2], s[:, 1:2], ACT.Exp, scale=-1.0, after=[D()])
                tt(s[:, 2:3], s[:, 0:1], gcol[:, 0, j, h:h + 1], ALU.mult, after=[A()])
                ts(VT_[:, h, t0s[j]], VT_[:, h, t0s[j]], gcol[:, 0, j, h:h + 1], None, ALU.mult)
                ts(GD[:, 8 + h, t0s[j]], KT_[:, h, t0s[j]], s[:, 2:3], None, ALU.mult, after=[E()])
                ts(KT_[:, h, t0s[j]], KT_[:, h, t0s[j]], s[:, 1:2], None, ALU.mult)
            vcp(XI[:, h, :].rearrange("p (j t) -> p j t", j=4), bc(ident.unsqueeze(1), [128, 4, 128]), [E()])
            vcp(XT[:, h, :].rearrange("p (j t) -> p j t", j=4), bc(ident.unsqueeze(1), [128, 4, 128]))
        CTs = [CB, BB]
        P1s = [TM, RL_]
        for lv in range(7):
            for h in range(4):
                ct, p1 = CTs[h % 2], P1s[h % 2]
                tt(ct.rearrange("p (j t) -> p j t", j=4), LT[:, h, :].rearrange("p (j t) -> p j t", j=4),
                   bc(lev[:, lv * 128:(lv + 1) * 128].unsqueeze(1), [128, 4, 128]), ALU.mult, after=[E(), A()])
                b = bank()
                for t0 in t0s:
                    mm(b.t[:, t0], ct[:, t0], XI[:, h, t0], True, True, AD() + b.free)
                act(p1, b.t[:, :], ACT.Copy, after=[E(), D()])
                b.free = AD()
                b = bank()
                for t0 in t0s:
                    mm(b.t[:, t0], p1[:, t0], XT[:, h, t0], True, True, AD() + b.free)
                if lv < 6:
                    b2 = bank()
                    for t0 in t0s:
                        mm(b2.t[:, t0], XT[:, h, t0], p1[:, t0], True, True, AD() + b2.free)
                    tt(XI[:, h, :], XI[:, h, :], b2.t[:, :], ALU.subtract, after=[E()])
                    b2.free = AD()
                tt(XT[:, h, :], XT[:, h, :], b.t[:, :], ALU.subtract, after=[E()])
                b.free = AD()
        dump(f"xt_{l}", XT, [128, 4, 512])
        for h in range(4):
            b = bank()
            for t0 in t0s:
                mm(b.t[:, t0], GD[:, 8 + h, t0], XT[:, h, t0], True, True, AD() + b.free)
            ts(XI[:, h, :], b.t[:, :], -1.0, None, ALU.mult, after=[E()])
            b.free = AD()
        SS = [LT[:, h, 0:128] for h in range(4)]
        VN = [LT[:, h, 128:256] for h in range(4)]
        SQ2 = [LT[:, h, 256:384] for h in range(4)]
        OG = GD[:, 4:8, :]
        gnw = cst("gnw")[:, 128 * l:128 * l + 128]
        for j in range(4):
            t0 = t0s[j]
            for h in range(4):
                b = bank()
                mm(b.t[:, 0:128], XT[:, h, t0], VT_[:, h, t0], True, j == 0, AD() + b.free)
                if j:
                    mm(b.t[:, 0:128], XI[:, h, t0], SS[h], False, True)
                evc(VN[h], b.t[:, 0:128], [E()])
                b.free = AD()
            for h in range(4):
                b = bank()
                if j:
                    mm(b.t[:, 0:128], GD[:, h, t0], SS[h], True, False, AD() + b.free)
                mm(b.t[:, 0:128], scT(h)[:, t0], VN[h], j == 0, True, AD() + b.free)
                if j < 3:
                    mm(b.t[:, 128:256], KT_[:, h, t0], VN[h], True, True)
                    if j == 0:
                        vcp(SS[h], b.t[:, 128:256], [E()])
                    else:
                        stt(SS[h], SS[h], elast[:, h, j:j + 1], b.t[:, 128:256], ALU.mult, ALU.add, [E()])
                a = SM[:, 232 + h:233 + h]
                act(SQ2[h], b.t[:, 0:128], ACT.Square, accum=a, after=[E(), D()])
                ts(a, a, 1.0 / 128, 1e-6, ALU.mult, ALU.add, after=[A()])
                pw(a)
                og = OG[:, j, h * 128:(h + 1) * 128]
                stt(og, b.t[:, 0:128], a, gnw, ALU.mult, ALU.mult, [E()])
                b.free = AD()
            tt(OG[:, j, :], OG[:, j, :], GZ[:, j, :], ALU.mult)
        to_fm(OG, H[:, 2:6, :], 4, after=[D(), E()])
        dump(f"y_{l}", H[:, :, :], [128, 8, 512])
        lin(H, 8, f"wo_{l}", 0, 512, False, res_add(None, 1.0, 0), AD())
        lin(H, 8, f"wo_{l}", 512, 512, False, res_add(None, 1.0, 512), AD())
        dump(f"m_{l}", X[:, :, :], [128, 4, 1024])

    even_mixer()
    mlp_ple(0)
    odd_mixer()
    mlp_ple(1)
    for l in range(2):
        ffn(l, 1)
        hybrid(l)
        ffn(l, 2)
    w, tok, slot = load("nfin", 0, 1, 0, 1024)
    ar = Arena()
    tmp = ar.take(1024)
    xo = ar.take(4, 1024)
    P.op("act", lambda e: e.activation(SM[:, 200:201], SM[:, 201:202], ACT.Copy), [E(), D()])
    for j in range(4):
        rms_rows(X[:, j, :], tmp, xo[:, j, :], 1024, None, 1e-6)
        tt(xo[:, j, :], xo[:, j, :], w[:, 0, :], ALU.mult, after=[tok])
    P.op("sp", lambda e, W, S: e.dma_start(W["out"], xo).then_inc(S["out"], 16), [D()])
    return P, stream


def emit(nc, ctx, P, W, n_out):
    S = {e: ctx.enter_context(nc.semaphore("s_" + e)) for e in ("pe", "act", "dve", "pool")}
    for n in ["c", "xt", "x", "pos", "out"] + [f"w{i}" for i in range(NS)]:
        S[n] = ctx.enter_context(nc.semaphore("s_" + n))
    block = ctx.enter_context(nc.Block())

    def run(eng, e):
        for fn, waits, inc in P.ops[e]:
            for s, v in waits:
                eng.wait_ge(S[s], v)
            if e == "sp":
                fn(eng, W, S)
            else:
                i = fn(eng)
                if inc:
                    i.then_inc(S[e], 1)

    @block.sync
    def _(eng):
        run(eng, "sp")
        eng.wait_ge(S["out"], 16 * n_out)

    @block.tensor
    def _(eng):
        run(eng, "pe")

    @block.scalar
    def _(eng):
        run(eng, "act")

    @block.vector
    def _(eng):
        run(eng, "dve")

    @block.gpsimd
    def _(eng):
        run(eng, "pool")


def const_block(I):
    f = np.float32
    C = np.zeros((128, NCB), f)

    def put(name, a, rows=128):
        o, w = COFF[name]
        C[:rows, o:o + w] = a.reshape(rows, w)

    def row(a):
        return np.broadcast_to(np.asarray(a).reshape(1, -1), (128, np.asarray(a).size))

    s = np.arange(128)
    put("ident", np.eye(128, dtype=f))
    lev = np.zeros((128, 8, 128), f)
    for lv in range(7):
        B = 1 << lv
        same = (s[:, None] // (2 * B)) == (s[None, :] // (2 * B))
        lev[:, lv, :] = same & ((s[:, None] // B) % 2 == 0) & ((s[None, :] // B) % 2 == 1)
    lev[:, 7, :] = np.eye(128)
    put("lev", lev)
    put("cmask", np.where(s[None, :] <= s[:, None], 0.0, NEG).astype(f))
    put("tmask", (s[:, None] <= s[None, :]).astype(f))
    put("ones", np.ones((128, 128), f))
    sel = np.zeros((128, 4, 128), f)
    for h in range(4):
        sel[h, h, :] = 1
    put("sel", sel)
    t = np.arange(4)[None, :, None] * 128 + s[:, None, None]
    ok = (np.arange(31) * 16 + 31)[None, None, :] <= t
    put("cmpadd", np.where(ok, 0.0, NEG).astype(f))
    put("cmp01", ok.astype(f))
    inv = [np.float32(10000.0) ** (-np.arange(0, d, 2, dtype=f) / np.float32(d)) for d in (64, 32)]
    put("invf", row(np.concatenate(inv).astype(f)))
    put("aconv", I["e_a_conv"][0].reshape(4, 8, 128).transpose(2, 1, 0))
    put("aib", I["e_a_i_b"][0], 4)
    put("afb", I["e_a_f_b"][0], 4)
    put("anorm", row(I["e_a_norm"][0]))
    cp = I["e_b_cmp_pos"][0].transpose(2, 0, 1)
    put("cpos", np.concatenate([cp, cp], 0))
    put("cw2", I["e_b_cmp_w2"][0].transpose(1, 0, 2))
    put("gb", row(I["e_b_g_b"][0]))
    put("qnorm", I["o_q_norm"][0].reshape(4, 128).T)
    put("kvnorm", row(I["o_kv_norm"][0]))
    put("ikg", row(I["o_ik_g"][0]))
    put("ikb", row(I["o_ik_b"][0]))
    for n, k in (("nf1", "norm_ffn1_2"), ("nmix", "norm_mix_2"), ("nf2", "norm_ffn2_2")):
        put(n, I[k].reshape(2, 8, 128).transpose(2, 0, 1))
    for n, k in (("hlb", "hg_lb_2"), ("rconvb", "rg_conv_b_2"), ("rbr", "rg_br_2"), ("rbi", "rg_bi_2"),
                 ("rlam", "rg_lambda_2")):
        put(n, I[k].reshape(2, 2, 128).transpose(2, 0, 1))
    put("hnw", row(I["hg_norm_w_2"]))
    put("gnw", row(I["gd_norm_w_2"]))
    put("gconv", I["gd_conv_w_2"].reshape(2, 4, 12, 128).transpose(3, 0, 2, 1))
    put("rconv", I["rg_conv_w_2"].reshape(2, 4, 2, 128).transpose(3, 0, 2, 1))
    put("galog", I["gd_a_log_2"].T, 4)
    put("gdt", I["gd_dt_bias_2"].T, 4)
    return C


def matrices(I):
    M = {}
    w = I["e_w_in"][0]
    o = np.cumsum([0, 512, 512, 512, 512, 4, 4, 512, 128, 128, 128, 128, 128, 128, 24])
    c = [w[:, o[i]:o[i + 1]] for i in range(14)]
    aq, ak, av, ao, ai, af, bq, bkc, bvc, bks, bvs, bkw, bvw, bg = c
    bq = bq.reshape(1024, 2, 4, 64).transpose(0, 2, 1, 3).reshape(1024, 512)
    M["e_in"] = np.concatenate([aq, ak, bkc, bvc, bks, bkw, bq, av, ao, bvs, bvw, bg, ai, af], 1)
    M["e_out"] = I["e_w_out"][0]
    cw = I["e_b_cmp_w1"][0].reshape(2, 32, 64, 128).transpose(0, 2, 1, 3).reshape(2, 64, 4096)
    M["cw1"] = np.concatenate([cw[0], cw[0], cw[1], cw[1]], 0)
    rep = lambda a: np.broadcast_to(np.concatenate([x.reshape(-1) for x in a])[None, :], (128, sum(x.size for x in a)))
    for l in range(2):
        M[f"ln1_{l}"] = rep([I["ln1_g"][l], I["ln1_b"][l]])
        M[f"ln2_{l}"] = rep([I["ln2_g"][l], I["ln2_b"][l]])
        M[f"w1_{l}"] = I["mlp_w1"][l]
        M[f"w2_{l}"] = I["mlp_w2"][l]
        M[f"pT_{l}"] = I["p"][l, 0].T
        M[f"pgw_{l}"] = I["ple_gate_w"][l]
        M[f"pw_{l}"] = I["ple_w"][l]
    M["o_in"] = I["o_w_in"][0]
    qb = I["o_w_qb"][0].reshape(512, 8, 192)
    M["o_qb"] = np.concatenate([qb[:, :, :128].reshape(512, 1024), qb[:, :, 128:].reshape(512, 512)], 1)
    M["o_iq"] = I["o_w_iq"][0]
    M["o_uk"] = I["o_w_uk"][0].transpose(2, 1, 0).reshape(128, 2048)
    M["o_uv"] = I["o_w_uv"][0].reshape(256, 1024)
    M["o_out"] = I["o_w_out"][0]
    so = np.cumsum([0, 256, 256, 256, 256, 512, 512, 512, 512, 4, 4, 256, 256])
    for l in range(2):
        for n in ("1", "2"):
            M[f"fg{n}_{l}"] = I[f"ffn{n}_gate_2"][l]
            M[f"fu{n}_{l}"] = I[f"ffn{n}_up_2"][l]
            M[f"fd{n}_{l}"] = I[f"ffn{n}_down_2"][l]
        w = I["w_in_2"][l]
        hq, hf, hi, hg, gq, gk, gv, gz, gb, ga, rx, rg = [w[:, so[i]:so[i + 1]] for i in range(12)]
        M[f"win_{l}"] = np.concatenate([hq, hf, gq, gk, gv, rx, rg, hi, hg, gz, gb, ga], 1)
        M[f"wo_{l}"] = I["w_out_2"][l]
        r = np.zeros((128, 4, 128), np.float32)
        for q, k in enumerate(("rg_wr_2", "rg_wi_2")):
            for n in range(4):
                p0 = 64 * (n % 2)
                r[p0:p0 + 64, 2 * q + n // 2, p0:p0 + 64] = I[k][l, n]
        M[f"rgw_{l}"] = r.reshape(128, 512)
    M["nfin"] = rep([I["norm_final_2"]])
    return M


def kernel(**inputs):
    import concourse.bacc as _bacc
    from concourse.bass_utils import run_bass_kernel_spmd as _run

    I = {k: np.asarray(v) for k, v in inputs.items()}
    nc = _bacc.Bacc("TRN2", target_bir_lowering=False, num_devices=1)
    with ExitStack() as ctx:
        P, stream = record(nc, ctx)
        M = matrices(I)
        parts, offs, off = [], [], 0
        for key, k0, nk, c0, ncol in stream:
            a = M[key][k0 * 128:(k0 + nk) * 128, c0:c0 + ncol].reshape(nk, 128, ncol).transpose(1, 0, 2)
            parts.append(a.reshape(-1))
            offs.append((off, nk * ncol))
            off += a.size
        arrays = {"wts": np.concatenate(parts), "cb": const_block(I),
                  "xT": np.ascontiguousarray(I["x"][0].T.reshape(8, 128, 512).transpose(1, 0, 2)),
                  "x": np.ascontiguousarray(I["x"][0].reshape(4, 128, 1024).transpose(1, 0, 2)),
                  "pos": np.ascontiguousarray(I["positions"][0].reshape(4, 128).T)}
        W = {}
        for n, a in arrays.items():
            t = nc.dram_tensor("in_" + n, a.shape, mybir.dt.from_np(a.dtype), kind="ExternalInput").ap()
            if n == "wts":
                for i, (o, w) in enumerate(offs):
                    W[i] = t[o:o + 128 * w].rearrange("(p n) -> p n", p=128)
            else:
                W[n] = t
        out = nc.dram_tensor("out_0", (1, 512, 1024), F32, kind="ExternalOutput").ap()
        W["out"] = out[0].rearrange("(j p) n -> p j n", p=128)
        emit(nc, ctx, P, W, 1)
    r = _run(nc, [{"in_" + n: a for n, a in arrays.items()}], core_ids=[0])
    return r.results[0]["out_0"]
```

```python
import numpy as np
import concourse.bass as bass
import concourse.mybir as mybir
from concourse.alu_op_type import AluOpType as ALU
from contextlib import ExitStack

F32 = mybir.dt.float32
F32R = mybir.dt.float32r
I32 = mybir.dt.int32
ACT = mybir.ActivationFunctionType
AX = mybir.AxisListType
T = 512
NS = 4
SLOT = 2048
NB = 32389
WS = 8192
UP = 14336
ALPHA = float((2.0 * 2) ** 0.25)
NEG = -1e30

CONSTS = [
    ("ident", 128), ("lev", 8 * 128), ("cmask", 128), ("tmask", 128), ("ones", 128), ("sel", 512),
    ("cmpadd", 124), ("cmp01", 124), ("invf", 48), ("zero", 1),
    ("aconv", 32), ("aib", 1), ("afb", 1), ("anorm", 512), ("cpos", 64), ("cw2", 128), ("gb", 24),
    ("qnorm", 4), ("kvnorm", 256), ("ikg", 64), ("ikb", 64),
    ("nf1", 16), ("nmix", 16), ("nf2", 16), ("hlb", 4), ("hnw", 128), ("gconv", 96), ("galog", 2), ("gdt", 2),
    ("gnw", 256), ("rconv", 16), ("rconvb", 4), ("rbr", 4), ("rbi", 4), ("rlam", 4),
]
COFF = {}
NCB = 0
for _n, _w in CONSTS:
    COFF[_n] = (NCB, _w)
    NCB += _w


class Prog:

    ENG = ("pe", "act", "dve", "pool", "sp")

    def __init__(self):
        self.ops = {e: [] for e in self.ENG}
        self.cnt = {e: 0 for e in self.ENG}
        self.seen = {e: {} for e in self.ENG}
        self.marks, self.hp = [], []
        self.pending, self.hold = [], False
        self.need = {e: [] for e in self.ENG}

    def flush(self):
        if self.pending and not self.hold:
            todo, self.pending = self.pending, []
            for f in todo:
                f()

    def last(self, e):
        self.flush()
        if not self.ops[e]:
            return (e, 0)
        o = self.ops[e][-1]
        if not o[2]:
            o[2] = True
            self.cnt[e] += 1
        return (e, self.cnt[e])

    def op(self, e, fn, after=(), chain=True):
        self.flush()
        waits = []
        after = [a for a in after if a is not None] + self.need[e]
        self.need[e] = []
        if chain and e in ("act", "dve", "pool"):
            after.append(self.last(e))
        for s, v in after:
            if v and self.seen[e].get(s, 0) < v and not (e == "pe" and s == "pe"):
                self.seen[e][s] = v
                waits.append((s, v))
        self.ops[e].append([fn, waits, False])


class Bank:
    def __init__(self, t):
        self.t = t
        self.free = []


class Region:

    def __init__(self, low, up):
        self.low, self.up = low, up

    def __getitem__(self, at):
        p, c = at
        if c.stop <= UP:
            return self.low[p, c]
        assert c.start >= UP and c.stop <= NB
        return self.up[p, c.start - UP:c.stop - UP]


def pipe(n, stages):
    for t in range(n + len(stages) - 1):
        for k in reversed(range(len(stages))):
            if 0 <= t - k < n:
                stages[k](t - k)


def bc(ap, shape):
    return ap.broadcast_to(shape)


def record(nc, ctx, dbg=None):
    P = Prog()
    sb = lambda n, s, d=F32: ctx.enter_context(nc.sbuf_tensor(n, s, d))
    RING = sb("ring", [128, NS, SLOT])
    X = sb("X", [128, 4, 1024])
    C = sb("C", [128, NCB])
    POS = sb("pos", [128, 4], I32)
    SM = sb("small", [128, 256])
    with nc.sbuf_tensor("arena0", [128, UP], F32) as a0:
        with nc.sbuf_tensor("arena1", [128, NB - UP], F32) as a1:
            ARENA = Region(a0, a1)
    ARENAR = Region(sb("split0", [128, UP], F32R), sb("split1", [128, NB - UP], F32R))
    banks = [Bank(ctx.enter_context(nc.psum_tensor(f"ps{i}", [128, 512], F32))) for i in range(8)]
    st = {"bank": 0, "ev": 0, "wb": 0}
    stream = []
    slotfree = [[] for _ in range(NS)]
    misc = []

    def cst(name):
        o, w = COFF[name]
        return C[:, o:o + w]

    def bank():
        P.flush()
        b = banks[st["bank"] % 8]
        st["bank"] += 1
        return b

    E = lambda: P.last("pe")
    A = lambda: P.last("act")
    D = lambda: P.last("dve")
    G = lambda: P.last("pool")
    AD = lambda: [A(), D()]

    class Arena:
        def __init__(self, o=UP, split=False):
            self.o, self.t = o, (ARENAR if split else ARENA)

        def take(self, *dims):
            n = int(np.prod(dims))
            v = self.t[:, self.o:self.o + n]
            self.o += n
            assert self.o <= NB, self.o
            if len(dims) == 2:
                v = v.rearrange("p (a b) -> p a b", a=dims[0])
            if len(dims) == 3:
                v = v.rearrange("p (a b c) -> p a b c", a=dims[0], b=dims[1])
            return v

        def at(self, o):
            self.o = o
            return self

    def mark(n):
        P.marks.append((n, len(P.ops["pe"])))

    def mm(out, l, r, start, stop, after=()):
        P.hp.append(1 if l.dtype == F32R else 2)
        P.op("pe", lambda e: e.matmul(out, l, r, start=start, stop=stop, skip_group_check=True), after)

    def tr(out, i, after=()):
        k = i.shape[0]
        P.hp.append(1)
        o, _ = COFF["ident"]
        s0 = i.base_partition() if callable(i.base_partition) else i.base_partition
        idn = C[s0:s0 + k, o + s0:o + s0 + k]
        P.op("pe", lambda e: e.transpose(out, i, idn), after)

    def act(out, i, f, bias=None, scale=None, accum=None, after=()):
        kw = {}
        if bias is not None:
            kw["bias"] = bias
        if scale is not None:
            kw["scale"] = scale
        if accum is not None:
            kw["accum_out"] = accum
        P.op("act", lambda e: e.activation(out, i, f, **kw), after)

    def ts(out, i, s1, s2, o0, o1=None, after=(), accum=None, eng="dve"):
        if o1 is None:
            P.op(eng, lambda e: e.tensor_scalar(out, i, s1, None, o0), after)
        elif accum is not None:
            P.op(eng, lambda e: e.tensor_scalar(out, i, s1, s2, o0, o1, accum_out=accum), after)
        else:
            P.op(eng, lambda e: e.tensor_scalar(out, i, s1, s2, o0, o1), after)

    def tt(out, a, b, o, after=(), eng="dve"):
        P.op(eng, lambda e: e.tensor_tensor(out, a, b, o), after)

    def stt(out, a, s, b, o0, o1, after=()):
        P.op("dve", lambda e: e.scalar_tensor_tensor(out, a, s, b, o0, o1), after)

    def vcp(out, i, after=()):
        P.op("dve", lambda e: e.tensor_copy(out, i), after)

    def bns(out, i, after=()):
        P.op("dve", lambda e: e.bn_stats(out, i), after)

    def bna(out, i):
        P.op("dve", lambda e: e.bn_aggr(out, i))

    def top8(m8, a):
        P.op("dve", lambda e: e.max(m8, a))
        P.op("dve", lambda e: e.match_replace(a, m8, a, -3.0e38))

    def recip(out, i, after=()):
        P.op("dve", lambda e: e.reciprocal(out, i), after)

    def scan(out, a, b, init, o0, o1, after=()):
        P.op("dve", lambda e: e.tensor_tensor_scan(out, a, b, init, o0, o1), after)

    def red(out, i, o, neg=False, after=()):
        P.op("dve", lambda e: e.tensor_reduce(out, i, AX.X, o, negate=neg), after)

    def evc(out, i, after=(), scale=None):
        st["ev"] += 1
        if st["ev"] % 2:
            act(out, i, ACT.Copy, scale=scale, after=after)
            return A()
        if scale is None:
            vcp(out, i, after)
        else:
            ts(out, i, scale, None, ALU.mult, after=after)
        return D()

    def load(key, k0, nk, c0, ncol):
        i = len(stream)
        slot = i % NS
        assert nk * ncol <= SLOT
        stream.append((key, k0, nk, c0, ncol))
        v = RING[:, slot, 0:nk * ncol]
        P.op("sp", lambda e, W, S: e.dma_start(v, W[i]).then_inc(S[f"w{slot}"], 16), slotfree[slot])
        slotfree[slot] = None
        return v.rearrange("p (k n) -> p k n", k=nk), (f"w{slot}", 16 * (i // NS + 1)), slot

    def release(slot, toks):
        slotfree[slot] = list(toks)

    wbuf = [[None, [], i] for i in range(3)]
    for w_ in wbuf:
        o_ = WS + w_[2] * 2048
        w_[0] = (ARENAR[:, o_:o_ + 1024], ARENAR[:, o_ + 1024:o_ + 2048])

    def f32(ap):
        return ap.bitcast(F32)

    def low(tok):
        for w_ in wbuf:
            w_[1] = list(tok)

    def split(view, after):
        w_ = wbuf[st["wb"] % 3]
        st["wb"] += 1
        n = view.shape[1]
        hi, lo = w_[0][0][:, 0:n], w_[0][1][:, 0:n]
        act(hi, view, ACT.Copy, after=list(after) + w_[1])
        tt(lo, view, f32(hi), ALU.subtract, after=[A()])
        return hi, lo, w_, D()

    def mm3(out, l, r, start, stop, after=()):
        mm(out, l[0], r[0], start, False, after)
        mm(out, l[0], r[1], False, False)
        mm(out, l[1], r[0], False, stop)

    def put(dst, k, src, after=(), gain=None, slc=slice(0, 512)):
        hi, lo = dst[0][:, k, slc], dst[1][:, k, slc]
        act(hi, src, ACT.Copy, scale=gain, after=list(after) + [D()])
        if gain is None:
            tt(lo, src, f32(hi), ALU.subtract, after=[A()])
        else:
            stt(lo, src, gain, f32(hi), ALU.mult, ALU.subtract, [A()])

    def pieces(key, nk, c0, ncol, kbase=0):
        per = max(1, min(2, 1024 // ncol))
        for kc in range(0, nk, 4):
            n = min(4, nk - kc)
            w, tok, slot = load(key, kbase + kc, n, c0, ncol)
            for q in range(0, n, per):
                c = min(per, n - q)
                hi, lo, w_, done = split(w[:, q:q + c, :].rearrange("p k n -> p (k n)"), [tok])
                if q + c == n:
                    release(slot, [A(), D()])
                yield kc + q, c, hi.rearrange("p (k n) -> p k n", k=c), lo.rearrange("p (k n) -> p k n", k=c), w_, done

    def ahead(gen):
        P.hold = True
        q = [next(gen)]
        x = next(gen, None)
        if x is not None:
            q.append(x)
        P.hold = False
        P.flush()
        while q:
            yield q.pop(0)
            x = next(gen, None)
            if x is not None:
                q.append(x)

    def lin(src, nk, key, c0, ncol, fm, evict, after=(), kbase=0):
        nm = ncol // 128 if fm else 4
        first = True
        for k0, c, hi, lo, w_, tok in ahead(pieces(key, nk, c0, ncol, kbase)):
            if first:
                bs = [bank() for _ in range(nm)]
                tk = after() if callable(after) else list(after)
                first = False
            for m in range(nm):
                for k in range(c):
                    kk = k0 + k
                    ms = slice(m * 128, (m + 1) * 128)
                    sh, sl_ = src[0][:, kk, :], src[1][:, kk, :]
                    if fm:
                        l, r = (hi[:, k, ms], lo[:, k, ms]), (sh, sl_)
                    else:
                        l, r = (sh[:, ms], sl_[:, ms]), (hi[:, k, :], lo[:, k, :])
                    nn = 512 if fm else ncol
                    mm3(bs[m].t[:, 0:nn], l, r, kk == 0, kk == nk - 1, [tok] + tk + bs[m].free)
            w_[1] = [E()]
        done = E()

        def out():
            for m in range(nm):
                evict(m, bs[m].t)
                bs[m].free = AD()
        P.pending.append(out)

    def lin_down(key, src, nk, k0, c, evict, after):
        lin(src, nk, key, c * 512, 512, False, evict, after, kbase=k0)

    def to_fm(src, dst, nf, gain=None, after=(), plain=False):
        for f in range(nf):
            b = bank()
            for j in range(4):
                tr(b.t[:, j * 128:(j + 1) * 128], src[:, j, f * 128:(f + 1) * 128], list(after) + b.free)
            if plain:
                evc(dst[:, f, :], b.t[:, :], [E()])
            else:
                put(dst, f, b.t[:, :], [E()], None if gain is None else gain[:, f:f + 1])
            b.free = AD()

    def pw(x):
        act(x, x, ACT.Sqrt, after=[D()])
        recip(x, x, after=[A()])

    def rsq(out, i, mul, eps):
        ts(out, i, mul, eps, ALU.mult, ALU.add)
        pw(out)

    def layer_norm(key):
        w, tok, slot = load(key, 0, 1, 0, 2048)
        sc = SM[:, 0:16]
        for j in range(4):
            bns(sc[:, 0:6], X[:, j, 0:512], after=[A()])
            bns(sc[:, 6:12], X[:, j, 512:1024])
            bna(sc[:, 12:14], sc[:, 0:12])
            rsq(sc[:, 14:15], sc[:, 13:14], 1.0, 1e-5)
            ts(X[:, j, :], X[:, j, :], sc[:, 12:13], sc[:, 14:15], ALU.subtract, ALU.mult)
            tt(X[:, j, :], X[:, j, :], w[:, 0, 0:1024], ALU.mult, [tok])
            tt(X[:, j, :], X[:, j, :], w[:, 0, 1024:2048], ALU.add)
        release(slot, [D()])

    def rms_rows(src, tmp, dst, n, out_scale, eps):
        a = SM[:, 16:17]
        act(tmp, src, ACT.Square, accum=a, after=[D()])
        ts(SM[:, 17:18], a, 1.0 / n, eps, ALU.mult, ALU.add, after=[A()])
        pw(SM[:, 17:18])
        ts(dst, src, SM[:, 17:18], None, ALU.mult)

    def dump(name, ap, shape):
        if dbg is None:
            return
        dbg.append((name, shape))
        P.op("sp", lambda e, W, S: e.dma_start(W["dbg_" + name], ap).then_inc(S["out"], 16), [E(), A(), D(), G()])

    P.op("sp", lambda e, W, S: e.dma_start(C[:, :], W["cb"]).then_inc(S["c"], 16))
    P.op("sp", lambda e, W, S: e.dma_start(X[:, :, :], W["x"]).then_inc(S["x"], 16))
    P.op("sp", lambda e, W, S: e.dma_start(POS[:, :], W["pos"]).then_inc(S["pos"], 16))
    cb_tok, x_tok, pos_tok = ("c", 16), ("x", 16), ("pos", 16)
    P.op("dve", lambda e: e.memset(SM[:, :], 0.0), [cb_tok, x_tok])
    P.op("act", lambda e: e.activation(SM[:, 200:201], SM[:, 201:202], ACT.Copy), [cb_tok, D()])
    P.op("pe", lambda e: e.transpose(banks[0].t[:, 0:128], C[:, COFF["ident"][0]:COFF["ident"][0] + 128],
                                     C[:, COFF["ident"][0]:COFF["ident"][0] + 128]), [cb_tok, D()])
    P.hp.append(1)
    H = (ARENAR[:, 0:4096].rearrange("p (a b) -> p a b", a=8), ARENAR[:, 4096:8192].rearrange("p (a b) -> p a b", a=8))
    HT = lambda: st["ht"]
    P.op("pool", lambda e: e.memset(SM[:, 202:203], 0.0), [cb_tok, D()])

    ident, ones, sel = cst("ident"), cst("ones"), cst("sel")

    def res_add(scale_x, scale_y, c0):
        def f(m, ps):
            xs = X[:, m, c0:c0 + 512]
            if scale_y is None:
                stt(xs, xs, scale_x, ps[:, :], ALU.mult, ALU.add, [E()])
            else:
                stt(xs, ps[:, :], scale_y, xs, ALU.mult, ALU.add, [E()])
        return f

    def even_mixer():
        to_fm(X, H, 8)
        st["ht"] = AD()
        ar = Arena()
        QK = ar.take(8, 512)
        AV = ar.take(4, 4, 129)
        BQ = ar.take(4, 512)
        KCV = ar.take(2, 512)
        KSW = ar.take(2, 512)
        VSW = ar.take(4, 256)
        GT = ar.take(4, 24)
        AO = ar.take(4, 512)
        base = ar.o
        raw = ar.take(2, 516)
        acc = ar.take(512)
        aconv = cst("aconv")
        P.op("pool", lambda e: e.memset(raw[:, :, 0:3], 0.0))
        P.op("pool", lambda e: e.memset(AV[:, :, :, 128:129], 1.0))
        g0 = G()

        def ev_qk(c):
            def f(m, ps):
                t = c * 4 + m
                r = raw[:, t % 2, :]
                act(r[:, 3:515], ps[:, :], ACT.Copy, after=[E(), D(), g0])
                ts(acc, r[:, 0:512], aconv[:, t * 4:t * 4 + 1], None, ALU.mult, after=[A()])
                for j in range(1, 4):
                    stt(acc, r[:, j:j + 512], aconv[:, t * 4 + j:t * 4 + j + 1], acc, ALU.mult, ALU.add)
                act(QK[:, t, :], acc, ACT.Silu, after=[D()])
            return f

        mark("e_lin")
        lin(H, 8, "e_in", 0, 512, True, ev_qk(0), HT)
        lin(H, 8, "e_in", 512, 512, True, ev_qk(1))

        def ev_k(m, ps):
            evc(KCV[:, m, :] if m < 2 else KSW[:, m - 2, :], ps[:, :], [E()])
        lin(H, 8, "e_in", 1024, 512, True, ev_k)
        lin(H, 8, "e_in", 1536, 512, True, lambda m, ps: evc(BQ[:, m, :], ps[:, :], [E()], scale=0.125))
        lin(H, 8, "e_in", 2048, 512, False,
            lambda m, ps: evc(AV[:, m, :, 0:128], ps[:, :].rearrange("p (h d) -> p h d", h=4), [E()]))
        lin(H, 8, "e_in", 2560, 512, False, lambda m, ps: act(AO[:, m, :], ps[:, :], ACT.Sigmoid, after=[E()]))

        mark("e_gates")
        R = [ARENA[0:4, base + i * 512:base + (i + 1) * 512] for i in range(7)]
        bs = [bank() for _ in range(6)]
        for k0, c, hi, lo, w_, tok in ahead(pieces("e_in", 8, 3072, 288)):
            for k in range(c):
                kk = k0 + k
                for m in range(4):
                    ms = slice(m * 128, (m + 1) * 128)
                    mm3(bs[m].t[:, 0:280], (H[0][:, kk, ms], H[1][:, kk, ms]), (hi[:, k, 0:280], lo[:, k, 0:280]), kk == 0,
                        kk == 7, [tok] + bs[m].free)
            w_[1] = [E()]
        w, tok, slot = load("e_g", 0, 8, 0, 8)
        for i in range(2):
            for k in range(8):
                mm(bs[4 + i].t[0:4, :], w[:, k, 4 * i:4 * i + 4], f32(H[0][:, k, :]), k == 0, False, [tok] + bs[4 + i].free)
                mm(bs[4 + i].t[0:4, :], w[:, k, 4 * i:4 * i + 4], f32(H[1][:, k, :]), False, k == 7)
        release(slot, [E()])
        for m in range(4):
            vcp(VSW[:, m, :], bs[m].t[:, 0:256], [E()])
            tt(GT[:, m, :], bs[m].t[:, 256:280], cst("gb"), ALU.add)
            bs[m].free = AD()
        act(GT, GT, ACT.Sigmoid, after=[D()])
        for i in range(2):
            ts(R[i], bs[4 + i].t[0:4, :], cst("aib" if i == 0 else "afb")[0:4, :], None, ALU.add, after=[E()])
            bs[4 + i].free = AD()
        stt(R[2], R[1], -1.0, R[1], ALU.mult, ALU.max)
        act(R[2], R[2], ACT.Exp, scale=-1.0, after=[D()])
        act(R[2], R[2], ACT.Ln, bias=ones[0:4, 0:1])
        stt(R[1], R[1], 0.0, R[2], ALU.min, ALU.subtract, [A()])
        scan(R[3], bc(ones[0:4, 0:1], [4, 512]), R[1], 0.0, ALU.mult, ALU.add)
        tt(R[4], R[0], R[3], ALU.subtract)
        scan(R[5], R[4], R[4], 0.0, ALU.max, ALU.max)
        tt(R[6], R[3], R[5], ALU.add)
        act(R[6], R[6], ACT.Exp, scale=-1.0, after=[D()])
        cols = SM[:, 32:64].rearrange("p (a b c) -> p a b c", a=2, b=4)
        b = bank()
        for a_, r in ((0, R[4]), (1, R[6])):
            for j in range(4):
                tr(b.t[:, (a_ * 4 + j) * 4:(a_ * 4 + j) * 4 + 4], r[:, j * 128:(j + 1) * 128], AD() + b.free)
        vcp(SM[:, 32:64], b.t[:, 0:32], [E()])
        b.free = AD()
        MR = ARENA[0:4, 14336 - 512:14336]
        vcp(MR, R[5], [E(), A()])
        R = R[0:5] + [MR]
        ar.at(0)
        mark("mlstm")
        PT = ar.take(2, 4, 512)
        MBS = ar.take(4, 512)
        BST = ar.take(16, 6)
        BAG = ar.take(16, 2)
        RST = ar.take(16)
        DEN = ar.take(16)
        DE2 = ar.take(16)
        t0 = AD()
        for h in range(4):
            b = bank()
            mm(b.t[:, :], sel[0:4, h * 128:(h + 1) * 128], R[5], True, True, t0 + b.free)
            b.free = [evc(MBS[:, h, :], b.t[:, :], [E()])]
        t0 = AD()
        d = {}

        def m0(t):
            h, i = t // 4, t % 4
            x = PT[:, h % 2, i, i * 128:512]
            ts(x, MBS[:, h, i * 128:512], cols[:, 0, i, h:h + 1], 0.0, ALU.subtract, ALU.max,
               after=[A()] if t == 0 else [d.get(("pv", h - 2))])
            d["g", t] = D()

        def m1(t):
            h, i = t // 4, t % 4
            x = PT[:, h % 2, i, i * 128:512]
            act(x, x, ACT.Exp, scale=-1.0, after=[d["g", t]])
            d["e", t] = A()
            b = d["b", t] = bank()
            mm(b.t[:, 0:512 - 128 * i], QK[:, 4 + h, i * 128:(i + 1) * 128], QK[:, h, i * 128:512], True, True, t0 + b.free)
            d["s", t] = E()

        def m2(t):
            h, i = t // 4, t % 4
            y = PT[:, h % 2, i, i * 128:(i + 1) * 128]
            x = PT[:, h % 2, i, i * 128:512]
            tt(y, y, cst("tmask"), ALU.mult, after=[d["e", t]])
            stt(x, d["b", t].t[:, 0:512 - 128 * i], 128.0 ** -0.5, x, ALU.mult, ALU.mult, [d["s", t]])
            d["b", t].free = [D()]
            d["p", h] = D()

        def m3(t):
            h = t // 4
            if t % 4 < 3:
                return
            for jp in range(2):
                b = d["n", h, jp] = bank()
                for jj in range(2):
                    j = jp * 2 + jj
                    for i in range(j + 1):
                        mm(b.t[:, jj * 129:(jj + 1) * 129], PT[:, h % 2, i, j * 128:(j + 1) * 128], AV[:, i, h, :], i == 0,
                           i == j, [d["p", h]] + b.free)
                d["nt", h, jp] = E()
            d["pv", h] = E()

        def m4(t):
            h = t // 4
            if t % 4 < 3:
                return
            for jp in range(2):
                b = d["n", h, jp]
                bv = b.t[:, 0:258].rearrange("p (j c) -> p j c", j=2)
                c0 = 4 * h + 2 * jp
                x, y = DEN[:, c0:c0 + 2], DE2[:, c0:c0 + 2]
                vcp(x, bv[:, :, 128], [d["nt", h, jp]])
                stt(y, x, -1.0, x, ALU.mult, ALU.max)
                tt(y, y, cols[:, 1, 2 * jp:2 * jp + 2, h], ALU.max)
                recip(y, y)
                q = QK[:, h, jp * 256:(jp + 1) * 256].rearrange("p (j c) -> p j c", j=2)
                tt(q, bv[:, :, 0:128], bc(y.unsqueeze(2), [128, 2, 128]), ALU.mult)
                b.free = [D()]
                for jj in range(2):
                    bns(BST[:, c0 + jj, :], q[:, jj, :])
                    bna(BAG[:, c0 + jj, :], BST[:, c0 + jj, :])
        pipe(16, [m0, m1, m2, m3, m4])
        rsq(RST, BAG[:, :, 1], 1.0, 1e-5)
        for h in range(4):
            q = QK[:, h, :].rearrange("p (j c) -> p j c", j=4)
            tt(q, q, bc(BAG[:, 4 * h:4 * h + 4, 0].unsqueeze(2), [128, 4, 128]), ALU.subtract)
            tt(q, q, bc(RST[:, 4 * h:4 * h + 4].unsqueeze(2), [128, 4, 128]), ALU.mult)
        free = ar.o
        YA = ar.at(base).take(4, 1024)
        for j in range(4):
            y = YA[:, j, 0:512]
            qv = QK[:, 0:4, j * 128:(j + 1) * 128]
            tt(y.rearrange("p (h d) -> p h d", h=4), qv, cst("anorm").rearrange("p (h d) -> p h d", h=4), ALU.mult,
               after=[E(), A()])
            tt(y, y, AO[:, j, :], ALU.mult)
        dump("ya", YA[:, :, 0:512], [128, 4, 512])

        mark("nsa_cmp")
        ar.at(UP)
        blk = ar.take(32, 31)
        PP = ar.take(2, 512)
        PT2 = ar.take(2, 512)
        hid = ar.take(2, 64)
        assert ar.o <= UP + 4096
        ar.at(free)
        kc = ar.take(31)
        vc = ar.take(2, 64)
        PC = ar.take(8, 32)
        PCT = ar.take(8, 128)
        rc = ar.take(3, 8)
        cpos = cst("cpos")
        for jj in range(2):
            w0, tok0, slot0 = load("cw1", jj, 1, 0, 2048)
            w1, tok1, slot1 = load("cw1", jj, 1, 2048, 2048)
            u = KCV[:, jj, :].rearrange("p (m l) -> p l m", l=16)
            pb = cpos[:, jj * 32:(jj + 1) * 32].unsqueeze(2)
            tt(blk[:, 0:16, :], u[:, :, 0:31], bc(pb[:, 0:16, :], [128, 16, 31]), ALU.add, after=[E(), A()])
            tt(blk[:, 16:32, :], u[:, :, 1:32], bc(pb[:, 16:32, :], [128, 16, 31]), ALU.add)
            hb = [bank(), bank()]
            for g in range(2):
                for l in range(32):
                    mm(hb[g].t[:, 0:31], (w0 if l < 16 else w1)[64 * g:64 * g + 64, 0, l % 16 * 128:(l % 16 + 1) * 128],
                       blk[64 * g:64 * g + 64, l, :], l == 0, l == 31, [tok0, tok1, D()] + hb[g].free)
            release(slot0, [E()])
            release(slot1, [E()])
            for g in range(2):
                act(hid[:, jj, g * 32:g * 32 + 31], hb[g].t[:, 0:31], ACT.Gelu_apprx_tanh, after=[E()])
                hb[g].free = AD()
            b = bank()
            cw2 = cst("cw2")[:, jj * 64:(jj + 1) * 64]
            for g in range(2):
                if jj == 0:
                    mm(b.t[64 * g:64 * g + 64, 0:31], cw2, hid[:, 0, g * 32:g * 32 + 31], True, True, [A()] + b.free)
                else:
                    mm(b.t[0:31, g * 64:(g + 1) * 64], hid[:, 1, g * 32:g * 32 + 31], cw2, True, True, [A()] + b.free)
            if jj == 0:
                vcp(kc, b.t[:, 0:31], [E()])
            else:
                vcp(vc[0:31, :, :].rearrange("p a b -> p (a b)"), b.t[0:31, 0:128], [E()])
            b.free = AD()
        dump("kc", kc, [128, 31])
        mark("nsa")
        ca, c01 = cst("cmpadd"), cst("cmp01")
        for i in range(4):
            cb = [bank(), bank()]
            for h in range(8):
                g, j = h // 4, h % 4
                mm(cb[g].t[:, j * 32:j * 32 + 31], BQ[64 * g:64 * g + 64, j, i * 128:(i + 1) * 128], kc[64 * g:64 * g + 64, :], True,
                   True, AD() + cb[g].free)
            pc = PC[:, :, 0:31]
            for g in range(2):
                tt(PC[:, 4 * g:4 * g + 4, 0:31], cb[g].t[:, 0:128].rearrange("p (h m) -> p h m", h=4)[:, :, 0:31],
                   bc(ca[:, i * 31:(i + 1) * 31].unsqueeze(1), [128, 4, 31]), ALU.add, after=[E()])
                cb[g].free = AD()
            red(rc[:, 0, :], pc, ALU.max)
            tt(pc, pc, bc(rc[:, 0, :].unsqueeze(2), [128, 8, 31]), ALU.subtract)
            act(pc, pc, ACT.Exp, after=[D()])
            red(rc[:, 1, :], pc, ALU.add, after=[A()])
            tt(pc, pc, bc(c01[:, i * 31:(i + 1) * 31].unsqueeze(1), [128, 8, 31]), ALU.mult)
            recip(rc[:, 2, :], rc[:, 1, :])
            tt(rc[:, 2, :], rc[:, 2, :], GT[:, i, 0:24:3], ALU.mult)
            for hh in range(2):
                b = bank()
                for q in range(4):
                    tr(b.t[0:31, q * 128:(q + 1) * 128], PC[:, hh * 4 + q, 0:31], [D()] + b.free)
                evc(PCT[0:31, hh * 4:hh * 4 + 4, :].rearrange("p a b -> p (a b)"), b.t[0:31, :], [E()])
                b.free = AD()
            b = bank()
            for h in range(8):
                mm(b.t[:, h * 64:(h + 1) * 64], PCT[0:31, h, :], vc[0:31, h // 4, :], True, True, AD() + b.free)
            tt(YA[:, i, 512:1024].rearrange("p (h d) -> p h d", h=8), b.t[:, :].rearrange("p (h d) -> p h d", h=8),
               bc(rc[:, 2, :].unsqueeze(2), [128, 8, 64]), ALU.mult, after=[E()])
            b.free = AD()
        RS = ar.take(8, 4)
        t0 = AD() + [E()]
        d = {}

        def where(t):
            i, h, br = t // 16, t // 2 % 8, t % 2
            return i, h, br, 128 * (i + 1), h // 4, h % 4

        def n0(t):
            i, h, br, n, g, j = where(t)
            sl = slice(64 * g, 64 * g + 64)
            b = d["s", t] = bank()
            mm(b.t[:, 0:n], BQ[sl, j, i * 128:(i + 1) * 128], KSW[sl, br, 0:n], True, False, t0 + b.free)
            mm(b.t[:, n - 128:n], ident, cst("cmask"), False, True)
            d["se", t] = E()

        def n1(t):
            i, h, br, n, g, j = where(t)
            b, rs = d["s", t], RS[:, t % 8, :]
            red(rs[:, 0:1], b.t[:, 0:n], ALU.max, neg=True, after=[d["se", t]] + (t0 if t == 0 else []))
            act(PP[:, t % 2, 0:n], b.t[:, 0:n], ACT.Exp, bias=rs[:, 0:1], accum=rs[:, 1:2],
                after=[D(), d.get(("tr", t - 2))])
            d["x", t] = A()
            b.free = [A()]

        def n2(t):
            i, h, br, n, g, j = where(t)
            b = d["t", t] = bank()
            for k in range(i + 1):
                tr(b.t[:, k * 128:(k + 1) * 128], PP[:, t % 2, k * 128:(k + 1) * 128], [d["x", t]] + b.free)
            d["tr", t] = E()

        def n3(t):
            i, h, br, n, g, j = where(t)
            rs, b = RS[:, t % 8, :], d["t", t]
            d["c", t] = evc(PT2[:, t % 2, 0:n], b.t[:, 0:n], [d["tr", t], d.get(("pv", t - 2))])
            b.free = [d["c", t]]
            recip(rs[:, 2:3], rs[:, 1:2], after=[d["x", t]])
            tt(rs[:, 2:3], rs[:, 2:3], GT[:, i, 3 * h + 1 + br:3 * h + 2 + br], ALU.mult)

        def n4(t):
            i, h, br, n, g, j = where(t)
            b = d["o", t] = bank()
            for k in range(i + 1):
                mm(b.t[:, 0:64], PT2[:, t % 2, k * 128:(k + 1) * 128], VSW[:, k, br * 128 + 64 * g:br * 128 + 64 * g + 64],
                   k == 0, k == i, [d["c", t]] + b.free)
            d["pv", t] = E()

        def n5(t):
            i, h, br, n, g, j = where(t)
            y = YA[:, i, 512 + 64 * h:576 + 64 * h]
            stt(y, d["o", t].t[:, 0:64], RS[:, t % 8, 2:3], y, ALU.mult, ALU.add, [d["pv", t]])
            d["o", t].free = [D()]
        pipe(64, [n0, n1, n2, n3, n4, n5])
        dump("yb", YA[:, :, 512:1024], [128, 4, 512])
        mark("e_out")
        low([E(), A(), D(), G()])
        act(SM[:, 200:201], SM[:, 201:202], ACT.Copy, after=[E(), D()])
        to_fm(YA, H, 8, after=AD() + [E()])
        st["ht"] = AD()
        lin(H, 8, "e_out", 0, 512, False, res_add(ALPHA, None, 0), HT)
        lin(H, 8, "e_out", 512, 512, False, res_add(ALPHA, None, 512))

    def hidden():
        r = Arena(split=True)
        U = [(r.take(8, 512), r.take(8, 512)) for _ in range(2)]
        return U, Arena(r.o).take(3, 512)

    def mlp_ple(l):
        mark(f"mlp{l}")
        layer_norm(f"ln1_{l}")
        to_fm(X, H, 8, after=[D(), E()])
        st["ht"] = AD()
        dump(f"ln1_{l}", X[:, :, :], [128, 4, 1024])
        U, tmp = hidden()
        utok = [None, None]

        def up(p):
            for c in range(2):
                def ev(m, ps, c=c):
                    t = tmp[:, m % 2, :]
                    hi, lo = U[p % 2][0][:, c * 4 + m, :], U[p % 2][1][:, c * 4 + m, :]
                    act(t, ps[:, :], ACT.Relu, after=[E(), D()])
                    act(hi, t, ACT.Square)
                    tt(t, t, t, ALU.mult, after=[A()])
                    tt(lo, t, f32(hi), ALU.subtract)
                    if m == 3:
                        utok[p % 2] = AD()
                lin(H, 8, f"w1_{l}", (2 * p + c) * 512, 512, True, ev, HT)

        def down(p):
            for c in range(2):
                lin_down(f"w2_{l}", U[p % 2], 8, 8 * p, c, res_add(ALPHA if p == 0 else 1.0, None, c * 512),
                         lambda: utok[p % 2])
        up(0)
        for p in range(4):
            if p < 3:
                up(p + 1)
            down(p)
        mark(f"ple{l}")
        layer_norm(f"ln2_{l}")
        to_fm(X, H, 8, after=[D(), E()])
        st["ht"] = AD()
        ar = Arena(split=True)
        pT = (ar.take(2, 512), ar.take(2, 512))
        pg = Arena(ar.o).take(4, 512)
        w, tok, slot = load(f"pT_{l}", 0, 2, 0, 512)
        for k in range(2):
            put(pT, k, w[:, k, :], [tok, E()])
        release(slot, AD())
        ptok = AD()
        for c in range(2):
            def ev(m, ps):
                act(pg[:, m, :], ps[:, :], ACT.Sigmoid, after=[E(), D()])

            def ev2(m, ps, c=c):
                tt(pg[:, m, :], pg[:, m, :], ps[:, :], ALU.mult, after=[E(), A()])
                tt(X[:, m, c * 512:(c + 1) * 512], X[:, m, c * 512:(c + 1) * 512], pg[:, m, :], ALU.add)
            lin(H, 8, f"pgw_{l}", c * 512, 512, False, ev, HT)
            lin(pT, 2, f"pw_{l}", c * 512, 512, False, ev2, ptok)
        dump(f"h_{l}", X[:, :, :], [128, 4, 1024])

    def odd_mixer():
        mark("o_lin")
        to_fm(X, H, 8, after=[D(), A(), E()])
        st["ht"] = AD()
        ar = Arena()
        CKV = ar.take(4, 256)
        CKT = ar.take(2, 512)
        KRT = ar.take(512)
        KIT = ar.take(512)
        WI = ar.take(4, 8)
        MADD = ar.take(3, 512)
        TAB = ar.take(4, 96)
        QRT = ar.take(4, 512)
        QN = ar.take(8, 512)
        base = ar.o
        CQ = ar.take(4, 512)
        KD = ar.take(4, 256)
        tmp = ar.take(512)
        ANG = ar.take(4, 48)
        KK = ar.take(4, 48)
        RR = ar.take(4, 48)
        pf = SM[:, 90:94]
        vcp(pf, POS[:, :], [pos_tok])
        tt(ANG, bc(pf.unsqueeze(2), [128, 4, 48]), bc(cst("invf").unsqueeze(1), [128, 4, 48]), ALU.mult)
        MAGIC = 12582912.0
        TWO_PI = (6.28125, 0.0019350051879882812, 3.0199160517e-07)
        for which in range(2):
            ts(KK, ANG, 1.0 / (2.0 * np.pi), 0.25 if which == 0 else 0.0, ALU.mult, ALU.add, after=[A()])
            ts(KK, KK, MAGIC, None, ALU.add)
            ts(KK, KK, MAGIC, None, ALU.subtract)
            stt(RR, KK, -TWO_PI[0], ANG, ALU.mult, ALU.add)
            stt(RR, KK, -TWO_PI[1], RR, ALU.mult, ALU.add)
            stt(RR, KK, -TWO_PI[2], RR, ALU.mult, ALU.add)
            if which == 0:
                ts(RR, RR, float(np.pi / 2), None, ALU.add)
            ts(RR, RR, 3.1415925, -3.1415925, ALU.min, ALU.max)
            act(TAB[:, :, 32 * which:32 * which + 32], RR[:, :, 0:32], ACT.Sin, after=[D()])
            act(TAB[:, :, 64 + 16 * which:80 + 16 * which], RR[:, :, 32:48], ACT.Sin)
        dump("tab", TAB, [128, 4, 96])

        def rope(dst, src, j, half, heads, t1, after=()):
            o = 0 if half == 32 else 64
            cs = bc(TAB[:, j, o:o + half].unsqueeze(1), [128, heads, half])
            sn = bc(TAB[:, j, o + half:o + 2 * half].unsqueeze(1), [128, heads, half])
            x1, x2 = src[:, :, 0:half], src[:, :, half:2 * half]
            tv = t1.rearrange("p (h d) -> p h d", h=heads)
            tt(tv, x2, sn, ALU.mult, after=after)
            tt(dst[:, :, 0:half], x1, cs, ALU.mult)
            tt(dst[:, :, 0:half], dst[:, :, 0:half], tv, ALU.subtract)
            tt(tv, x1, sn, ALU.mult)
            tt(dst[:, :, half:2 * half], x2, cs, ALU.mult)
            tt(dst[:, :, half:2 * half], dst[:, :, half:2 * half], tv, ALU.add)

        lin(H, 8, "o_in", 0, 512, False, lambda m, ps: evc(CQ[:, m, :], ps[:, :], [E()]), HT)

        def ev2(m, ps):
            kv = CKV[:, m, :]
            evc(tmp[:, 0:392], ps[:, 0:392], [E(), D(), A()])
            a0 = [A(), D()]
            act(kv, tmp[:, 0:256], ACT.Square, accum=SM[:, 95:96], after=a0)
            ts(SM[:, 96:97], SM[:, 95:96], 1.0 / 256, 1e-5, ALU.mult, ALU.add, after=[A()])
            pw(SM[:, 96:97])
            ts(kv, tmp[:, 0:256], SM[:, 96:97], None, ALU.mult)
            tt(kv, kv, cst("kvnorm"), ALU.mult)
            rope(KD[:, m, 0:64].unsqueeze(1), tmp[:, 256:320].unsqueeze(1), m, 32, 1, tmp[:, 400:432])
            vcp(KD[:, m, 64:128], KD[:, m, 0:64])
            bns(SM[:, 98:104], tmp[:, 320:384])
            bna(SM[:, 104:106], SM[:, 98:104])
            rsq(SM[:, 106:107], SM[:, 105:106], 1.0, 1e-5)
            ki = KD[:, m, 128:192]
            ts(ki, tmp[:, 320:384], SM[:, 104:105], SM[:, 106:107], ALU.subtract, ALU.mult)
            tt(ki, ki, cst("ikg"), ALU.mult)
            tt(ki, ki, cst("ikb"), ALU.add)
            rope(KD[:, m, 192:224].unsqueeze(1), KD[:, m, 128:160].unsqueeze(1), m, 16, 1, tmp[:, 400:416])
            vcp(KD[:, m, 128:160], KD[:, m, 192:224])
            vcp(KD[:, m, 192:256], KD[:, m, 128:192])
            ts(WI[:, m, :], tmp[:, 384:392], float(8 ** -0.5 * 64 ** -0.5), None, ALU.mult)
        lin(H, 8, "o_in", 512, 392, False, ev2, HT)
        to_fm(CKV, CKT, 2, after=[D()], plain=True)
        for m in range(4):
            rms_rows(CQ[:, m, :], tmp, CQ[:, m, :], 512, None, 1e-5)
        CQT = (H[0][:, 0:4, :], H[1][:, 0:4, :])
        to_fm(CQ, CQT, 4, gain=cst("qnorm"), after=[D()])
        st["ht"] = AD()
        for f, dst in ((0, KRT), (1, KIT)):
            b = bank()
            for j in range(4):
                tr(b.t[:, j * 128:(j + 1) * 128], KD[:, j, f * 128:(f + 1) * 128], [D()] + b.free)
            evc(dst, b.t[:, :], [E()])
            b.free = AD()
        dump("ckv", CKV, [128, 4, 256])
        dump("krt", KRT, [128, 512])
        dump("kit", KIT, [128, 512])
        QR = CQ
        def ev3(m, ps):
            evc(tmp, ps[:, :], [E(), D(), A()])
            rope(QR[:, m, :].rearrange("p (h d) -> p h d", h=8), tmp.rearrange("p (h d) -> p h d", h=8), m, 32, 8,
                 KD2, after=[A(), D(), E()])
        KD2 = ar.take(256)
        lin(CQT, 4, "o_qb", 1024, 512, False, ev3, HT)
        to_fm(QR, QRT, 4, after=[D()], plain=True)
        dump("qrt", QRT, [128, 4, 512])
        for c in range(2):
            lin(CQT, 4, "o_qb", c * 512, 512, True,
                lambda m, ps, c=c: evc(QN[:, c * 4 + m, :], ps[:, :], [E()]), HT)
        mark("index")
        P.flush()
        ar.at(base)
        QIT = ar.take(4, 384)
        QI = ar.take(3, 512)
        tmp = ar.take(512)
        t2 = ar.take(256)
        ISC = ar.take(3, 512)
        RL = ar.take(2, 512)
        m8 = ar.take(8)
        def ev4(m, ps):
            if m == 0:
                return
            q = m - 1
            act(tmp, ps[:, :], ACT.Copy, after=[E(), D()])
            qv = QI[:, q, :].rearrange("p (h d) -> p h d", h=8)
            tv = tmp.rearrange("p (h d) -> p h d", h=8)
            rope(qv[:, :, 0:32], tv[:, :, 0:32], m, 16, 8, t2[:, 0:128], after=[A(), E()])
            vcp(qv[:, :, 32:64], tv[:, :, 32:64])
        lin(CQT, 4, "o_iq", 0, 512, False, ev4, HT)
        for f in range(4):
            b = bank()
            for q in range(3):
                tr(b.t[:, q * 128:(q + 1) * 128], QI[:, q, f * 128:(f + 1) * 128], [D(), A()] + b.free)
            evc(QIT[:, f, :], b.t[:, 0:384], [E()])
            b.free = AD()
        for q in range(3):
            m = 1 + q
            n = 128 * (m + 1)
            isc = ISC[:, q, :]
            if n < 512:
                P.op("dve", lambda e, a=isc[:, n:512]: e.memset(a, NEG))
            t0 = AD()
            d = {}

            def i0(h):
                b = d["b", h] = bank()
                sl = slice(64 * (h % 2), 64 * (h % 2) + 64)
                mm(b.t[:, 0:n], QIT[sl, h // 2, q * 128:(q + 1) * 128], KIT[sl, 0:n], True, True, t0 + b.free)
                d["e", h] = E()

            def i1(h):
                act(RL[:, h % 2, 0:n], d["b", h].t[:, 0:n], ACT.Relu, after=[d["e", h], d.get(("s", h - 2))] + t0)
                d["b", h].free = [A()]
                d["r", h] = A()

            def i2(h):
                if h == 0:
                    ts(isc[:, 0:n], RL[:, 0, 0:n], WI[:, m, 0:1], None, ALU.mult, after=[d["r", h]])
                else:
                    stt(isc[:, 0:n], RL[:, h % 2, 0:n], WI[:, m, h:h + 1], isc[:, 0:n], ALU.mult, ALU.add, [d["r", h]])
                d["s", h] = D()
            pipe(8, [i0, i1, i2])
            tt(isc[:, n - 128:n], isc[:, n - 128:n], cst("cmask"), ALU.add)
            dump(f"isc{q}", isc, [128, 512])
            for it in range(16):
                top8(m8, isc[:, 0:n])
            ts(MADD[:, q, :], isc, -2.0e38, NEG, ALU.is_gt, ALU.mult)
            dump(f"madd{q}", MADD[:, q, :], [128, 512])
        mark("mla")
        ar.at(WS)
        QA = ar.take(2, 2, 512)
        PP = ar.take(3, 512)
        PT0 = ar.take(4, 512)
        OL = ar.at(base).take(2, 2, 512)
        PTs = [PT0, ar.take(4, 512)]
        RS = ar.take(8, 4)
        uk, ktok, kslot = load("o_uk", 0, 1, 0, 2048)
        uv, vtok, vslot = load("o_uv", 0, 2, 0, 1024)
        SC = float((128 + 64) ** -0.5)
        t0 = AD() + [E()]
        d = {}

        def a0(t):
            h = t // 4
            if t % 4:
                return
            for c in range(2):
                b = d["q", h, c] = bank()
                mm(b.t[:, :], uk[:, 0, h * 256 + c * 128:h * 256 + (c + 1) * 128], QN[:, h, :], True, True,
                   [ktok] + t0 + b.free)
            d["qe", h] = E()

        def a1(t):
            h = t // 4
            if t % 4:
                return
            for c in range(2):
                b = d["q", h, c]
                d["qt", h, c] = evc(QA[:, h % 2, c, :], b.t[:, :], [d["qe", h], d.get(("s", 4 * h - 5))] + (t0 if t == 0 else []))
                b.free = [d["qt", h, c]]

        def a2(t):
            h, i = t // 4, t % 4
            n = 128 * (i + 1)
            sl = slice(64 * (h % 2), 64 * (h % 2) + 64)
            qa = QA[:, h % 2, :, :]
            s = d["sb", t] = bank()
            mm(s.t[:, 0:n], qa[:, 0, i * 128:n], CKT[:, 0, 0:n], True, False, [d["qt", h, 0], d["qt", h, 1]] + s.free)
            mm(s.t[:, 0:n], qa[:, 1, i * 128:n], CKT[:, 1, 0:n], False, False)
            mm(s.t[:, 0:n], QRT[sl, h // 2, i * 128:n], KRT[sl, 0:n], False, False)
            if i < 1:
                mm(s.t[:, n - 128:n], ident, cst("cmask"), False, True)
            else:
                mm(s.t[:, 0:n], ident, MADD[:, i - 1, 0:n], False, True)
            d["s", t] = E()

        def a3(t):
            n = 128 * (t % 4 + 1)
            rs, s = RS[:, t % 8, :], d["sb", t]
            red(rs[:, 0:1], s.t[:, 0:n], ALU.max, neg=True, after=[d["s", t]])
            ts(rs[:, 0:1], rs[:, 0:1], SC, None, ALU.mult)
            act(PP[:, t % 3, 0:n], s.t[:, 0:n], ACT.Exp, bias=rs[:, 0:1], scale=SC, accum=rs[:, 1:2],
                after=[D(), d.get(("tr", t - 3))])
            s.free = [A()]
            d["x", t] = A()

        def a4(t):
            n = 128 * (t % 4 + 1)
            rs, pp = RS[:, t % 8, :], PP[:, t % 3, 0:n]
            recip(rs[:, 2:3], rs[:, 1:2], after=[d["x", t]])
            ts(pp, pp, rs[:, 2:3], None, ALU.mult)
            d["n", t] = D()

        def a5(t):
            b = d["t", t] = bank()
            for k in range(t % 4 + 1):
                tr(b.t[:, k * 128:(k + 1) * 128], PP[:, t % 3, k * 128:(k + 1) * 128], [d["n", t]] + b.free)
            d["tr", t] = E()

        def a6(t):
            h, i = t // 4, t % 4
            n = 128 * (i + 1)
            b = d["t", t]
            d["c", t] = evc(PTs[h % 2][:, 0:i + 1, i * 128:n], b.t[:, 0:n].rearrange("p (k t) -> p k t", t=128),
                            [d["tr", t], d.get(("ol", h - 2))])
            b.free = [d["c", t]]

        def a7(t):
            h = t // 4
            if t % 4 < 3:
                return
            for c in range(2):
                b = d["l", h, c] = bank()
                for k in range(4):
                    mm(b.t[:, 128 * k:512], CKV[:, k, c * 128:(c + 1) * 128], PTs[h % 2][:, k, 128 * k:512], k == 0, k == 3,
                       [d["c", 4 * h + x] for x in range(4)] + b.free)
            d["ol", h] = E()

        def a8(t):
            h = t // 4
            if t % 4 < 3:
                return
            for c in range(2):
                b = d["l", h, c]
                d["lt", h, c] = evc(OL[:, h % 2, c, :], b.t[:, :], [d["ol", h], d.get(("v", h - 2))])
                b.free = [d["lt", h, c]]

        def a9(t):
            h = t // 4
            if t % 4 < 3:
                return
            b = d["vb", h] = bank()
            for c in range(2):
                mm(b.t[:, :], uv[:, c, h * 128:(h + 1) * 128], OL[:, h % 2, c, :], c == 0, c == 1,
                   [vtok, d["lt", h, 0], d["lt", h, 1]] + b.free)
            d["v", h] = E()

        def a10(t):
            h = t // 4
            if t % 4 < 3:
                return
            put(H, h, d["vb", h].t[:, :], [d["v", h]])
            d["vb", h].free = [D()]
        pipe(32, [a0, a1, a2, a3, a4, a5, a6, a7, a8, a9, a10])
        release(kslot, [E()])
        release(vslot, [E()])
        mark("o_out")
        low([E(), A(), D()])
        st["ht"] = AD()
        lin(H, 8, "o_out", 0, 512, False, res_add(ALPHA, None, 0), HT)
        lin(H, 8, "o_out", 512, 512, False, res_add(ALPHA, None, 512))

    def rms_to_fm(gain):
        ar = Arena()
        tmp = ar.take(1024)
        xn = ar.take(4, 1024)
        act(SM[:, 200:201], SM[:, 201:202], ACT.Copy, after=[E(), D()])
        for j in range(4):
            rms_rows(X[:, j, :], tmp, xn[:, j, :], 1024, None, 1e-6)
        to_fm(xn, H, 8, gain=gain, after=[D(), E()])
        st["ht"] = AD()

    def ffn(l, which):
        mark(f"ffn{which}_{l}")
        rms_to_fm(cst("nf1" if which == 1 else "nf2")[:, 8 * l:8 * l + 8])
        U, tmp = hidden()
        utok = [None, None]
        tiles = (8, 8, 6)

        def up(p):
            for c in range(tiles[p] // 2):
                def ev(m, ps, c=c):
                    t = tmp[:, m % 2, :]
                    if m < 2:
                        act(t, ps[:, :], ACT.Silu, after=[E(), D()])
                        return
                    tt(t, t, ps[:, :], ALU.mult, after=[E(), A()])
                    put(U[p % 2], c * 2 + m - 2, t)
                    utok[p % 2] = AD()
                lin(H, 8, f"fgu{which}_{l}", (4 * p + c) * 512, 512, True, ev, HT)

        def down(p):
            for c in range(2):
                lin_down(f"fd{which}_{l}", U[p % 2], tiles[p], 8 * p, c, res_add(None, 0.5, c * 512),
                         lambda: utok[p % 2])
        up(0)
        for p in range(3):
            if p < 2:
                up(p + 1)
            down(p)
        dump(f"f{which}_{l}", X[:, :, :], [128, 4, 1024])

    def hybrid(l):
        key = f"win_{l}"
        mark(f"hyb{l}_lin")
        rms_to_fm(cst("nmix")[:, 8 * l:8 * l + 8])
        ar = Arena()
        GD = ar.take(12, 512)
        GZ = ar.take(4, 512)
        HQ = ar.take(2, 512)
        HK = ar.take(2, 512)
        CUM = ar.take(2, 512)
        HI = ar.take(4, 256)
        HG = ar.take(4, 256)
        XC = ar.take(2, 512)
        RG = ar.take(2, 512)
        GROW = ar.take(2, 512)
        base = ar.o
        raw = ar.take(2, 516)
        acc = ar.take(512)
        LB = SM[:, 120:124]
        start_act = [E(), D(), A()]
        P.op("pool", lambda e: e.memset(raw[:, :, 0:3], 0.0), [E(), D(), A()])
        g0 = G()
        if l == 0:
            P.op("dve", lambda e: e.memset(LB[:, 0:2], 0.0))
        else:
            hl = cst("hlb")
            s = SM[:, 124:140]
            tt(s[:, 0:2], hl[:, 0:2], hl[:, 2:4], ALU.max)
            tt(s[:, 2:4], hl[:, 0:2], s[:, 0:2], ALU.subtract)
            tt(s[:, 4:6], hl[:, 2:4], s[:, 0:2], ALU.subtract)
            act(s[:, 2:6], s[:, 2:6], ACT.Exp, after=[D()])
            tt(s[:, 6:8], s[:, 2:4], s[:, 4:6], ALU.add, after=[A()])
            recip(s[:, 6:8], s[:, 6:8])
            tt(s[:, 8:10], s[:, 2:4], s[:, 6:8], ALU.mult)
            tt(s[:, 10:12], s[:, 4:6], s[:, 6:8], ALU.mult)
            tt(s[:, 12:14], s[:, 8:10], s[:, 10:12], ALU.add)
            tt(LB[:, 0:2], s[:, 12:14], s[:, 8:10], ALU.subtract)
        ts(LB[:, 2:4], LB[:, 0:2], -1.0, 1.0, ALU.mult, ALU.add)

        def ev_hg(m, ps):
            if m < 2:
                act(HQ[:, m, :], ps[:, :], ACT.Silu, after=[E(), D()])
            else:
                m -= 2
                act(HK[:, m, :], ps[:, :], ACT.Sigmoid, after=[E(), D()])
                ts(CUM[:, m, :], HK[:, m, :], LB[:, 2 + m:3 + m], LB[:, m:m + 1], ALU.mult, ALU.add, after=[A()])
                ts(HK[:, m, :], CUM[:, m, :], -1.0, 1.0, ALU.mult, ALU.add)
                ts(CUM[:, m, :], CUM[:, m, :], 6.0e-20, None, ALU.max)
        lin(H, 8, key, 0, 512, True, ev_hg, HT)
        ts(HQ, HQ, 64.0 ** -0.5, None, ALU.mult, after=[A()])
        gconv = cst("gconv")[:, 48 * l:48 * l + 48]
        rconv = cst("rconv")[:, 8 * l:8 * l + 8]

        def conv_to(dst, ps, w, t, fin):
            r = raw[:, t % 2, :]
            act(r[:, 3:515], ps[:, :], ACT.Copy, after=[E(), D(), g0])
            ts(acc, r[:, 0:512], w[:, 0:1], None, ALU.mult, after=[A()])
            for j in range(1, 4):
                stt(acc, r[:, j:j + 512], w[:, j:j + 1], acc, ALU.mult, ALU.add)
            if fin is None:
                act(dst, acc, ACT.Silu, after=[D()])
            else:
                ts(dst, acc, fin, None, ALU.add)
        for c in range(3):
            lin(H, 8, key, 512 + c * 512, 512, True,
                lambda m, ps, c=c: conv_to(GD[:, c * 4 + m, :], ps, gconv[:, (c * 4 + m) * 4:(c * 4 + m) * 4 + 4], m, None),
                HT)

        def ev_rg(m, ps):
            if m < 2:
                conv_to(XC[:, m, :], ps, rconv[:, m * 4:m * 4 + 4], m, cst("rconvb")[:, 2 * l + m:2 * l + m + 1])
            else:
                act(RG[:, m - 2, :], ps[:, :], ACT.Gelu_apprx_tanh, after=[E(), D()])
        lin(H, 8, key, 2048, 512, True, ev_rg, HT)

        def ev_ig(m, ps):
            vcp(HI[:, m, :], ps[:, 0:256], [E()])
            act(HG[:, m, :], ps[:, 256:512], ACT.Silu, after=[E(), D()])
        lin(H, 8, key, 2560, 512, False, ev_ig, HT)
        lin(H, 8, key, 3072, 512, False, lambda m, ps: act(GZ[:, m, :], ps[:, :], ACT.Silu, after=[E()]), HT)
        w, tok, slot = load(key, 0, 8, 3584, 8)
        P.flush()
        tok = AD() + [tok]
        for i in range(2):
            b = bank()
            for k in range(8):
                mm(b.t[0:4, :], w[:, k, 4 * i:4 * i + 4], f32(H[0][:, k, :]), k == 0, False, tok + b.free)
                mm(b.t[0:4, :], w[:, k, 4 * i:4 * i + 4], f32(H[1][:, k, :]), False, k == 7)
            r = GROW[0:4, i, :]
            if i == 0:
                act(r, b.t[0:4, :], ACT.Sigmoid, after=[E()])
            else:
                ts(r, b.t[0:4, :], cst("gdt")[0:4, l:l + 1], None, ALU.add, after=[E()])
                t3 = acc[0:4, :]
                stt(t3, r, -1.0, r, ALU.mult, ALU.max)
                act(t3, t3, ACT.Exp, scale=-1.0, after=[D()])
                act(t3, t3, ACT.Ln, bias=ones[0:4, 0:1])
                stt(t3, r, 0.0, t3, ALU.max, ALU.add, [A()])
                act(SM[0:4, 142:143], cst("galog")[0:4, l:l + 1], ACT.Exp)
                ts(t3, t3, SM[0:4, 142:143], -1.0, ALU.mult, ALU.mult, after=[A()])
                for j in range(4):
                    scan(r[:, j * 128:(j + 1) * 128], bc(ones[0:4, 0:1], [4, 128]), t3[:, j * 128:(j + 1) * 128], 0.0,
                         ALU.mult, ALU.add)
            b.free = AD()
        release(slot, [E()])

        mark("rg")
        ar.at(WS)
        LA = ar.take(2, 512)
        IG = ar.take(2, 512)
        TA = ar.take(2, 512)
        TBf = ar.take(2, 512)
        w, tok, slot = load(f"rgw_{l}", 0, 1, 0, 512)
        lam = cst("rlam")[:, 2 * l:2 * l + 2]
        s = SM[:, 144:148]
        stt(s[:, 0:2], lam, -1.0, lam, ALU.mult, ALU.max)
        act(s[:, 0:2], s[:, 0:2], ACT.Exp, scale=-1.0, after=[D()])
        act(s[:, 0:2], s[:, 0:2], ACT.Ln, bias=ones[:, 0:1])
        ts(s[:, 2:4], lam, -1.0, 0.0, ALU.mult, ALU.max, after=[A()])
        tt(s[:, 0:2], s[:, 0:2], s[:, 2:4], ALU.add)
        ts(s[:, 0:2], s[:, 0:2], -8.0, None, ALU.mult)
        for m in range(2):
            for q, dst, bias in ((0, LA, "rbr"), (1, IG, "rbi")):
                b = bank()
                mm(b.t[:, :], w[:, 0, (2 * q + m) * 128:(2 * q + m + 1) * 128], XC[:, m, :], True, True,
                   [tok] + AD() + b.free)
                act(dst[:, m, :], b.t[:, :], ACT.Sigmoid, bias=cst(bias)[:, 2 * l + m:2 * l + m + 1], after=[E(), D()])
                b.free = AD()
            ts(LA[:, m, :], LA[:, m, :], s[:, m:m + 1], None, ALU.mult, after=[A()])
        release(slot, [E()])
        act(TA, LA, ACT.Tanh, scale=-1.0, after=[D()])
        act(LA, LA, ACT.Exp)
        ts(TBf, TA, 1.0, None, ALU.add, after=[A()])
        recip(TBf, TBf)
        stt(TA, TA, 2.0, TBf, ALU.mult, ALU.mult)
        act(TA, TA, ACT.Sqrt, after=[D()])
        tt(IG, IG, XC, ALU.mult)
        tt(IG, IG, TA, ALU.mult, after=[A()])
        for m in range(2):
            scan(TBf[:, m, :], LA[:, m, :], IG[:, m, :], 0.0, ALU.mult, ALU.add)
            tt(TBf[:, m, :], TBf[:, m, :], RG[:, m, :], ALU.mult, after=[E(), A()])
            put(H, 6 + m, TBf[:, m, :], [E()])

        mark("hg")
        ar.at(WS)
        XL = ar.take(2, 512)
        DF = ar.take(2, 512)
        QD = XC
        KDc = RG
        act(CUM, CUM, ACT.Ln, after=[D()])
        vcp(DF, CUM, [A(), E()])
        for m in range(2):
            for j in range(4):
                scan(CUM[:, m, j * 128:(j + 1) * 128], bc(ones[:, 0:1], [128, 128]), DF[:, m, j * 128:(j + 1) * 128], 0.0,
                     ALU.mult, ALU.add)
        dump(f"cum_{l}", CUM, [128, 2, 512])
        ET = SM[:, 150:158].rearrange("p (m j) -> p m j", m=2)
        act(ET, CUM.rearrange("p m (j t) -> p m j t", t=128)[:, :, :, 127], ACT.Exp, after=[D()])
        ST = [ar.take(10, 128) for _ in range(3)] + [Arena(base).take(10, 128)]
        for sv in ST:
            P.op("pool", lambda e, sv=sv: e.memset(sv, 0.0), [E(), D(), A()])
        act(QD, CUM, ACT.Exp, after=[D(), E()])
        tt(QD, QD, HQ, ALU.mult, after=[A()])
        for m in range(2):
            for j in range(4):
                t0 = slice(j * 128, (j + 1) * 128)
                ts(KDc[:, m, t0], CUM[:, m, t0], CUM[:, m, j * 128 + 127:j * 128 + 128], None, ALU.subtract)
        act(KDc, KDc, ACT.Exp, scale=-1.0, after=[D()])
        tt(KDc, KDc, HK, ALU.mult, after=[A()])
        hsl = lambda h: slice(64 * (h % 2), 64 * (h % 2) + 64)
        for j in range(1, 4):
            for h in range(4):
                b = bank()
                for i in range(j):
                    mm(b.t[:, i * 128:(i + 1) * 128], KDc[hsl(h), h // 2, i * 128:(i + 1) * 128],
                       QD[hsl(h), h // 2, j * 128:(j + 1) * 128], True, True, AD() + b.free)
                evc(ST[h][:, j * (j + 1) // 2:j * (j + 1) // 2 + j, :], b.t[:, 0:j * 128].rearrange("p (k t) -> p k t", t=128),
                    [E(), G()])
                b.free = AD()
            if j < 3:
                for m in range(2):
                    ts(KDc[:, m, 0:j * 128], KDc[:, m, 0:j * 128], ET[:, m, j:j + 1], None, ALU.mult, after=[E(), A()])
        lev = cst("lev")
        for lv in range(8):
            if lv < 7:
                Bs = 1 << lv
                nb = 512 // (2 * Bs)
                xv = XL.rearrange("p m (n b) -> p (m n) b", b=2 * Bs)
                dv_ = DF.rearrange("p m (n b) -> p (m n) b", b=2 * Bs)
                cv = CUM.rearrange("p m (n b) -> p (m n) b", b=2 * Bs)
                qv = HQ.rearrange("p m (n b) -> p (m n) b", b=2 * Bs)
                kv = HK.rearrange("p m (n b) -> p (m n) b", b=2 * Bs)
                r = bc(cv[:, :, Bs - 1:Bs], [128, 2 * nb, Bs])
                tt(dv_[:, :, Bs:2 * Bs], cv[:, :, Bs:2 * Bs], r, ALU.subtract, after=[A()])
                tt(dv_[:, :, 0:Bs], r, cv[:, :, 0:Bs], ALU.subtract)
                act(DF, DF, ACT.Exp, after=[D()])
                tt(xv[:, :, Bs:2 * Bs], dv_[:, :, Bs:2 * Bs], qv[:, :, Bs:2 * Bs], ALU.mult, after=[A(), E()])
                tt(xv[:, :, 0:Bs], dv_[:, :, 0:Bs], kv[:, :, 0:Bs], ALU.mult)
                L_, R_ = XL, XL
            else:
                L_, R_ = HK, HQ
            for h in range(4):
                b = bank()
                for j in range(4):
                    t0 = slice(j * 128, (j + 1) * 128)
                    mm(b.t[:, t0], L_[hsl(h), h // 2, t0], R_[hsl(h), h // 2, t0], True, True, AD() + b.free)
                for j in range(4):
                    t0 = slice(j * 128, (j + 1) * 128)
                    P.op("dve", lambda e, o=ST[h][:, j * (j + 1) // 2 + j, :], mk=lev[:, lv * 128:(lv + 1) * 128].bitcast(I32),
                         d=b.t[:, t0]: e.copy_predicated(o, mk, d), [E(), G(), A()])
                b.free = AD()
        
        OT = DF.rearrange("p a b -> p (a b)")
        OH = OT.rearrange("p (j c) -> p j c", j=4)
        SQ = XL.rearrange("p a b -> p (a b)")[:, 0:256]
        hnw = cst("hnw")[:, 64 * l:64 * l + 64]
        for j in range(4):
            b = bank()
            for h in range(4):
                for i in range(j + 1):
                    mm(b.t[:, h * 64:(h + 1) * 64], ST[h][:, j * (j + 1) // 2 + i, :], HI[:, i, h * 64:(h + 1) * 64],
                       i == 0, i == j, AD() + b.free)
            act(SQ, b.t[:, 0:256], ACT.Square, after=[E(), D()])
            red(SM[:, 160:164], SQ.rearrange("p (h d) -> p h d", h=4), ALU.add, after=[A()])
            rsq(SM[:, 160:164], SM[:, 160:164], 1.0 / 64, 1e-6)
            o3 = OH[:, j, :].rearrange("p (h d) -> p h d", h=4)
            tt(o3, b.t[:, 0:256].rearrange("p (h d) -> p h d", h=4), bc(SM[:, 160:164].unsqueeze(2), [128, 4, 64]), ALU.mult)
            tt(o3, o3, bc(hnw.unsqueeze(1), [128, 4, 64]), ALU.mult)
            tt(OH[:, j, :], OH[:, j, :], HG[:, j, :], ALU.mult)
            b.free = AD()
        to_fm(OH, H, 2, after=[D(), E()])

        mark("gd")
        hq_off = UP + 16 * 512
        ar.at(hq_off)
        KT_ = ar.take(4, 512)
        VT_ = ar.take(4, 512)
        SCT = ar.take(4, 512)
        CB = ar.take(512)
        BB = ar.take(512)
        assert ar.o <= base - 2 * 512
        ar.at(WS)
        XI = ar.take(4, 512)
        XT = ar.take(4, 512)
        LT = ar.take(4, 512)
        ar.at(base)
        TM = ar.take(512)
        RL_ = ar.take(512)
        LT2 = ar.take(4, 16)
        scT = lambda h: SCT[:, h, :]
        gcol = SM[:, 164:196].rearrange("p (a j h) -> p a j h", a=2, j=4)
        b = bank()
        for a_ in range(2):
            for j in range(4):
                tr(b.t[:, (a_ * 4 + j) * 4:(a_ * 4 + j) * 4 + 4], GROW[0:4, a_, j * 128:(j + 1) * 128], AD() + b.free)
        vcp(SM[:, 164:196], b.t[:, 0:32], [E()])
        b.free = AD()
        t0s = [slice(j * 128, (j + 1) * 128) for j in range(4)]
        by4 = lambda ap: ap.rearrange("p (j t) -> p j t", j=4)
        CBh, BBh = [XI[:, h, :] for h in range(4)], [XT[:, h, :] for h in range(4)]
        tks = AD() + [E()]
        d = {}

        def p0(t):
            b = d["b", t] = bank()
            mm(b.t[:, :], sel[0:4, t // 2 * 128:(t // 2 + 1) * 128], GROW[0:4, 1 - t % 2, :], True, True, tks + b.free)
            d["e", t] = E()

        def p1(t):
            b = d["b", t]
            b.free = [evc((CBh, BBh)[t % 2][t // 2], b.t[:, :], [d["e", t]] + tks)]
        pipe(8, [p0, p1])
        TMS = [LT[:, h, :] for h in range(4)] + [TM, RL_]

        def q0(t):
            act(TMS[t % 6], GD[:, t, :], ACT.Square, after=[d.get(("q5", t - 6))])
            d["q0", t] = A()

        def q1(t):
            b = d["b", t] = bank()
            mm(b.t[:, :], ones, TMS[t % 6], True, True, [d["q0", t]] + b.free)
            d["q1", t] = E()

        def q2(t):
            ts(TMS[t % 6], d["b", t].t[:, :], 1e-6, None, ALU.add, after=[d["q1", t]])
            d["b", t].free = [D()]
            d["q2", t] = D()

        def q3(t):
            act(TMS[t % 6], TMS[t % 6], ACT.Sqrt, after=[d["q2", t]])
            d["q3", t] = A()

        def q4(t):
            recip(TMS[t % 6], TMS[t % 6], after=[d["q3", t]])
            stt(GD[:, t, :], GD[:, t, :], 128.0 ** -0.5 if t < 4 else 1.0, TMS[t % 6], ALU.mult, ALU.mult)
            d["q5", t] = D()
        pipe(8, [q0, q1, q2, q3, q4])
        tks = AD()

        def r0(t):
            b = d["b", t] = bank()
            for j in range(4):
                tr(b.t[:, t0s[j]], GD[:, 4 + t, t0s[j]], tks + b.free)
            d["e", t] = E()

        def r1(t):
            b = d["b", t]
            b.free = [evc(KT_[:, t, :] if t < 4 else VT_[:, t - 4, :], b.t[:, :], [d["e", t]])]
        pipe(8, [r0, r1])
        tks = AD()

        def s0(h):
            for j in range(4):
                ts(LT[:, h, t0s[j]], CBh[h][:, t0s[j]], gcol[:, 1, j, h:h + 1], 0.0, ALU.subtract, ALU.min)
            d["s0", h] = D()
            act((TM, RL_)[h % 2], CBh[h], ACT.Exp, after=[d.get(("s2", h - 2))] + tks)
            d["x", h] = A()

        def s1(h):
            act(LT[:, h, :], LT[:, h, :], ACT.Exp, after=[d["s0", h]])
            d["s1", h] = A()
            for x, o in (("a", h), ("k", 4 + h)):
                b = d[x, h] = bank()
                for j in range(4):
                    mm(b.t[:, t0s[j]], GD[:, 4 + h, t0s[j]], GD[:, o, t0s[j]], True, True, tks + b.free)
            d["e", h] = E()

        def s2(h):
            lt = LT[:, h, :]
            tt(by4(lt), by4(lt), bc(cst("tmask").unsqueeze(1), [128, 4, 128]), ALU.mult, after=[d["s1", h]])
            tt(scT(h), d["a", h].t[:, :], lt, ALU.mult, after=[d["e", h]])
            d["a", h].free = [D()]
            tt(lt, lt, BBh[h], ALU.mult)
            tt(lt, d["k", h].t[:, :], lt, ALU.mult)
            d["k", h].free = [D()]
            tt(GD[:, h, :], GD[:, h, :], (TM, RL_)[h % 2], ALU.mult, after=[d["x", h]])
            d["s2", h] = D()
        pipe(4, [s0, s1, s2])
        cumc, betac = gcol[:, 1, :, :], gcol[:, 0, :, :]
        EC, EL, EX = (LT2[:, x, :].rearrange("p (j h) -> p j h", j=4) for x in range(3))
        for h in range(4):
            vcp(EX[:, :, h], by4(CBh[h])[:, :, 127])
        tt(EL, EX, cumc, ALU.subtract)
        act(EC, cumc, ACT.Exp, after=[D()])
        act(EL, EL, ACT.Exp)
        act(EX, EX, ACT.Exp)
        tt(EC, EC, betac, ALU.mult, after=[A()])
        for h in range(4):
            w3 = lambda ap: bc(ap[:, :, h].unsqueeze(2), [128, 4, 128])
            tt(by4(VT_[:, h, :]), by4(VT_[:, h, :]), w3(betac), ALU.mult)
            tt(by4(GD[:, 8 + h, :]), by4(KT_[:, h, :]), w3(EC), ALU.mult, after=[E()])
            tt(by4(KT_[:, h, :]), by4(KT_[:, h, :]), w3(EL), ALU.mult)
        for h in range(4):
            vcp(by4(XI[:, h, :]), bc(ident.unsqueeze(1), [128, 4, 128]))
            vcp(by4(XT[:, h, :]), bc(ident.unsqueeze(1), [128, 4, 128]))
        mark("gd_inv")
        CTs = [CB, BB]
        P1s = [TM, RL_]
        for h in range(4):
            d["xi", h] = D()

        def v0(t):
            lv, h = t // 4, t % 4
            tt(by4(CTs[t % 2]), by4(LT[:, h, :]), bc(lev[:, lv * 128:(lv + 1) * 128].unsqueeze(1), [128, 4, 128]), ALU.mult,
               after=[d.get(("v1", t - 2))] + (AD() if t < 2 else []))
            d["v0", t] = D()

        def v1(t):
            lv, h = t // 4, t % 4
            b = d["b", t] = bank()
            for t0 in t0s:
                mm(b.t[:, t0], CTs[t % 2][:, t0], XI[:, h, t0], True, True, [d["v0", t], d["xi", h]] + b.free)
            d["v1", t] = E()

        def v2(t):
            act(P1s[t % 2], d["b", t].t[:, :], ACT.Copy, after=[d["v1", t], d.get(("v3", t - 2))] + ([D()] if t < 2 else []))
            d["b", t].free = [A()]
            d["v2", t] = A()

        def v3(t):
            lv, h = t // 4, t % 4
            p1 = P1s[t % 2]
            b = d["x", t] = bank()
            for t0 in t0s:
                mm(b.t[:, t0], p1[:, t0], XT[:, h, t0], True, True, [d["v2", t]] + b.free)
            if lv < 6:
                b2 = d["y", t] = bank()
                for t0 in t0s:
                    mm(b2.t[:, t0], XT[:, h, t0], p1[:, t0], True, True, b2.free)
            d["v3", t] = E()

        def v4(t):
            lv, h = t // 4, t % 4
            if lv < 6:
                tt(XI[:, h, :], XI[:, h, :], d["y", t].t[:, :], ALU.subtract, after=[d["v3", t]])
                d["y", t].free = [D()]
            tt(XT[:, h, :], XT[:, h, :], d["x", t].t[:, :], ALU.subtract, after=[d["v3", t]])
            d["x", t].free = [D()]
            d["xi", h] = D()
        pipe(28, [v0, v1, v2, v3, v4])
        dump(f"xt_{l}", XT, [128, 4, 512])
        mark("gd_chain")
        for h in range(4):
            b = bank()
            for t0 in t0s:
                mm(b.t[:, t0], GD[:, 8 + h, t0], XT[:, h, t0], True, True, AD() + b.free)
            ts(XI[:, h, :], b.t[:, :], -1.0, None, ALU.mult, after=[E()])
            b.free = AD()
        SS = [LT[:, h, 0:128] for h in range(4)]
        VN = [LT[:, h, 128:256] for h in range(4)]
        SQ2 = [LT[:, h, 256:384] for h in range(4)]
        OG = GD[:, 4:8, :]
        gnw = cst("gnw")[:, 128 * l:128 * l + 128]
        SS2 = LT2[:, 3, :].rearrange("p (j h) -> p j h", j=4)
        tks = AD()
        for h in range(4):
            d["S", h] = None

        def c0(t):
            j, h = t // 4, t % 4
            b = d["b", t] = bank()
            mm(b.t[:, 0:128], XT[:, h, t0s[j]], VT_[:, h, t0s[j]], True, j == 0, tks + b.free)
            if j:
                mm(b.t[:, 0:128], XI[:, h, t0s[j]], SS[h], False, True, [d["S", h]])
            d["c0", t] = E()

        def c1(t):
            h = t % 4
            act(VN[h], d["b", t].t[:, 0:128], ACT.Copy, after=[d["c0", t], d.get(("c2", t - 4))] + (tks if t < 4 else []))
            d["b", t].free = [A()]
            d["c1", t] = A()

        def c2(t):
            j, h = t // 4, t % 4
            b = d["o", t] = bank()
            if j:
                mm(b.t[:, 0:128], GD[:, h, t0s[j]], SS[h], True, False, b.free)
            mm(b.t[:, 0:128], scT(h)[:, t0s[j]], VN[h], j == 0, True, [d["c1", t]] + b.free)
            if j < 3:
                mm(b.t[:, 128:256], KT_[:, h, t0s[j]], VN[h], True, True)
            d["c2", t] = E()

        def c3(t):
            j, h = t // 4, t % 4
            b = d["o", t]
            if j == 0:
                vcp(SS[h], b.t[:, 128:256], [d["c2", t]])
            elif j < 3:
                stt(SS[h], SS[h], EX[:, j, h:h + 1], b.t[:, 128:256], ALU.mult, ALU.add, [d["c2", t]])
            d["S", h] = D()
            tt(OG[:, j, h * 128:(h + 1) * 128], b.t[:, 0:128], gnw, ALU.mult, after=[d["c2", t]])
            act(SQ2[h], b.t[:, 0:128], ACT.Square, accum=SS2[:, j, h:h + 1], after=[D()])
            b.free = [A()]
        pipe(16, [c0, c1, c2, c3])
        ts(SS2, SS2, 1.0 / 128, 1e-6, ALU.mult, ALU.add, after=[A()])
        pw(SS2)
        for j in range(4):
            og = OG[:, j, :].rearrange("p (h c) -> p h c", h=4)
            tt(og, og, bc(SS2[:, j, :].unsqueeze(2), [128, 4, 128]), ALU.mult)
            tt(OG[:, j, :], OG[:, j, :], GZ[:, j, :], ALU.mult)
        to_fm(OG, (H[0][:, 2:6, :], H[1][:, 2:6, :]), 4, after=[D(), E()])
        st["ht"] = AD()
        low([E(), A(), D(), G()])
        mark(f"wo{l}")
        lin(H, 8, f"wo_{l}", 0, 512, False, res_add(None, 1.0, 0), HT)
        lin(H, 8, f"wo_{l}", 512, 512, False, res_add(None, 1.0, 512), HT)
        dump(f"m_{l}", X[:, :, :], [128, 4, 1024])

    even_mixer()
    mlp_ple(0)
    odd_mixer()
    mlp_ple(1)
    for l in range(2):
        ffn(l, 1)
        hybrid(l)
        ffn(l, 2)
    w, tok, slot = load("nfin", 0, 1, 0, 1024)
    P.flush()
    ar = Arena()
    tmp = ar.take(1024)
    xo = ar.take(4, 1024)
    P.op("act", lambda e: e.activation(SM[:, 200:201], SM[:, 201:202], ACT.Copy), [E(), D()])
    for j in range(4):
        rms_rows(X[:, j, :], tmp, xo[:, j, :], 1024, None, 1e-6)
        tt(xo[:, j, :], xo[:, j, :], w[:, 0, :], ALU.mult, after=[tok])
    P.op("sp", lambda e, W, S: e.dma_start(W["out"], xo).then_inc(S["out"], 16), [D()])
    return P, stream


def emit(nc, ctx, P, W, n_out):
    S = {e: ctx.enter_context(nc.semaphore("s_" + e)) for e in ("pe", "act", "dve", "pool")}
    for n in ["c", "x", "pos", "out"] + [f"w{i}" for i in range(NS)]:
        S[n] = ctx.enter_context(nc.semaphore("s_" + n))
    block = ctx.enter_context(nc.Block())

    def run(eng, e):
        for fn, waits, inc in P.ops[e]:
            for s, v in waits:
                eng.wait_ge(S[s], v)
            if e == "sp":
                fn(eng, W, S)
            else:
                i = fn(eng)
                if inc:
                    i.then_inc(S[e], 1)

    @block.sync
    def _(eng):
        run(eng, "sp")
        eng.wait_ge(S["out"], 16 * n_out)

    @block.tensor
    def _(eng):
        run(eng, "pe")

    @block.scalar
    def _(eng):
        run(eng, "act")

    @block.vector
    def _(eng):
        run(eng, "dve")

    @block.gpsimd
    def _(eng):
        run(eng, "pool")


def const_block(I):
    f = np.float32
    C = np.zeros((128, NCB), f)

    def put(name, a, rows=128):
        o, w = COFF[name]
        C[:rows, o:o + w] = a.reshape(rows, w)

    def row(a):
        return np.broadcast_to(np.asarray(a).reshape(1, -1), (128, np.asarray(a).size))

    s = np.arange(128)
    put("ident", np.eye(128, dtype=f))
    lev = np.zeros((128, 8, 128), f)
    for lv in range(7):
        B = 1 << lv
        same = (s[:, None] // (2 * B)) == (s[None, :] // (2 * B))
        lev[:, lv, :] = same & ((s[:, None] // B) % 2 == 0) & ((s[None, :] // B) % 2 == 1)
    lev[:, 7, :] = np.eye(128)
    put("lev", lev)
    put("cmask", np.where(s[None, :] <= s[:, None], 0.0, NEG).astype(f))
    put("tmask", (s[:, None] <= s[None, :]).astype(f))
    put("ones", np.ones((128, 128), f))
    sel = np.zeros((128, 4, 128), f)
    for h in range(4):
        sel[h, h, :] = 1
    put("sel", sel)
    t = np.arange(4)[None, :, None] * 128 + s[:, None, None]
    ok = (np.arange(31) * 16 + 31)[None, None, :] <= t
    put("cmpadd", np.where(ok, 0.0, NEG).astype(f))
    put("cmp01", ok.astype(f))
    inv = [np.float32(10000.0) ** (-np.arange(0, d, 2, dtype=f) / np.float32(d)) for d in (64, 32)]
    put("invf", row(np.concatenate(inv).astype(f)))
    put("aconv", I["e_a_conv"][0].reshape(4, 8, 128).transpose(2, 1, 0))
    put("aib", I["e_a_i_b"][0], 4)
    put("afb", I["e_a_f_b"][0], 4)
    put("anorm", row(I["e_a_norm"][0]))
    cp = I["e_b_cmp_pos"][0].transpose(2, 0, 1)
    put("cpos", np.concatenate([cp, cp], 0))
    put("cw2", I["e_b_cmp_w2"][0].transpose(1, 0, 2))
    put("gb", row(I["e_b_g_b"][0]))
    put("qnorm", I["o_q_norm"][0].reshape(4, 128).T)
    put("kvnorm", row(I["o_kv_norm"][0]))
    put("ikg", row(I["o_ik_g"][0]))
    put("ikb", row(I["o_ik_b"][0]))
    for n, k in (("nf1", "norm_ffn1_2"), ("nmix", "norm_mix_2"), ("nf2", "norm_ffn2_2")):
        put(n, I[k].reshape(2, 8, 128).transpose(2, 0, 1))
    for n, k in (("hlb", "hg_lb_2"), ("rconvb", "rg_conv_b_2"), ("rbr", "rg_br_2"), ("rbi", "rg_bi_2"),
                 ("rlam", "rg_lambda_2")):
        put(n, I[k].reshape(2, 2, 128).transpose(2, 0, 1))
    put("hnw", row(I["hg_norm_w_2"]))
    put("gnw", row(I["gd_norm_w_2"]))
    put("gconv", I["gd_conv_w_2"].reshape(2, 4, 12, 128).transpose(3, 0, 2, 1))
    put("rconv", I["rg_conv_w_2"].reshape(2, 4, 2, 128).transpose(3, 0, 2, 1))
    put("galog", I["gd_a_log_2"].T, 4)
    put("gdt", I["gd_dt_bias_2"].T, 4)
    return C


def matrices(I):
    M = {}
    w = I["e_w_in"][0]
    o = np.cumsum([0, 512, 512, 512, 512, 4, 4, 512, 128, 128, 128, 128, 128, 128, 24])
    c = [w[:, o[i]:o[i + 1]] for i in range(14)]
    aq, ak, av, ao, ai, af, bq, bkc, bvc, bks, bvs, bkw, bvw, bg = c
    bq = bq.reshape(1024, 2, 4, 64).transpose(0, 2, 1, 3).reshape(1024, 512)
    M["e_in"] = np.concatenate([aq, ak, bkc, bvc, bks, bkw, bq, av, ao, bvs, bvw, bg, ai, af], 1)
    M["e_g"] = np.concatenate([ai, af], 1)
    M["e_out"] = I["e_w_out"][0]
    cw = I["e_b_cmp_w1"][0].reshape(2, 32, 64, 128).transpose(0, 2, 1, 3).reshape(2, 64, 4096)
    M["cw1"] = np.concatenate([cw[0], cw[0], cw[1], cw[1]], 0)
    rep = lambda a: np.broadcast_to(np.concatenate([x.reshape(-1) for x in a])[None, :], (128, sum(x.size for x in a)))
    for l in range(2):
        M[f"ln1_{l}"] = rep([I["ln1_g"][l], I["ln1_b"][l]])
        M[f"ln2_{l}"] = rep([I["ln2_g"][l], I["ln2_b"][l]])
        M[f"w1_{l}"] = I["mlp_w1"][l]
        M[f"w2_{l}"] = I["mlp_w2"][l]
        M[f"pT_{l}"] = I["p"][l, 0].T
        M[f"pgw_{l}"] = I["ple_gate_w"][l]
        M[f"pw_{l}"] = I["ple_w"][l]
    M["o_in"] = I["o_w_in"][0]
    qb = I["o_w_qb"][0].reshape(512, 8, 192)
    M["o_qb"] = np.concatenate([qb[:, :, :128].reshape(512, 1024), qb[:, :, 128:].reshape(512, 512)], 1)
    M["o_iq"] = I["o_w_iq"][0]
    M["o_uk"] = I["o_w_uk"][0].transpose(2, 1, 0).reshape(128, 2048)
    M["o_uv"] = I["o_w_uv"][0].reshape(256, 1024)
    M["o_out"] = I["o_w_out"][0]
    so = np.cumsum([0, 256, 256, 256, 256, 512, 512, 512, 512, 4, 4, 256, 256])
    for l in range(2):
        for n in ("1", "2"):
            g, u = (I[f"ffn{n}_{k}_2"][l].reshape(1024, 11, 256) for k in ("gate", "up"))
            M[f"fgu{n}_{l}"] = np.concatenate([g, u], 2).reshape(1024, 5632)
            M[f"fd{n}_{l}"] = I[f"ffn{n}_down_2"][l]
        w = I["w_in_2"][l]
        hq, hf, hi, hg, gq, gk, gv, gz, gb, ga, rx, rg = [w[:, so[i]:so[i + 1]] for i in range(12)]
        M[f"win_{l}"] = np.concatenate([hq, hf, gq, gk, gv, rx, rg, hi, hg, gz, gb, ga], 1)
        M[f"wo_{l}"] = I["w_out_2"][l]
        r = np.zeros((128, 4, 128), np.float32)
        for q, k in enumerate(("rg_wr_2", "rg_wi_2")):
            for n in range(4):
                p0 = 64 * (n % 2)
                r[p0:p0 + 64, 2 * q + n // 2, p0:p0 + 64] = I[k][l, n]
        M[f"rgw_{l}"] = r.reshape(128, 512)
    M["nfin"] = rep([I["norm_final_2"]])
    return M


def kernel(**inputs):
    import concourse.bacc as _bacc
    from concourse.bass_utils import run_bass_kernel_spmd as _run

    I = {k: np.asarray(v) for k, v in inputs.items()}
    nc = _bacc.Bacc("TRN2", target_bir_lowering=False, num_devices=1)
    with ExitStack() as ctx:
        P, stream = record(nc, ctx)
        M = matrices(I)
        parts, offs, off = [], [], 0
        for key, k0, nk, c0, ncol in stream:
            a = M[key][k0 * 128:(k0 + nk) * 128, c0:c0 + ncol].reshape(nk, 128, ncol).transpose(1, 0, 2)
            parts.append(a.reshape(-1))
            offs.append((off, nk * ncol))
            off += a.size
        arrays = {"wts": np.concatenate(parts), "cb": const_block(I),
                  "x": np.ascontiguousarray(I["x"][0].reshape(4, 128, 1024).transpose(1, 0, 2)),
                  "pos": np.ascontiguousarray(I["positions"][0].reshape(4, 128).T)}
        W = {}
        for n, a in arrays.items():
            t = nc.dram_tensor("in_" + n, a.shape, mybir.dt.from_np(a.dtype), kind="ExternalInput").ap()
            if n == "wts":
                for i, (o, w) in enumerate(offs):
                    W[i] = t[o:o + 128 * w].rearrange("(p n) -> p n", p=128)
            else:
                W[n] = t
        out = nc.dram_tensor("out_0", (1, 512, 1024), F32, kind="ExternalOutput").ap()
        W["out"] = out[0].rearrange("(j p) n -> p j n", p=128)
        emit(nc, ctx, P, W, 1)
    r = _run(nc, [{"in_" + n: a for n, a in arrays.items()}], core_ids=[0])
    return r.results[0]["out_0"]
```

```python
import numpy as np
import concourse.bass as bass
import concourse.mybir as mybir
from concourse.alu_op_type import AluOpType as ALU
from contextlib import ExitStack

F32 = mybir.dt.float32
F32R = mybir.dt.float32r
I32 = mybir.dt.int32
ACT = mybir.ActivationFunctionType
AX = mybir.AxisListType
T = 512
NS = 4
SLOT = 2048
NB = 32389
WS = 8192
UP = 14336
ALPHA = float((2.0 * 2) ** 0.25)
NEG = -1e30

CONSTS = [
    ("ident", 128), ("lev", 8 * 128), ("cmask", 128), ("tmask", 128), ("ones", 128), ("sel", 512),
    ("cmpadd", 124), ("cmp01", 124), ("invf", 48), ("zero", 1),
    ("aconv", 32), ("aib", 1), ("afb", 1), ("anorm", 512), ("cpos", 64), ("cw2", 128), ("gb", 24),
    ("qnorm", 4), ("kvnorm", 256), ("ikg", 64), ("ikb", 64),
    ("nf1", 16), ("nmix", 16), ("nf2", 16), ("hlb", 4), ("hnw", 128), ("gconv", 96), ("galog", 2), ("gdt", 2),
    ("gnw", 256), ("rconv", 16), ("rconvb", 4), ("rbr", 4), ("rbi", 4), ("rlam", 4),
]
COFF = {}
NCB = 0
for _n, _w in CONSTS:
    COFF[_n] = (NCB, _w)
    NCB += _w


class Prog:

    ENG = ("pe", "act", "dve", "pool", "sp")

    def __init__(self):
        self.ops = {e: [] for e in self.ENG}
        self.cnt = {e: 0 for e in self.ENG}
        self.seen = {e: {} for e in self.ENG}
        self.marks, self.hp = [], []
        self.pending, self.hold = [], False
        self.late = []
        self.need = {e: [] for e in self.ENG}

    def flush(self):
        if self.pending and not self.hold:
            todo, self.pending = self.pending, []
            for f in todo:
                f()

    def last(self, e):
        self.flush()
        if not self.ops[e]:
            return (e, 0)
        o = self.ops[e][-1]
        if not o[2]:
            o[2] = True
            self.cnt[e] += 1
        return (e, self.cnt[e])

    def op(self, e, fn, after=(), chain=True):
        self.flush()
        waits = []
        after = [a for a in after if a is not None] + self.need[e]
        self.need[e] = []
        if chain and e in ("act", "dve", "pool"):
            after.append(self.last(e))
        for s, v in after:
            if v and self.seen[e].get(s, 0) < v and not (e == "pe" and s == "pe"):
                self.seen[e][s] = v
                waits.append((s, v))
        self.ops[e].append([fn, waits, False])


class Bank:
    def __init__(self, t):
        self.t = t
        self.free = []
        self.busy = False


class Region:

    def __init__(self, low, up):
        self.low, self.up = low, up

    def __getitem__(self, at):
        p, c = at
        if c.stop <= UP:
            return self.low[p, c]
        assert c.start >= UP and c.stop <= NB
        return self.up[p, c.start - UP:c.stop - UP]


def pipe(n, stages):
    for t in range(n + len(stages) - 1):
        for k in reversed(range(len(stages))):
            if 0 <= t - k < n:
                stages[k](t - k)


def bc(ap, shape):
    return ap.broadcast_to(shape)


def record(nc, ctx, dbg=None):
    P = Prog()
    sb = lambda n, s, d=F32: ctx.enter_context(nc.sbuf_tensor(n, s, d))
    RING = sb("ring", [128, NS, SLOT])
    X = sb("X", [128, 4, 1024])
    C = sb("C", [128, NCB])
    POS = sb("pos", [128, 4], I32)
    SM = sb("small", [128, 256])
    with nc.sbuf_tensor("arena0", [128, UP], F32) as a0:
        with nc.sbuf_tensor("arena1", [128, NB - UP], F32) as a1:
            ARENA = Region(a0, a1)
    ARENAR = Region(sb("split0", [128, UP], F32R), sb("split1", [128, NB - UP], F32R))
    banks = [Bank(ctx.enter_context(nc.psum_tensor(f"ps{i}", [128, 512], F32))) for i in range(8)]
    st = {"bank": 0, "ev": 0, "wb": 0, "done": None}
    stream = []
    slotfree = [[] for _ in range(NS)]
    misc = []

    def cst(name):
        o, w = COFF[name]
        return C[:, o:o + w]

    def bank():
        P.flush()
        b = banks[st["bank"] % 8]
        if b.busy:
            held, P.hold = P.hold, False
            P.flush()
            P.hold = held
        st["bank"] += 1
        return b

    E = lambda: st["done"] or P.last("pe")
    A = lambda: P.last("act")
    D = lambda: P.last("dve")
    G = lambda: P.last("pool")
    AD = lambda: [A(), D()]

    class Arena:
        def __init__(self, o=UP, split=False):
            self.o, self.t = o, (ARENAR if split else ARENA)

        def take(self, *dims):
            n = int(np.prod(dims))
            v = self.t[:, self.o:self.o + n]
            self.o += n
            assert self.o <= NB, self.o
            if len(dims) == 2:
                v = v.rearrange("p (a b) -> p a b", a=dims[0])
            if len(dims) == 3:
                v = v.rearrange("p (a b c) -> p a b c", a=dims[0], b=dims[1])
            return v

        def at(self, o):
            self.o = o
            return self

    def mark(n):
        P.marks.append((n, len(P.ops["pe"])))

    def mm(out, l, r, start, stop, after=()):
        P.hp.append(1 if l.dtype == F32R else 2)
        P.op("pe", lambda e: e.matmul(out, l, r, start=start, stop=stop, skip_group_check=True), after)

    def tr(out, i, after=()):
        k = i.shape[0]
        P.hp.append(1)
        o, _ = COFF["ident"]
        s0 = i.base_partition() if callable(i.base_partition) else i.base_partition
        idn = C[s0:s0 + k, o + s0:o + s0 + k]
        P.op("pe", lambda e: e.transpose(out, i, idn), after)

    def act(out, i, f, bias=None, scale=None, accum=None, after=()):
        kw = {}
        if bias is not None:
            kw["bias"] = bias
        if scale is not None:
            kw["scale"] = scale
        if accum is not None:
            kw["accum_out"] = accum
        P.op("act", lambda e: e.activation(out, i, f, **kw), after)

    def ts(out, i, s1, s2, o0, o1=None, after=(), accum=None, eng="dve"):
        if o1 is None:
            P.op(eng, lambda e: e.tensor_scalar(out, i, s1, None, o0), after)
        elif accum is not None:
            P.op(eng, lambda e: e.tensor_scalar(out, i, s1, s2, o0, o1, accum_out=accum), after)
        else:
            P.op(eng, lambda e: e.tensor_scalar(out, i, s1, s2, o0, o1), after)

    def tt(out, a, b, o, after=(), eng="dve"):
        P.op(eng, lambda e: e.tensor_tensor(out, a, b, o), after)

    def stt(out, a, s, b, o0, o1, after=()):
        P.op("dve", lambda e: e.scalar_tensor_tensor(out, a, s, b, o0, o1), after)

    def vcp(out, i, after=()):
        P.op("dve", lambda e: e.tensor_copy(out, i), after)

    def bns(out, i, after=()):
        P.op("dve", lambda e: e.bn_stats(out, i), after)

    def bna(out, i):
        P.op("dve", lambda e: e.bn_aggr(out, i))

    def top8(m8, a):
        P.op("dve", lambda e: e.max(m8, a))
        P.op("dve", lambda e: e.match_replace(a, m8, a, -3.0e38))

    def recip(out, i, after=()):
        P.op("dve", lambda e: e.reciprocal(out, i), after)

    def scan(out, a, b, init, o0, o1, after=()):
        P.op("dve", lambda e: e.tensor_tensor_scan(out, a, b, init, o0, o1), after)

    def red(out, i, o, neg=False, after=()):
        P.op("dve", lambda e: e.tensor_reduce(out, i, AX.X, o, negate=neg), after)

    def evc(out, i, after=(), scale=None):
        st["ev"] += 1
        if st["ev"] % 2:
            act(out, i, ACT.Copy, scale=scale, after=after)
            return A()
        if scale is None:
            vcp(out, i, after)
        else:
            ts(out, i, scale, None, ALU.mult, after=after)
        return D()

    def load(key, k0, nk, c0, ncol):
        i = len(stream)
        slot = i % NS
        assert nk * ncol <= SLOT
        stream.append((key, k0, nk, c0, ncol))
        v = RING[:, slot, 0:nk * ncol]
        P.op("sp", lambda e, W, S: e.dma_start(v, W[i]).then_inc(S[f"w{slot}"], 16), slotfree[slot])
        slotfree[slot] = None
        return v.rearrange("p (k n) -> p k n", k=nk), (f"w{slot}", 16 * (i // NS + 1)), slot

    def release(slot, toks):
        slotfree[slot] = list(toks)

    wbuf = [[None, [], i] for i in range(3)]
    for w_ in wbuf:
        o_ = WS + w_[2] * 2048
        w_[0] = (ARENAR[:, o_:o_ + 1024], ARENAR[:, o_ + 1024:o_ + 2048])

    def f32(ap):
        return ap.bitcast(F32)

    def low(tok):
        for w_ in wbuf:
            w_[1] = list(tok)

    def split(view, after):
        w_ = wbuf[st["wb"] % 3]
        st["wb"] += 1
        n = view.shape[1]
        hi, lo = w_[0][0][:, 0:n], w_[0][1][:, 0:n]
        act(hi, view, ACT.Copy, after=list(after) + w_[1])
        tt(lo, view, f32(hi), ALU.subtract, after=[A()])
        return hi, lo, w_, D()

    def mm3(out, l, r, start, stop, after=()):
        mm(out, l[0], r[0], start, False, after)
        mm(out, l[0], r[1], False, False)
        mm(out, l[1], r[0], False, stop)

    def put(dst, k, src, after=(), gain=None, slc=slice(0, 512), dve=None):
        hi, lo = dst[0][:, k, slc], dst[1][:, k, slc]
        act(hi, src, ACT.Copy, scale=gain, after=list(after) + [D() if dve is None else dve])
        if gain is None:
            tt(lo, src, f32(hi), ALU.subtract, after=[A()])
        else:
            stt(lo, src, gain, f32(hi), ALU.mult, ALU.subtract, [A()])

    def pieces(key, nk, c0, ncol, kbase=0):
        per = max(1, min(2, 1024 // ncol))
        for kc in range(0, nk, 4):
            n = min(4, nk - kc)
            w, tok, slot = load(key, kbase + kc, n, c0, ncol)
            for q in range(0, n, per):
                c = min(per, n - q)
                hi, lo, w_, done = split(w[:, q:q + c, :].rearrange("p k n -> p (k n)"), [tok])
                if q + c == n:
                    release(slot, [A(), D()])
                yield kc + q, c, hi.rearrange("p (k n) -> p k n", k=c), lo.rearrange("p (k n) -> p k n", k=c), w_, done

    def between():
        if P.pending:
            P.pending.pop(0)()
        elif P.late:
            P.late.pop(0)()

    def prime(key, nk, c0, ncol, kbase=0):
        P.hold = True
        g = pieces(key, nk, c0, ncol, kbase)
        st["primed"] = ((key, c0, kbase), g, [next(g), next(g)])
        P.hold = False

    def ahead(gen, got=()):
        P.hold = True
        q = list(got)
        if not q:
            q = [next(gen)]
            x = next(gen, None)
            if x is not None:
                q.append(x)
        while q:
            between()
            yield q.pop(0)
            between()
            x = next(gen, None)
            if x is not None:
                q.append(x)
        P.hold = False

    def lin(src, nk, key, c0, ncol, fm, evict, after=(), kbase=0):
        nm = ncol // 128 if fm else 4
        first = True
        gen, got = pieces(key, nk, c0, ncol, kbase), ()
        if st.get("primed"):
            assert st["primed"][0] == (key, c0, kbase)
            gen, got = st["primed"][1:]
            st["primed"] = None
        for k0, c, hi, lo, w_, tok in ahead(gen, got):
            if first:
                bs = [bank() for _ in range(nm)]
                tk = after() if callable(after) else after
                tk = tk if isinstance(tk, tuple) and tk else (list(tk),) * nk
                first = False
            for m in range(nm):
                for k in range(c):
                    kk = k0 + k
                    ms = slice(m * 128, (m + 1) * 128)
                    sh, sl_ = src[0][:, kk, :], src[1][:, kk, :]
                    if fm:
                        l, r = (hi[:, k, ms], lo[:, k, ms]), (sh, sl_)
                    else:
                        l, r = (sh[:, ms], sl_[:, ms]), (hi[:, k, :], lo[:, k, :])
                    nn = 512 if fm else ncol
                    mm3(bs[m].t[:, 0:nn], l, r, kk == 0, kk == nk - 1, [tok] + tk[kk] + bs[m].free)
            w_[1] = [E()]
        P.hold = True
        done = E()
        P.hold = False

        def out(m):
            st["done"] = done
            evict(m, bs[m].t)
            st["done"] = None
            bs[m].free = AD()
            bs[m].busy = False
        for m in range(nm):
            bs[m].busy = True
            P.pending.append(lambda m=m: out(m))

    def lin_down(key, src, nk, k0, c, evict, after):
        lin(src, nk, key, c * 512, 512, False, evict, after, kbase=k0)

    def to_fm(src, dst, nf, gain=None, after=(), plain=False):
        d0, toks = D(), []
        for f in range(nf):
            b = bank()
            for j in range(4):
                tr(b.t[:, j * 128:(j + 1) * 128], src[:, j, f * 128:(f + 1) * 128], list(after) + b.free)
            if plain:
                evc(dst[:, f, :], b.t[:, :], [E()])
            else:
                put(dst, f, b.t[:, :], [E()], None if gain is None else gain[:, f:f + 1], dve=d0)
            b.free = AD()
            toks.append(AD())
        return tuple(toks)

    def pw(x):
        act(x, x, ACT.Sqrt, after=[D()])
        recip(x, x, after=[A()])

    def rsq(out, i, mul, eps):
        ts(out, i, mul, eps, ALU.mult, ALU.add)
        pw(out)

    def layer_norm(key):
        w, tok, slot = load(key, 0, 1, 0, 2048)
        sc, ag, rs, nb = SM[:, 0:12], SM[:, 12:20].rearrange("p (j c) -> p j c", j=4), SM[:, 20:24], SM[:, 24:28]
        for j in range(4):
            bns(sc[:, 0:6], X[:, j, 0:512], [A()])
            bns(sc[:, 6:12], X[:, j, 512:1024])
            bna(ag[:, j, :], sc)
        rsq(rs, ag[:, :, 1], 1.0, 1e-5)
        stt(nb, ag[:, :, 0], -1.0, rs, ALU.mult, ALU.mult)
        t0 = D()
        for j in range(4):
            act(X[:, j, :], X[:, j, :], ACT.Identity, bias=nb[:, j:j + 1], scale=rs[:, j:j + 1], after=[t0])
            tt(X[:, j, :], X[:, j, :], w[:, 0, 0:1024], ALU.mult, [tok, A()])
            tt(X[:, j, :], X[:, j, :], w[:, 0, 1024:2048], ALU.add)
            st["xt", j] = [D()]
        release(slot, [D()])

    def x_to_fm(src, dst, gain=None):
        bs = [bank() for _ in range(8)]
        d0, toks, done = D(), [], []
        for j in range(4):
            for f in range(8):
                tr(bs[f].t[:, j * 128:(j + 1) * 128], src[:, j, f * 128:(f + 1) * 128], st["xt", j] + bs[f].free)
                if j == 3:
                    done.append(E())
        for f in range(8):
            put(dst, f, bs[f].t[:, :], [done[f]], None if gain is None else gain[:, f:f + 1], dve=d0)
            bs[f].free = AD()
            toks.append(AD())
        st["ht"] = tuple(toks)

    def rms_rows(src, tmp, dst, n, out_scale, eps):
        a = SM[:, 16:17]
        act(tmp, src, ACT.Square, accum=a, after=[D()])
        ts(SM[:, 17:18], a, 1.0 / n, eps, ALU.mult, ALU.add, after=[A()])
        pw(SM[:, 17:18])
        ts(dst, src, SM[:, 17:18], None, ALU.mult)

    def dump(name, ap, shape):
        if dbg is None:
            return
        dbg.append((name, shape))
        P.op("sp", lambda e, W, S: e.dma_start(W["dbg_" + name], ap).then_inc(S["out"], 16), [E(), A(), D(), G()])

    P.op("sp", lambda e, W, S: e.dma_start(C[:, :], W["cb"]).then_inc(S["c"], 16))
    P.op("sp", lambda e, W, S: e.dma_start(X[:, :, :], W["x"]).then_inc(S["x"], 16))
    P.op("sp", lambda e, W, S: e.dma_start(POS[:, :], W["pos"]).then_inc(S["pos"], 16))
    cb_tok, x_tok, pos_tok = ("c", 16), ("x", 16), ("pos", 16)
    P.op("dve", lambda e: e.memset(SM[:, :], 0.0), [cb_tok, x_tok])
    P.op("act", lambda e: e.activation(SM[:, 200:201], SM[:, 201:202], ACT.Copy), [cb_tok, D()])
    P.op("pe", lambda e: e.transpose(banks[0].t[:, 0:128], C[:, COFF["ident"][0]:COFF["ident"][0] + 128],
                                     C[:, COFF["ident"][0]:COFF["ident"][0] + 128]), [cb_tok, D()])
    P.hp.append(1)
    H = (ARENAR[:, 0:4096].rearrange("p (a b) -> p a b", a=8), ARENAR[:, 4096:8192].rearrange("p (a b) -> p a b", a=8))
    HT = lambda: st["ht"]
    P.op("pool", lambda e: e.memset(SM[:, 202:203], 0.0), [cb_tok, D()])

    ident, ones, sel = cst("ident"), cst("ones"), cst("sel")

    def res_add(scale_x, scale_y, c0):
        def f(m, ps):
            xs = X[:, m, c0:c0 + 512]
            if scale_y is None:
                stt(xs, xs, scale_x, ps[:, :], ALU.mult, ALU.add, [E()])
            else:
                stt(xs, ps[:, :], scale_y, xs, ALU.mult, ALU.add, [E()])
        return f

    def even_mixer():
        st["ht"] = to_fm(X, H, 8)
        ar = Arena()
        QK = ar.take(8, 512)
        AV = ar.take(4, 4, 129)
        BQ = ar.take(4, 512)
        KCV = ar.take(2, 512)
        KSW = ar.take(2, 512)
        VSW = ar.take(4, 256)
        GT = ar.take(4, 24)
        AO = ar.take(4, 512)
        base = ar.o
        raw = ar.take(2, 516)
        acc = ar.take(512)
        aconv = cst("aconv")
        P.op("pool", lambda e: e.memset(raw[:, :, 0:3], 0.0))
        P.op("pool", lambda e: e.memset(AV[:, :, :, 128:129], 1.0))
        g0 = G()

        def ev_qk(c):
            def f(m, ps):
                t = c * 4 + m
                r = raw[:, t % 2, :]
                act(r[:, 3:515], ps[:, :], ACT.Copy, after=[E(), D(), g0])
                ts(acc, r[:, 0:512], aconv[:, t * 4:t * 4 + 1], None, ALU.mult, after=[A()])
                for j in range(1, 4):
                    stt(acc, r[:, j:j + 512], aconv[:, t * 4 + j:t * 4 + j + 1], acc, ALU.mult, ALU.add)
                act(QK[:, t, :], acc, ACT.Silu, after=[D()])
            return f

        mark("e_lin")
        lin(H, 8, "e_in", 0, 512, True, ev_qk(0), HT)
        lin(H, 8, "e_in", 512, 512, True, ev_qk(1))

        def ev_k(m, ps):
            evc(KCV[:, m, :] if m < 2 else KSW[:, m - 2, :], ps[:, :], [E()])
        lin(H, 8, "e_in", 1024, 512, True, ev_k)
        lin(H, 8, "e_in", 1536, 512, True, lambda m, ps: evc(BQ[:, m, :], ps[:, :], [E()], scale=0.125))
        lin(H, 8, "e_in", 2048, 512, False,
            lambda m, ps: evc(AV[:, m, :, 0:128], ps[:, :].rearrange("p (h d) -> p h d", h=4), [E()]))
        lin(H, 8, "e_in", 2560, 512, False, lambda m, ps: act(AO[:, m, :], ps[:, :], ACT.Sigmoid, after=[E()]))

        mark("e_gates")
        R = [ARENA[0:4, base + i * 512:base + (i + 1) * 512] for i in range(7)]
        bs = [bank() for _ in range(6)]
        for k0, c, hi, lo, w_, tok in ahead(pieces("e_in", 8, 3072, 288)):
            for k in range(c):
                kk = k0 + k
                for m in range(4):
                    ms = slice(m * 128, (m + 1) * 128)
                    mm3(bs[m].t[:, 0:288], (H[0][:, kk, ms], H[1][:, kk, ms]), (hi[:, k, 0:288], lo[:, k, 0:288]), kk == 0,
                        kk == 7, [tok] + bs[m].free)
            w_[1] = [E()]
        P.flush()
        GC = ar.at(base + 7 * 512).take(4, 8)
        for m in range(4):
            vcp(VSW[:, m, :], bs[m].t[:, 0:256], [E()])
            tt(GT[:, m, :], bs[m].t[:, 256:280], cst("gb"), ALU.add)
            vcp(GC[:, m, :], bs[m].t[:, 280:288])
            bs[m].free = AD()
        for i in range(2):
            for m in range(4):
                tr(bs[4 + i].t[0:4, m * 128:(m + 1) * 128], GC[:, m, 4 * i:4 * i + 4], [D()] + bs[4 + i].free)
        act(GT, GT, ACT.Sigmoid, after=[D()])
        for i in range(2):
            ts(R[i], bs[4 + i].t[0:4, :], cst("aib" if i == 0 else "afb")[0:4, :], None, ALU.add, after=[E()])
            bs[4 + i].free = AD()
        stt(R[2], R[1], -1.0, R[1], ALU.mult, ALU.max)
        act(R[2], R[2], ACT.Exp, scale=-1.0, after=[D()])
        act(R[2], R[2], ACT.Ln, bias=ones[0:4, 0:1])
        stt(R[1], R[1], 0.0, R[2], ALU.min, ALU.subtract, [A()])
        scan(R[3], bc(ones[0:4, 0:1], [4, 512]), R[1], 0.0, ALU.mult, ALU.add)
        tt(R[4], R[0], R[3], ALU.subtract)
        scan(R[5], R[4], R[4], 0.0, ALU.max, ALU.max)
        tt(R[6], R[3], R[5], ALU.add)
        act(R[6], R[6], ACT.Exp, scale=-1.0, after=[D()])
        cols = SM[:, 32:64].rearrange("p (a b c) -> p a b c", a=2, b=4)
        b = bank()
        for a_, r in ((0, R[4]), (1, R[6])):
            for j in range(4):
                tr(b.t[:, (a_ * 4 + j) * 4:(a_ * 4 + j) * 4 + 4], r[:, j * 128:(j + 1) * 128], AD() + b.free)
        vcp(SM[:, 32:64], b.t[:, 0:32], [E()])
        b.free = AD()
        MR = ARENA[0:4, 14336 - 512:14336]
        vcp(MR, R[5], [E(), A()])
        R = R[0:5] + [MR]
        ar.at(0)
        mark("mlstm")
        PT = ar.take(2, 4, 512)
        MBS = ar.take(4, 512)
        BST = ar.take(16, 6)
        BAG = ar.take(16, 2)
        RST = ar.take(16)
        DEN = ar.take(16)
        DE2 = ar.take(16)
        t0 = AD()
        for h in range(4):
            b = bank()
            mm(b.t[:, :], sel[0:4, h * 128:(h + 1) * 128], R[5], True, True, t0 + b.free)
            b.free = [evc(MBS[:, h, :], b.t[:, :], [E()])]
        t0 = AD()
        d = {}

        def m0(t):
            h, i = t // 4, t % 4
            x = PT[:, h % 2, i, i * 128:512]
            ts(x, MBS[:, h, i * 128:512], cols[:, 0, i, h:h + 1], 0.0, ALU.subtract, ALU.max,
               after=[A()] if t == 0 else [d.get(("pv", h - 2))])
            d["g", t] = D()

        def m1(t):
            h, i = t // 4, t % 4
            x = PT[:, h % 2, i, i * 128:512]
            act(x, x, ACT.Exp, scale=-1.0, after=[d["g", t]])
            d["e", t] = A()
            b = d["b", t] = bank()
            mm(b.t[:, 0:512 - 128 * i], QK[:, 4 + h, i * 128:(i + 1) * 128], QK[:, h, i * 128:512], True, True, t0 + b.free)
            d["s", t] = E()

        def m2(t):
            h, i = t // 4, t % 4
            y = PT[:, h % 2, i, i * 128:(i + 1) * 128]
            x = PT[:, h % 2, i, i * 128:512]
            tt(y, y, cst("tmask"), ALU.mult, after=[d["e", t]])
            stt(x, d["b", t].t[:, 0:512 - 128 * i], 128.0 ** -0.5, x, ALU.mult, ALU.mult, [d["s", t]])
            d["b", t].free = [D()]
            d["p", h] = D()

        def m3(t):
            h = t // 4
            if t % 4 < 3:
                return
            for jp in range(2):
                b = d["n", h, jp] = bank()
                for jj in range(2):
                    j = jp * 2 + jj
                    for i in range(j + 1):
                        mm(b.t[:, jj * 129:(jj + 1) * 129], PT[:, h % 2, i, j * 128:(j + 1) * 128], AV[:, i, h, :], i == 0,
                           i == j, [d["p", h]] + b.free)
                d["nt", h, jp] = E()
            d["pv", h] = E()

        def m4(t):
            h = t // 4
            if t % 4 < 3:
                return
            for jp in range(2):
                b = d["n", h, jp]
                bv = b.t[:, 0:258].rearrange("p (j c) -> p j c", j=2)
                c0 = 4 * h + 2 * jp
                x, y = DEN[:, c0:c0 + 2], DE2[:, c0:c0 + 2]
                vcp(x, bv[:, :, 128], [d["nt", h, jp]])
                stt(y, x, -1.0, x, ALU.mult, ALU.max)
                tt(y, y, cols[:, 1, 2 * jp:2 * jp + 2, h], ALU.max)
                recip(y, y)
                q = QK[:, h, jp * 256:(jp + 1) * 256].rearrange("p (j c) -> p j c", j=2)
                tt(q, bv[:, :, 0:128], bc(y.unsqueeze(2), [128, 2, 128]), ALU.mult)
                b.free = [D()]
                for jj in range(2):
                    bns(BST[:, c0 + jj, :], q[:, jj, :])
                    bna(BAG[:, c0 + jj, :], BST[:, c0 + jj, :])
        pipe(16, [m0, m1, m2, m3, m4])
        rsq(RST, BAG[:, :, 1], 1.0, 1e-5)
        for h in range(4):
            q = QK[:, h, :].rearrange("p (j c) -> p j c", j=4)
            tt(q, q, bc(BAG[:, 4 * h:4 * h + 4, 0].unsqueeze(2), [128, 4, 128]), ALU.subtract)
            tt(q, q, bc(RST[:, 4 * h:4 * h + 4].unsqueeze(2), [128, 4, 128]), ALU.mult)
        free = ar.o
        YA = ar.at(base).take(4, 1024)
        for j in range(4):
            y = YA[:, j, 0:512]
            qv = QK[:, 0:4, j * 128:(j + 1) * 128]
            tt(y.rearrange("p (h d) -> p h d", h=4), qv, cst("anorm").rearrange("p (h d) -> p h d", h=4), ALU.mult,
               after=[E(), A()])
            tt(y, y, AO[:, j, :], ALU.mult)
        dump("ya", YA[:, :, 0:512], [128, 4, 512])

        mark("nsa_cmp")
        ar.at(UP)
        blk = ar.take(16, 2, 31)
        PP = ar.take(2, 512)
        PT2 = ar.take(2, 512)
        hid = ar.take(2, 64)
        assert ar.o <= UP + 4096
        ar.at(free)
        kc = ar.take(31)
        vc = ar.take(2, 64)
        PCs = ar.take(4, 8, 32)
        PCTs = ar.take(2, 8, 128)
        rcs = ar.take(4, 3, 8)
        KSWP = ar.take(2, 512)
        cpos = cst("cpos")
        for jj in range(2):
            b = bank()
            for q in range(2):
                mm(b.t[64 * q:64 * q + 64, :], ident[:, 64 - 64 * q:128 - 64 * q], KCV[:, jj, :], True, True, AD() + b.free)
            act(KSWP[:, jj, :], b.t[:, :], ACT.Copy, after=[E()])
            b.free = [A()]
        for jj in range(2):
            w0, tok0, slot0 = load("cw1", jj, 1, 0, 2048)
            for g in range(2):
                for q in range(2):
                    rows = slice(64 * q, 64 * q + 64)
                    u = (KCV if g == q else KSWP)[rows, jj, :].rearrange("p (m l) -> p l m", l=16)
                    pb = cpos[rows, jj * 32 + q:(jj + 1) * 32:2].unsqueeze(2)
                    tt(blk[rows, 0:8, g, :], u[:, q:16:2, 0:31], bc(pb[:, 0:8, :], [64, 8, 31]), ALU.add, after=[E(), A()])
                    tt(blk[rows, 8:16, g, :], u[:, q:16:2, 1:32], bc(pb[:, 8:16, :], [64, 8, 31]), ALU.add)
            hb = bank()
            for l in range(16):
                mm(hb.t[:, 0:62], w0[:, 0, l * 128:(l + 1) * 128], blk[:, l, :, :].rearrange("p g m -> p (g m)"),
                   l == 0, l == 15, [tok0, D()] + hb.free)
            release(slot0, [E()])
            act(hid[:, jj, :].rearrange("p (g m) -> p g m", g=2)[:, :, 0:31],
                hb.t[:, 0:62].rearrange("p (g m) -> p g m", g=2), ACT.Gelu_apprx_tanh, after=[E()])
            hb.free = AD()
            b = bank()
            cw2 = cst("cw2")[:, jj * 64:(jj + 1) * 64]
            for g in range(2):
                if jj == 0:
                    mm(b.t[64 * g:64 * g + 64, 0:31], cw2, hid[:, 0, g * 32:g * 32 + 31], True, True, [A()] + b.free)
                else:
                    mm(b.t[0:31, g * 64:(g + 1) * 64], hid[:, 1, g * 32:g * 32 + 31], cw2, True, True, [A()] + b.free)
            if jj == 0:
                vcp(kc, b.t[:, 0:31], [E()])
            else:
                vcp(vc[0:31, :, :].rearrange("p a b -> p (a b)"), b.t[0:31, 0:128], [E()])
            b.free = AD()
        dump("kc", kc, [128, 31])
        mark("nsa")
        ca, c01 = cst("cmpadd"), cst("cmp01")
        t0 = AD() + [E()]
        d = {}

        def b0(i):
            cb = d["b", i] = [bank(), bank()]
            for h in range(8):
                g, j = h // 4, h % 4
                mm(cb[g].t[:, j * 32:j * 32 + 31], BQ[64 * g:64 * g + 64, j, i * 128:(i + 1) * 128], kc[64 * g:64 * g + 64, :], True,
                   True, t0 + cb[g].free)
            d["q", i] = E()

        def b1(i):
            cb = d["b", i]
            pc, rc = PCs[:, i, :, 0:31], rcs[:, i, :, :]
            for g in range(2):
                tt(pc[:, 4 * g:4 * g + 4, :], cb[g].t[:, 0:128].rearrange("p (h m) -> p h m", h=4)[:, :, 0:31],
                   bc(ca[:, i * 31:(i + 1) * 31].unsqueeze(1), [128, 4, 31]), ALU.add, after=[d["q", i]] + t0)
                cb[g].free = [D()]
            red(rc[:, 0, :], pc, ALU.max)
            tt(pc, pc, bc(rc[:, 0, :].unsqueeze(2), [128, 8, 31]), ALU.subtract)
            d["1", i] = D()
            act(pc, pc, ACT.Exp, after=[d["1", i]])
            d["2", i] = A()

        def b2(i):
            pc, rc = PCs[:, i, :, 0:31], rcs[:, i, :, :]
            red(rc[:, 1, :], pc, ALU.add, after=[d["2", i]])
            tt(pc, pc, bc(c01[:, i * 31:(i + 1) * 31].unsqueeze(1), [128, 8, 31]), ALU.mult)
            d["3", i] = D()
            recip(rc[:, 2, :], rc[:, 1, :])
            tt(rc[:, 2, :], rc[:, 2, :], GT[:, i, 0:24:3], ALU.mult)

        def b3(i):
            for hh in range(2):
                b = d["t", i, hh] = bank()
                for q in range(4):
                    tr(b.t[0:31, q * 128:(q + 1) * 128], PCs[:, i, hh * 4 + q, 0:31], [d["3", i]] + b.free)
                d["te", i, hh] = E()

        def b4(i):
            for hh in range(2):
                b = d["t", i, hh]
                d["c", i, hh] = evc(PCTs[0:31, i % 2, hh * 4:hh * 4 + 4, :].rearrange("p a b -> p (a b)"), b.t[0:31, :],
                                    [d["te", i, hh], d.get(("v", i - 2))])
                b.free = [d["c", i, hh]]

        def b5(i):
            b = d["o", i] = bank()
            for h in range(8):
                mm(b.t[:, h * 64:(h + 1) * 64], PCTs[0:31, i % 2, h, :], vc[0:31, h // 4, :], True, True,
                   [d["c", i, 0], d["c", i, 1]] + b.free)
            d["v", i] = E()

        def b6(i):
            b = d["o", i]
            tt(YA[:, i, 512:1024].rearrange("p (h d) -> p h d", h=8), b.t[:, :].rearrange("p (h d) -> p h d", h=8),
               bc(rcs[:, i, 2, :].unsqueeze(2), [128, 8, 64]), ALU.mult, after=[d["v", i]])
            b.free = [D()]
        pipe(4, [b0, b1, b2, b3, b4, b5, b6])
        RS = ar.take(8, 4)
        t0 = AD() + [E()]
        d = {}

        def where(t):
            i, h, br = t // 16, t // 2 % 8, t % 2
            return i, h, br, 128 * (i + 1), h // 4, h % 4

        def n0(t):
            i, h, br, n, g, j = where(t)
            sl = slice(64 * g, 64 * g + 64)
            b = d["s", t] = bank()
            mm(b.t[:, 0:n], BQ[sl, j, i * 128:(i + 1) * 128], KSW[sl, br, 0:n], True, False, t0 + b.free)
            mm(b.t[:, n - 128:n], ident, cst("cmask"), False, True)
            d["se", t] = E()

        def n1(t):
            i, h, br, n, g, j = where(t)
            b, rs = d["s", t], RS[:, t % 8, :]
            red(rs[:, 0:1], b.t[:, 0:n], ALU.max, neg=True, after=[d["se", t]] + (t0 if t == 0 else []))
            act(PP[:, t % 2, 0:n], b.t[:, 0:n], ACT.Exp, bias=rs[:, 0:1], accum=rs[:, 1:2],
                after=[D(), d.get(("tr", t - 2))])
            d["x", t] = A()
            b.free = [A()]

        def n2(t):
            i, h, br, n, g, j = where(t)
            b = d["t", t] = bank()
            for k in range(i + 1):
                tr(b.t[:, k * 128:(k + 1) * 128], PP[:, t % 2, k * 128:(k + 1) * 128], [d["x", t]] + b.free)
            d["tr", t] = E()

        def n3(t):
            i, h, br, n, g, j = where(t)
            rs, b = RS[:, t % 8, :], d["t", t]
            d["c", t] = evc(PT2[:, t % 2, 0:n], b.t[:, 0:n], [d["tr", t], d.get(("pv", t - 2))])
            b.free = [d["c", t]]
            recip(rs[:, 2:3], rs[:, 1:2], after=[d["x", t]])
            tt(rs[:, 2:3], rs[:, 2:3], GT[:, i, 3 * h + 1 + br:3 * h + 2 + br], ALU.mult)

        def n4(t):
            i, h, br, n, g, j = where(t)
            b = d["o", t] = bank()
            for k in range(i + 1):
                mm(b.t[:, 0:64], PT2[:, t % 2, k * 128:(k + 1) * 128], VSW[:, k, br * 128 + 64 * g:br * 128 + 64 * g + 64],
                   k == 0, k == i, [d["c", t]] + b.free)
            d["pv", t] = E()

        def n5(t):
            i, h, br, n, g, j = where(t)
            y = YA[:, i, 512 + 64 * h:576 + 64 * h]
            stt(y, d["o", t].t[:, 0:64], RS[:, t % 8, 2:3], y, ALU.mult, ALU.add, [d["pv", t]])
            d["o", t].free = [D()]
        pipe(64, [n0, n1, n2, n3, n4, n5])
        dump("yb", YA[:, :, 512:1024], [128, 4, 512])
        mark("e_out")
        low([E(), A(), D(), G()])
        act(SM[:, 200:201], SM[:, 201:202], ACT.Copy, after=[E(), D()])
        st["ht"] = to_fm(YA, H, 8, after=AD() + [E()])
        lin(H, 8, "e_out", 0, 512, False, res_add(ALPHA, None, 0), HT)
        lin(H, 8, "e_out", 512, 512, False, res_add(ALPHA, None, 512))

    def hidden():
        r = Arena(split=True)
        U = [(r.take(8, 512), r.take(8, 512)) for _ in range(2)]
        return U, Arena(r.o).take(3, 512)

    def mlp_ple(l):
        mark(f"mlp{l}")
        prime(f"w1_{l}", 8, 0, 512)
        layer_norm(f"ln1_{l}")
        x_to_fm(X, H)
        dump(f"ln1_{l}", X[:, :, :], [128, 4, 1024])
        U, tmp = hidden()
        utok = [None, None]

        def up(p):
            for c in range(2):
                def ev(m, ps, c=c):
                    t = tmp[:, m % 2, :]
                    hi, lo = U[p % 2][0][:, c * 4 + m, :], U[p % 2][1][:, c * 4 + m, :]
                    act(t, ps[:, :], ACT.Relu, after=[E(), D()])
                    act(hi, t, ACT.Square)
                    tt(t, t, t, ALU.mult, after=[A()])
                    tt(lo, t, f32(hi), ALU.subtract)
                    if m == 3:
                        utok[p % 2] = AD()
                lin(H, 8, f"w1_{l}", (2 * p + c) * 512, 512, True, ev, HT)

        def down(p):
            for c in range(2):
                lin_down(f"w2_{l}", U[p % 2], 8, 8 * p, c, res_add(ALPHA if p == 0 else 1.0, None, c * 512),
                         lambda: utok[p % 2])
        up(0)
        for p in range(4):
            if p < 3:
                up(p + 1)
            down(p)
        mark(f"ple{l}")
        prime(f"pgw_{l}", 8, 0, 512)
        layer_norm(f"ln2_{l}")
        x_to_fm(X, H)
        ar = Arena(split=True)
        pT = (ar.take(2, 512), ar.take(2, 512))
        pg = Arena(ar.o).take(4, 512)
        w, tok, slot = load(f"pT_{l}", 0, 2, 0, 512)
        for k in range(2):
            put(pT, k, w[:, k, :], [tok, E()])
        release(slot, AD())
        ptok = AD()
        for c in range(2):
            def ev(m, ps):
                act(pg[:, m, :], ps[:, :], ACT.Sigmoid, after=[E(), D()])

            def ev2(m, ps, c=c):
                tt(pg[:, m, :], pg[:, m, :], ps[:, :], ALU.mult, after=[E(), A()])
                tt(X[:, m, c * 512:(c + 1) * 512], X[:, m, c * 512:(c + 1) * 512], pg[:, m, :], ALU.add)
            lin(H, 8, f"pgw_{l}", c * 512, 512, False, ev, HT)
            lin(pT, 2, f"pw_{l}", c * 512, 512, False, ev2, ptok)
        dump(f"h_{l}", X[:, :, :], [128, 4, 1024])

    def odd_mixer():
        mark("o_lin")
        st["ht"] = to_fm(X, H, 8, after=[D(), A(), E()])
        ar = Arena()
        CKV = ar.take(4, 256)
        CKT = ar.take(2, 512)
        KRT = ar.take(512)
        KIT = ar.take(512)
        WI = ar.take(4, 8)
        MADD = ar.take(3, 512)
        TAB = ar.take(4, 96)
        QRT = ar.take(4, 512)
        QN = ar.take(8, 512)
        base = ar.o
        CQ = ar.take(4, 512)
        KD = ar.take(4, 256)
        tmp = ar.take(512)
        QI = Arena(ar.o).take(3, 512)
        T4 = ar.take(4, 392)
        tmpc = ar.take(512)
        ANG = ar.take(4, 48)
        KK = ar.take(4, 48)
        RR = ar.take(4, 48)

        def tables():
            pf = SM[:, 90:94]
            vcp(pf, POS[:, :], [pos_tok, A()])
            tt(ANG, bc(pf.unsqueeze(2), [128, 4, 48]), bc(cst("invf").unsqueeze(1), [128, 4, 48]), ALU.mult)
            MAGIC = 12582912.0
            TWO_PI = (6.28125, 0.0019350051879882812, 3.0199160517e-07)
            for which in range(2):
                ts(KK, ANG, 1.0 / (2.0 * np.pi), 0.25 if which == 0 else 0.0, ALU.mult, ALU.add, after=[A()])
                ts(KK, KK, MAGIC, None, ALU.add)
                ts(KK, KK, MAGIC, None, ALU.subtract)
                stt(RR, KK, -TWO_PI[0], ANG, ALU.mult, ALU.add)
                stt(RR, KK, -TWO_PI[1], RR, ALU.mult, ALU.add)
                stt(RR, KK, -TWO_PI[2], RR, ALU.mult, ALU.add)
                if which == 0:
                    ts(RR, RR, float(np.pi / 2), None, ALU.add)
                ts(RR, RR, 3.1415925, -3.1415925, ALU.min, ALU.max)
                act(TAB[:, :, 32 * which:32 * which + 32], RR[:, :, 0:32], ACT.Sin, after=[D()])
                act(TAB[:, :, 64 + 16 * which:80 + 16 * which], RR[:, :, 32:48], ACT.Sin)

        def rope(dst, src, j, half, heads, t1, after=()):
            o = 0 if half == 32 else 64
            cs = bc(TAB[:, j, o:o + half].unsqueeze(1), [128, heads, half])
            sn = bc(TAB[:, j, o + half:o + 2 * half].unsqueeze(1), [128, heads, half])
            x1, x2 = src[:, :, 0:half], src[:, :, half:2 * half]
            tv = t1.rearrange("p (h d) -> p h d", h=heads)
            tt(tv, x2, sn, ALU.mult, after=after)
            tt(dst[:, :, 0:half], x1, cs, ALU.mult)
            tt(dst[:, :, 0:half], dst[:, :, 0:half], tv, ALU.subtract)
            tt(tv, x1, sn, ALU.mult)
            tt(dst[:, :, half:2 * half], x2, cs, ALU.mult)
            tt(dst[:, :, half:2 * half], dst[:, :, half:2 * half], tv, ALU.add)

        def ev_cq(m, ps):
            evc(CQ[:, m, :], ps[:, :], [E()])
            t0 = [A(), D()]
            a = SM[:, 16 + m:17 + m]
            act(tmpc, CQ[:, m, :], ACT.Square, accum=a, after=t0)
            ts(a, a, 1.0 / 512, 1e-5, ALU.mult, ALU.add, after=[A()])
            pw(a)
            ts(CQ[:, m, :], CQ[:, m, :], a, None, ALU.mult)
        lin(H, 8, "o_in", 0, 512, False, ev_cq, HT)

        def latent(m):
            kv, raw = CKV[:, m, :], T4[:, m, :]
            act(kv, raw[:, 0:256], ACT.Square, accum=SM[:, 95:96], after=[D()])
            ts(SM[:, 96:97], SM[:, 95:96], 1.0 / 256, 1e-5, ALU.mult, ALU.add, after=[A()])
            pw(SM[:, 96:97])
            ts(kv, raw[:, 0:256], SM[:, 96:97], None, ALU.mult)
            tt(kv, kv, cst("kvnorm"), ALU.mult)
            rope(KD[:, m, 0:64].unsqueeze(1), raw[:, 256:320].unsqueeze(1), m, 32, 1, tmp[:, 400:432])
            vcp(KD[:, m, 64:128], KD[:, m, 0:64])
            bns(SM[:, 98:104], raw[:, 320:384])
            bna(SM[:, 104:106], SM[:, 98:104])
            rsq(SM[:, 106:107], SM[:, 105:106], 1.0, 1e-5)
            ki = KD[:, m, 128:192]
            ts(ki, raw[:, 320:384], SM[:, 104:105], SM[:, 106:107], ALU.subtract, ALU.mult)
            tt(ki, ki, cst("ikg"), ALU.mult)
            tt(ki, ki, cst("ikb"), ALU.add)
            rope(KD[:, m, 192:224].unsqueeze(1), KD[:, m, 128:160].unsqueeze(1), m, 16, 1, tmp[:, 400:416])
            vcp(KD[:, m, 128:160], KD[:, m, 192:224])
            vcp(KD[:, m, 192:256], KD[:, m, 128:192])
            ts(WI[:, m, :], raw[:, 384:392], float(8 ** -0.5 * 64 ** -0.5), None, ALU.mult)
        lin(H, 8, "o_in", 512, 392, False, lambda m, ps: evc(T4[:, m, :], ps[:, 0:392], [E(), D(), A()]), HT)
        CQT = (H[0][:, 0:4, :], H[1][:, 0:4, :])
        st["ht"] = to_fm(CQ, CQT, 4, gain=cst("qnorm"), after=[D()])

        def first():
            tables()
            latent(0)
        P.late = [first, lambda: latent(1), lambda: latent(2), lambda: latent(3)]
        for c in range(2):
            lin(CQT, 4, "o_qb", c * 512, 512, True,
                lambda m, ps, c=c: evc(QN[:, c * 4 + m, :], ps[:, :], [E()]), HT)
        assert not P.late
        QR = CQ
        def ev3(m, ps):
            evc(tmp, ps[:, :], [E(), D(), A()])
            rope(QR[:, m, :].rearrange("p (h d) -> p h d", h=8), tmp.rearrange("p (h d) -> p h d", h=8), m, 32, 8,
                 tmpc[:, 0:256], after=[A(), D(), E()])
        lin(CQT, 4, "o_qb", 1024, 512, False, ev3, HT)
        mark("index")
        t2 = tmpc
        def ev4(m, ps):
            if m == 0:
                return
            q = m - 1
            act(tmp, ps[:, :], ACT.Copy, after=[E(), D()])
            qv = QI[:, q, :].rearrange("p (h d) -> p h d", h=8)
            tv = tmp.rearrange("p (h d) -> p h d", h=8)
            rope(qv[:, :, 0:32], tv[:, :, 0:32], m, 16, 8, t2[:, 0:128], after=[A(), E()])
            vcp(qv[:, :, 32:64], tv[:, :, 32:64])
        lin(CQT, 4, "o_iq", 0, 512, False, ev4, HT)
        P.hold = True
        to_fm(CKV, CKT, 2, after=[D()], plain=True)
        for f, dst in ((0, KRT), (1, KIT)):
            b = bank()
            for j in range(4):
                tr(b.t[:, j * 128:(j + 1) * 128], KD[:, j, f * 128:(f + 1) * 128], [D()] + b.free)
            evc(dst, b.t[:, :], [E()])
            b.free = AD()
        P.hold = False
        to_fm(QR, QRT, 4, after=[D()], plain=True)
        ar.at(base)
        m8 = ar.take(8)
        ISC = ar.take(3, 512)
        RL = ar.take(2, 512)
        QIT = Arena(WS).take(4, 384)
        for f in range(4):
            b = bank()
            for q in range(3):
                tr(b.t[:, q * 128:(q + 1) * 128], QI[:, q, f * 128:(f + 1) * 128], [D(), A()] + b.free)
            evc(QIT[:, f, :], b.t[:, 0:384], [E()])
            b.free = AD()
        for q in range(3):
            m = 1 + q
            n = 128 * (m + 1)
            isc = ISC[:, q, :]
            if n < 512:
                P.op("dve", lambda e, a=isc[:, n:512]: e.memset(a, NEG), [E()])
            t0 = AD()
            d = {}

            def i0(h):
                b = d["b", h] = bank()
                sl = slice(64 * (h % 2), 64 * (h % 2) + 64)
                mm(b.t[:, 0:n], QIT[sl, h // 2, q * 128:(q + 1) * 128], KIT[sl, 0:n], True, True, t0 + b.free)
                d["e", h] = E()

            def i1(h):
                act(RL[:, h % 2, 0:n], d["b", h].t[:, 0:n], ACT.Relu, after=[d["e", h], d.get(("s", h - 2))] + t0)
                d["b", h].free = [A()]
                d["r", h] = A()

            def i2(h):
                if h == 0:
                    ts(isc[:, 0:n], RL[:, 0, 0:n], WI[:, m, 0:1], None, ALU.mult, after=[d["r", h]])
                else:
                    stt(isc[:, 0:n], RL[:, h % 2, 0:n], WI[:, m, h:h + 1], isc[:, 0:n], ALU.mult, ALU.add, [d["r", h]])
                d["s", h] = D()
            pipe(8, [i0, i1, i2])
            tt(isc[:, n - 128:n], isc[:, n - 128:n], cst("cmask"), ALU.add)
            dump(f"isc{q}", isc, [128, 512])
            for it in range(16):
                top8(m8, isc[:, 0:n])
            ts(MADD[:, q, :], isc, -2.0e38, NEG, ALU.is_gt, ALU.mult)
            dump(f"madd{q}", MADD[:, q, :], [128, 512])
        mark("mla")
        ar.at(WS)
        QA = ar.take(2, 2, 512)
        PP = ar.take(3, 512)
        PT0 = ar.take(4, 512)
        OL = ar.at(base).take(2, 2, 512)
        PTs = [PT0, ar.take(4, 512)]
        RS = ar.take(8, 4)
        uk, ktok, kslot = load("o_uk", 0, 1, 0, 2048)
        uv, vtok, vslot = load("o_uv", 0, 2, 0, 1024)
        SC = float((128 + 64) ** -0.5)
        t0 = AD() + [E()]
        d = {}

        def a0(t):
            h = t // 4
            if t % 4:
                return
            for c in range(2):
                b = d["q", h, c] = bank()
                mm(b.t[:, :], uk[:, 0, h * 256 + c * 128:h * 256 + (c + 1) * 128], QN[:, h, :], True, True,
                   [ktok] + t0 + b.free)
            d["qe", h] = E()

        def a1(t):
            h = t // 4
            if t % 4:
                return
            for c in range(2):
                b = d["q", h, c]
                d["qt", h, c] = evc(QA[:, h % 2, c, :], b.t[:, :], [d["qe", h], d.get(("s", 4 * h - 5))] + (t0 if t == 0 else []))
                b.free = [d["qt", h, c]]

        def a2(t):
            h, i = t // 4, t % 4
            n = 128 * (i + 1)
            sl = slice(64 * (h % 2), 64 * (h % 2) + 64)
            qa = QA[:, h % 2, :, :]
            s = d["sb", t] = bank()
            mm(s.t[:, 0:n], qa[:, 0, i * 128:n], CKT[:, 0, 0:n], True, False, [d["qt", h, 0], d["qt", h, 1]] + s.free)
            mm(s.t[:, 0:n], qa[:, 1, i * 128:n], CKT[:, 1, 0:n], False, False)
            mm(s.t[:, 0:n], QRT[sl, h // 2, i * 128:n], KRT[sl, 0:n], False, False)
            if i < 1:
                mm(s.t[:, n - 128:n], ident, cst("cmask"), False, True)
            else:
                mm(s.t[:, 0:n], ident, MADD[:, i - 1, 0:n], False, True)
            d["s", t] = E()

        def a3(t):
            n = 128 * (t % 4 + 1)
            rs, s = RS[:, t % 8, :], d["sb", t]
            red(rs[:, 0:1], s.t[:, 0:n], ALU.max, neg=True, after=[d["s", t]])
            ts(rs[:, 0:1], rs[:, 0:1], SC, None, ALU.mult)
            act(PP[:, t % 3, 0:n], s.t[:, 0:n], ACT.Exp, bias=rs[:, 0:1], scale=SC, accum=rs[:, 1:2],
                after=[D(), d.get(("tr", t - 3))])
            s.free = [A()]
            d["x", t] = A()

        def a4(t):
            n = 128 * (t % 4 + 1)
            rs, pp = RS[:, t % 8, :], PP[:, t % 3, 0:n]
            recip(rs[:, 2:3], rs[:, 1:2], after=[d["x", t]])
            ts(pp, pp, rs[:, 2:3], None, ALU.mult)
            d["n", t] = D()

        def a5(t):
            b = d["t", t] = bank()
            for k in range(t % 4 + 1):
                tr(b.t[:, k * 128:(k + 1) * 128], PP[:, t % 3, k * 128:(k + 1) * 128], [d["n", t]] + b.free)
            d["tr", t] = E()

        def a6(t):
            h, i = t // 4, t % 4
            n = 128 * (i + 1)
            b = d["t", t]
            d["c", t] = evc(PTs[h % 2][:, 0:i + 1, i * 128:n], b.t[:, 0:n].rearrange("p (k t) -> p k t", t=128),
                            [d["tr", t], d.get(("ol", h - 2))])
            b.free = [d["c", t]]

        def a7(t):
            h = t // 4
            if t % 4 < 3:
                return
            for c in range(2):
                b = d["l", h, c] = bank()
                for k in range(4):
                    mm(b.t[:, 128 * k:512], CKV[:, k, c * 128:(c + 1) * 128], PTs[h % 2][:, k, 128 * k:512], k == 0, k == 3,
                       [d["c", 4 * h + x] for x in range(4)] + b.free)
            d["ol", h] = E()

        def a8(t):
            h = t // 4
            if t % 4 < 3:
                return
            for c in range(2):
                b = d["l", h, c]
                d["lt", h, c] = evc(OL[:, h % 2, c, :], b.t[:, :], [d["ol", h], d.get(("v", h - 2))])
                b.free = [d["lt", h, c]]

        def a9(t):
            h = t // 4
            if t % 4 < 3:
                return
            b = d["vb", h] = bank()
            for c in range(2):
                mm(b.t[:, :], uv[:, c, h * 128:(h + 1) * 128], OL[:, h % 2, c, :], c == 0, c == 1,
                   [vtok, d["lt", h, 0], d["lt", h, 1]] + b.free)
            d["v", h] = E()

        def a10(t):
            h = t // 4
            if t % 4 < 3:
                return
            put(H, h, d["vb", h].t[:, :], [d["v", h]])
            d["vb", h].free = [D()]
        pipe(32, [a0, a1, a2, a3, a4, a5, a6, a7, a8, a9, a10])
        release(kslot, [E()])
        release(vslot, [E()])
        mark("o_out")
        low([E(), A(), D()])
        st["ht"] = AD()
        lin(H, 8, "o_out", 0, 512, False, res_add(ALPHA, None, 0), HT)
        lin(H, 8, "o_out", 512, 512, False, res_add(ALPHA, None, 512))

    def rms_x(tmp, xn):
        r = SM[:, 20:24]
        for j in range(4):
            act(tmp, X[:, j, :], ACT.Square, accum=r[:, j:j + 1], after=[D()] if j == 0 else [])
        ts(r, r, 1.0 / 1024, 1e-6, ALU.mult, ALU.add, after=[A()])
        pw(r)
        t0 = D()
        for j in range(4):
            if j % 2:
                act(xn[:, j, :], X[:, j, :], ACT.Copy, scale=r[:, j:j + 1], after=[t0])
                st["xt", j] = [A()]
            else:
                ts(xn[:, j, :], X[:, j, :], r[:, j:j + 1], None, ALU.mult)
                st["xt", j] = [D()]

    def rms_to_fm(gain):
        ar = Arena()
        tmp = ar.take(1024)
        xn = ar.take(4, 1024)
        act(SM[:, 200:201], SM[:, 201:202], ACT.Copy, after=[E(), D()])
        rms_x(tmp, xn)
        x_to_fm(xn, H, gain)

    def ffn(l, which):
        mark(f"ffn{which}_{l}")
        prime(f"fgu{which}_{l}", 8, 0, 512)
        rms_to_fm(cst("nf1" if which == 1 else "nf2")[:, 8 * l:8 * l + 8])
        U, tmp = hidden()
        utok = [None, None]
        tiles = (8, 8, 6)

        def up(p):
            for c in range(tiles[p] // 2):
                def ev(m, ps, c=c):
                    t = tmp[:, m % 2, :]
                    if m < 2:
                        act(t, ps[:, :], ACT.Silu, after=[E(), D()])
                        return
                    tt(t, t, ps[:, :], ALU.mult, after=[E(), A()])
                    put(U[p % 2], c * 2 + m - 2, t)
                    utok[p % 2] = AD()
                lin(H, 8, f"fgu{which}_{l}", (4 * p + c) * 512, 512, True, ev, HT)

        def down(p):
            for c in range(2):
                lin_down(f"fd{which}_{l}", U[p % 2], tiles[p], 8 * p, c, res_add(None, 0.5, c * 512),
                         lambda: utok[p % 2])
        up(0)
        for p in range(3):
            if p < 2:
                up(p + 1)
            down(p)
        dump(f"f{which}_{l}", X[:, :, :], [128, 4, 1024])

    def hybrid(l):
        key = f"win_{l}"
        mark(f"hyb{l}_lin")
        prime(f"win_{l}", 8, 0, 512)
        rms_to_fm(cst("nmix")[:, 8 * l:8 * l + 8])
        ar = Arena()
        GD = ar.take(12, 512)
        GZ = ar.take(4, 512)
        HQ = ar.take(2, 512)
        HK = ar.take(2, 512)
        CUM = ar.take(2, 512)
        HI = ar.take(4, 256)
        HG = ar.take(4, 256)
        XC = ar.take(2, 512)
        RG = ar.take(2, 512)
        GROW = ar.take(2, 512)
        base = ar.o
        raw = ar.take(2, 516)
        acc = ar.take(512)
        LB = SM[:, 120:124]
        start_act = [E(), D(), A()]
        P.op("pool", lambda e: e.memset(raw[:, :, 0:3], 0.0), [E(), D(), A()])
        g0 = G()
        if l == 0:
            P.op("dve", lambda e: e.memset(LB[:, 0:2], 0.0))
        else:
            hl = cst("hlb")
            s = SM[:, 124:140]
            tt(s[:, 0:2], hl[:, 0:2], hl[:, 2:4], ALU.max)
            tt(s[:, 2:4], hl[:, 0:2], s[:, 0:2], ALU.subtract)
            tt(s[:, 4:6], hl[:, 2:4], s[:, 0:2], ALU.subtract)
            act(s[:, 2:6], s[:, 2:6], ACT.Exp, after=[D()])
            tt(s[:, 6:8], s[:, 2:4], s[:, 4:6], ALU.add, after=[A()])
            recip(s[:, 6:8], s[:, 6:8])
            tt(s[:, 8:10], s[:, 2:4], s[:, 6:8], ALU.mult)
            tt(s[:, 10:12], s[:, 4:6], s[:, 6:8], ALU.mult)
            tt(s[:, 12:14], s[:, 8:10], s[:, 10:12], ALU.add)
            tt(LB[:, 0:2], s[:, 12:14], s[:, 8:10], ALU.subtract)
        ts(LB[:, 2:4], LB[:, 0:2], -1.0, 1.0, ALU.mult, ALU.add)

        def ev_hg(m, ps):
            if m < 2:
                act(HQ[:, m, :], ps[:, :], ACT.Silu, after=[E(), D()])
                ts(HQ[:, m, :], HQ[:, m, :], 64.0 ** -0.5, None, ALU.mult, after=[A()])
            else:
                m -= 2
                act(HK[:, m, :], ps[:, :], ACT.Sigmoid, after=[E(), D()])
                ts(CUM[:, m, :], HK[:, m, :], LB[:, 2 + m:3 + m], LB[:, m:m + 1], ALU.mult, ALU.add, after=[A()])
                ts(HK[:, m, :], CUM[:, m, :], -1.0, 1.0, ALU.mult, ALU.add)
                ts(CUM[:, m, :], CUM[:, m, :], 6.0e-20, None, ALU.max)
        lin(H, 8, key, 0, 512, True, ev_hg, HT)
        gconv = cst("gconv")[:, 48 * l:48 * l + 48]
        rconv = cst("rconv")[:, 8 * l:8 * l + 8]

        cv = {"silu": None}

        def conv_silu():
            if cv["silu"] is not None:
                dst, tok = cv["silu"]
                cv["silu"] = None
                act(dst, dst, ACT.Silu, after=[tok])

        def conv_to(dst, ps, w, t, fin):
            r = raw[:, t % 2, :]
            act(r[:, 3:515], ps[:, :], ACT.Copy, after=[E(), cv.get(t % 2), g0])
            a0 = A()
            conv_silu()
            ts(dst, r[:, 0:512], w[:, 0:1], None, ALU.mult, after=[a0])
            for j in range(1, 4):
                stt(dst, r[:, j:j + 512], w[:, j:j + 1], dst, ALU.mult, ALU.add)
            cv[t % 2] = D()
            if fin is None:
                cv["silu"] = (dst, D())
            else:
                ts(dst, dst, fin, None, ALU.add)
        for c in range(3):
            lin(H, 8, key, 512 + c * 512, 512, True,
                lambda m, ps, c=c: conv_to(GD[:, c * 4 + m, :], ps, gconv[:, (c * 4 + m) * 4:(c * 4 + m) * 4 + 4], m, None),
                HT)

        def ev_rg(m, ps):
            if m < 2:
                conv_to(XC[:, m, :], ps, rconv[:, m * 4:m * 4 + 4], m, cst("rconvb")[:, 2 * l + m:2 * l + m + 1])
            else:
                conv_silu()
                act(RG[:, m - 2, :], ps[:, :], ACT.Gelu_apprx_tanh, after=[E(), D()])
        lin(H, 8, key, 2048, 512, True, ev_rg, HT)

        LA, IG = GZ[:, 0:2, :], GZ[:, 2:4, :]
        TA, TBf = Arena(base).take(2, 512), GROW
        lam = cst("rlam")[:, 2 * l:2 * l + 2]
        s = SM[:, 144:148]

        def gates(m):
            if m == 0:
                stt(s[:, 0:2], lam, -1.0, lam, ALU.mult, ALU.max)
                act(s[:, 0:2], s[:, 0:2], ACT.Exp, scale=-1.0, after=[D()])
                act(s[:, 0:2], s[:, 0:2], ACT.Ln, bias=ones[:, 0:1])
                ts(s[:, 2:4], lam, -1.0, 0.0, ALU.mult, ALU.max, after=[A()])
                tt(s[:, 0:2], s[:, 0:2], s[:, 2:4], ALU.add)
                ts(s[:, 0:2], s[:, 0:2], -8.0, None, ALU.mult)
                cv["w"] = load(f"rgw_{l}", 0, 1, 0, 512)
            w, tok, slot = cv["w"]
            for q, dst, bias in ((0, LA, "rbr"), (1, IG, "rbi")):
                b = bank()
                mm(b.t[:, :], w[:, 0, (2 * q + m) * 128:(2 * q + m + 1) * 128], XC[:, m, :], True, True,
                   [tok] + AD() + b.free)
                act(dst[:, m, :], b.t[:, :], ACT.Sigmoid, bias=cst(bias)[:, 2 * l + m:2 * l + m + 1], after=[E(), D()])
                b.free = AD()
            ts(LA[:, m, :], LA[:, m, :], s[:, m:m + 1], None, ALU.mult, after=[A()])
            if m == 1:
                release(slot, [E()])

        def lru0():
            act(TA, LA, ACT.Tanh, scale=-1.0, after=[D()])
            act(LA, LA, ACT.Exp)
            ts(TBf, TA, 1.0, None, ALU.add, after=[A()])
            recip(TBf, TBf)
            stt(TA, TA, 2.0, TBf, ALU.mult, ALU.mult)
            act(TA, TA, ACT.Sqrt, after=[D()])

        def lru1():
            tt(IG, IG, XC, ALU.mult, after=[E()])
            tt(IG, IG, TA, ALU.mult, after=[A()])
            for m in range(2):
                scan(TBf[:, m, :], LA[:, m, :], IG[:, m, :], 0.0, ALU.mult, ALU.add)
                tt(XC[:, m, :], TBf[:, m, :], RG[:, m, :], ALU.mult)
        P.late = [lambda: gates(0), lambda: gates(1), lru0, lru1]

        def ev_ig(m, ps):
            vcp(HI[:, m, :], ps[:, 0:256], [E()])
            act(HG[:, m, :], ps[:, 256:512], ACT.Silu, after=[E(), D()])
        lin(H, 8, key, 2560, 512, False, ev_ig, HT)
        assert not P.late
        bg = bank()
        for k0, c, hi, lo, w_, tok in ahead(pieces(key, 8, 3584, 8)):
            for m in range(4):
                for k in range(c):
                    kk = k0 + k
                    ms = slice(m * 128, (m + 1) * 128)
                    mm3(bg.t[:, m * 8:m * 8 + 8], (H[0][:, kk, ms], H[1][:, kk, ms]), (hi[:, k, :], lo[:, k, :]),
                        kk == 0 and m == 0, kk == 7, [tok] + bg.free)
            w_[1] = [E()]
        P.hold = True
        bg_done = E()
        P.hold = False
        GC = SM[:, 164:196].rearrange("p (m g) -> p m g", m=4)

        def rows0():
            vcp(SM[:, 164:196], bg.t[:, 0:32], [bg_done])
            bg.free = [D()]
            cv["gc"] = D()

        def rows_t():
            for i in range(2):
                b = cv["row", i] = bank()
                for m in range(4):
                    tr(b.t[0:4, m * 128:(m + 1) * 128], GC[:, m, 4 * i:4 * i + 4], [cv["gc"]] + b.free)
            cv["rows"] = E()
            act(GROW[0:4, 0, :], cv["row", 0].t[0:4, :], ACT.Sigmoid, after=[cv["rows"], D()])
            cv["row", 0].free = [A()]

        def rows1():
            b, r, t3 = cv["row", 1], GROW[0:4, 1, :], acc[0:4, :]
            ts(r, b.t[0:4, :], cst("gdt")[0:4, l:l + 1], None, ALU.add, after=[cv["rows"], A()])
            b.free = [D()]
            stt(t3, r, -1.0, r, ALU.mult, ALU.max)
            act(t3, t3, ACT.Exp, scale=-1.0, after=[D()])
            act(t3, t3, ACT.Ln, bias=ones[0:4, 0:1])
            act(SM[0:4, 142:143], cst("galog")[0:4, l:l + 1], ACT.Exp)

        def rows2():
            r, t3 = GROW[0:4, 1, :], acc[0:4, :]
            stt(t3, r, 0.0, t3, ALU.max, ALU.add, [A()])
            ts(t3, t3, SM[0:4, 142:143], -1.0, ALU.mult, ALU.mult)
            for j in range(4):
                scan(r[:, j * 128:(j + 1) * 128], bc(ones[0:4, 0:1], [4, 128]), t3[:, j * 128:(j + 1) * 128], 0.0,
                     ALU.mult, ALU.add)
        P.late = [rows0, rows_t, rows1, rows2]
        lin(H, 8, key, 3072, 512, False, lambda m, ps: act(GZ[:, m, :], ps[:, :], ACT.Silu, after=[E(), D()]), HT)
        assert not P.late

        mark("rg")
        for m in range(2):
            put(H, 6 + m, XC[:, m, :], [E()])

        mark("hg")
        ar.at(WS)
        XL = ar.take(2, 512)
        DF = ar.take(2, 512)
        QD = XC
        KDc = RG
        act(CUM, CUM, ACT.Ln, after=[D()])
        vcp(DF, CUM, [A(), E()])
        for m in range(2):
            for j in range(4):
                scan(CUM[:, m, j * 128:(j + 1) * 128], bc(ones[:, 0:1], [128, 128]), DF[:, m, j * 128:(j + 1) * 128], 0.0,
                     ALU.mult, ALU.add)
        dump(f"cum_{l}", CUM, [128, 2, 512])
        ET = SM[:, 150:158].rearrange("p (m j) -> p m j", m=2)
        act(ET, CUM.rearrange("p m (j t) -> p m j t", t=128)[:, :, :, 127], ACT.Exp, after=[D()])
        ST = [ar.take(10, 128) for _ in range(3)] + [Arena(base).take(10, 128)]
        for sv in ST:
            P.op("pool", lambda e, sv=sv: e.memset(sv, 0.0), [E(), D(), A()])
        act(QD, CUM, ACT.Exp, after=[D(), E()])
        tt(QD, QD, HQ, ALU.mult, after=[A()])
        for m in range(2):
            for j in range(4):
                t0 = slice(j * 128, (j + 1) * 128)
                ts(KDc[:, m, t0], CUM[:, m, t0], CUM[:, m, j * 128 + 127:j * 128 + 128], None, ALU.subtract)
        act(KDc, KDc, ACT.Exp, scale=-1.0, after=[D()])
        tt(KDc, KDc, HK, ALU.mult, after=[A()])
        hsl = lambda h: slice(64 * (h % 2), 64 * (h % 2) + 64)
        at = lambda i, j: j if i == j else 4 + j * (j - 1) // 2 + i
        for j in range(1, 4):
            kt = AD() + [G()]
            for h in range(4):
                b = bank()
                for i in range(j):
                    mm(b.t[:, i * 128:(i + 1) * 128], KDc[hsl(h), h // 2, i * 128:(i + 1) * 128],
                       QD[hsl(h), h // 2, j * 128:(j + 1) * 128], True, True, kt + b.free)
                b.free = [evc(ST[h][:, at(0, j):at(0, j) + j, :], b.t[:, 0:j * 128].rearrange("p (k t) -> p k t", t=128),
                              [E()] + kt)]
            if j < 3:
                for m in range(2):
                    ts(KDc[:, m, 0:j * 128], KDc[:, m, 0:j * 128], ET[:, m, j:j + 1], None, ALU.mult, after=[E(), A()])
        lev = cst("lev")
        XLs, DFs = [XL, XC], [DF, RG]
        d = {}
        nbv = lambda t, Bs: t.rearrange("p m (n b) -> p (m n) b", b=2 * Bs)
        tks = AD() + [E()]

        def h0(lv):
            if lv == 7:
                return
            Bs = 1 << lv
            dv_, cv = nbv(DFs[lv % 2], Bs), nbv(CUM, Bs)
            r = bc(cv[:, :, Bs - 1:Bs], [128, 512 // Bs, Bs])
            tt(dv_[:, :, Bs:2 * Bs], cv[:, :, Bs:2 * Bs], r, ALU.subtract, after=tks)
            tt(dv_[:, :, 0:Bs], r, cv[:, :, 0:Bs], ALU.subtract)
            d["0", lv] = D()

        def h1(lv):
            if lv < 7:
                act(DFs[lv % 2], DFs[lv % 2], ACT.Exp, after=[d["0", lv]])
                d["1", lv] = A()

        def h2(lv):
            if lv == 7:
                return
            Bs = 1 << lv
            xv, dv_, qv, kv = (nbv(t, Bs) for t in (XLs[lv % 2], DFs[lv % 2], HQ, HK))
            tt(xv[:, :, Bs:2 * Bs], dv_[:, :, Bs:2 * Bs], qv[:, :, Bs:2 * Bs], ALU.mult, after=[d["1", lv], d.get(("3", lv - 2))])
            tt(xv[:, :, 0:Bs], dv_[:, :, 0:Bs], kv[:, :, 0:Bs], ALU.mult)
            d["2", lv] = D()

        def h3(lv):
            L_, R_ = (XLs[lv % 2],) * 2 if lv < 7 else (HK, HQ)
            for h in range(4):
                b = d["b", lv, h] = bank()
                for j in range(4):
                    t0 = slice(j * 128, (j + 1) * 128)
                    mm(b.t[:, t0], L_[hsl(h), h // 2, t0], R_[hsl(h), h // 2, t0], True, True, [d.get(("2", lv))] + b.free)
                d["e", lv, h] = E()
            d["3", lv] = E()

        def h4(lv):
            mk = bc(lev[:, lv * 128:(lv + 1) * 128].bitcast(I32).unsqueeze(1), [128, 4, 128])
            for h in range(4):
                b = d["b", lv, h]
                P.op("dve", lambda e, o=ST[h][:, 0:4, :], v=b.t[:, :].rearrange("p (j t) -> p j t", j=4):
                     e.copy_predicated(o, mk, v), [d["e", lv, h]])
                b.free = [D()]
        pipe(8, [h0, h1, h2, h3, h4])
        OH = DF.rearrange("p a b -> p (a b)").rearrange("p (j c) -> p j c", j=4)
        SQ = XL.rearrange("p a b -> p (a b)").rearrange("p (j c) -> p j c", j=4)
        hnw = cst("hnw")[:, 64 * l:64 * l + 64]
        tks = AD() + [E()]
        SSH = SM[:, 64:80].rearrange("p (j h) -> p j h", j=4)

        def g0_(j):
            b = d["b", j] = bank()
            for h in range(4):
                for i in range(j + 1):
                    mm(b.t[:, h * 64:(h + 1) * 64], ST[h][:, at(i, j), :], HI[:, i, h * 64:(h + 1) * 64],
                       i == 0, i == j, tks + b.free)
            d["e", j] = E()

        def g1_(j):
            b = d["b", j]
            act(SQ[:, j, :], b.t[:, 0:256], ACT.Square, after=[d["e", j]] + tks)
            o3 = OH[:, j, :].rearrange("p (h c) -> p h c", h=4)
            tt(o3, b.t[:, 0:256].rearrange("p (h c) -> p h c", h=4), bc(hnw.unsqueeze(1), [128, 4, 64]), ALU.mult,
               after=[A()])
            b.free = [D()]
            red(SSH[:, j, :], SQ[:, j, :].rearrange("p (h c) -> p h c", h=4), ALU.add)
            tt(OH[:, j, :], OH[:, j, :], HG[:, j, :], ALU.mult)
        pipe(4, [g0_, g1_])
        rsq(SSH, SSH, 1.0 / 64, 1e-6)
        for j in range(4):
            o3 = OH[:, j, :].rearrange("p (h c) -> p h c", h=4)
            tt(o3, o3, bc(SSH[:, j, :].unsqueeze(2), [128, 4, 64]), ALU.mult)
        to_fm(OH, H, 2, after=[D(), E()])

        mark("gd")
        hq_off = UP + 16 * 512
        ar.at(hq_off)
        KT_ = ar.take(4, 512)
        VT_ = ar.take(4, 512)
        SCT = ar.take(4, 512)
        CB = ar.take(512)
        BB = ar.take(512)
        assert ar.o <= base - 2 * 512
        ar.at(WS)
        XI = ar.take(4, 512)
        XT = ar.take(4, 512)
        LT = ar.take(4, 512)
        ar.at(base)
        TM = ar.take(512)
        RL_ = ar.take(512)
        LT2 = ar.take(4, 16)
        scT = lambda h: SCT[:, h, :]
        gcol = SM[:, 164:196].rearrange("p (a j h) -> p a j h", a=2, j=4)
        b = bank()
        for a_ in range(2):
            for j in range(4):
                tr(b.t[:, (a_ * 4 + j) * 4:(a_ * 4 + j) * 4 + 4], GROW[0:4, a_, j * 128:(j + 1) * 128], AD() + b.free)
        vcp(SM[:, 164:196], b.t[:, 0:32], [E()])
        b.free = AD()
        t0s = [slice(j * 128, (j + 1) * 128) for j in range(4)]
        by4 = lambda ap: ap.rearrange("p (j t) -> p j t", j=4)
        CBh, BBh = [XI[:, h, :] for h in range(4)], [XT[:, h, :] for h in range(4)]
        tks = AD() + [E()]
        d = {}

        def p0(t):
            b = d["b", t] = bank()
            mm(b.t[:, :], sel[0:4, t // 2 * 128:(t // 2 + 1) * 128], GROW[0:4, 1 - t % 2, :], True, True, tks + b.free)
            d["e", t] = E()

        def p1(t):
            b = d["b", t]
            b.free = [evc((CBh, BBh)[t % 2][t // 2], b.t[:, :], [d["e", t]] + tks)]
        pipe(8, [p0, p1])
        TMS = [LT[:, h, :] for h in range(4)] + [TM, RL_]

        def q0(t):
            act(TMS[t % 6], GD[:, t, :], ACT.Square, after=[d.get(("q5", t - 6))])
            d["q0", t] = A()

        def q1(t):
            b = d["b", t] = bank()
            mm(b.t[:, :], ones, TMS[t % 6], True, True, [d["q0", t]] + b.free)
            d["q1", t] = E()

        def q2(t):
            ts(TMS[t % 6], d["b", t].t[:, :], 1e-6, None, ALU.add, after=[d["q1", t]])
            d["b", t].free = [D()]
            d["q2", t] = D()

        def q3(t):
            act(TMS[t % 6], TMS[t % 6], ACT.Sqrt, after=[d["q2", t]])
            d["q3", t] = A()

        def q4(t):
            recip(TMS[t % 6], TMS[t % 6], after=[d["q3", t]])
            stt(GD[:, t, :], GD[:, t, :], 128.0 ** -0.5 if t < 4 else 1.0, TMS[t % 6], ALU.mult, ALU.mult)
            d["q5", t] = D()
        pipe(8, [q0, q1, q2, q3, q4])
        tks = AD()

        def r0(t):
            b = d["b", t] = bank()
            for j in range(4):
                tr(b.t[:, t0s[j]], GD[:, 4 + t, t0s[j]], tks + b.free)
            d["e", t] = E()

        def r1(t):
            b = d["b", t]
            b.free = [evc(KT_[:, t, :] if t < 4 else VT_[:, t - 4, :], b.t[:, :], [d["e", t]])]
        pipe(8, [r0, r1])
        tks = AD()

        def s0(h):
            for j in range(4):
                ts(LT[:, h, t0s[j]], CBh[h][:, t0s[j]], gcol[:, 1, j, h:h + 1], 0.0, ALU.subtract, ALU.min)
            d["s0", h] = D()
            act((TM, RL_)[h % 2], CBh[h], ACT.Exp, after=[d.get(("s2", h - 2))] + tks)
            d["x", h] = A()

        def s1(h):
            act(LT[:, h, :], LT[:, h, :], ACT.Exp, after=[d["s0", h]])
            d["s1", h] = A()
            for x, o in (("a", h), ("k", 4 + h)):
                b = d[x, h] = bank()
                for j in range(4):
                    mm(b.t[:, t0s[j]], GD[:, 4 + h, t0s[j]], GD[:, o, t0s[j]], True, True, tks + b.free)
            d["e", h] = E()

        def s2(h):
            lt = LT[:, h, :]
            tt(by4(lt), by4(lt), bc(cst("tmask").unsqueeze(1), [128, 4, 128]), ALU.mult, after=[d["s1", h]])
            tt(scT(h), d["a", h].t[:, :], lt, ALU.mult, after=[d["e", h]])
            d["a", h].free = [D()]
            tt(lt, lt, BBh[h], ALU.mult)
            tt(lt, d["k", h].t[:, :], lt, ALU.mult)
            d["k", h].free = [D()]
            tt(GD[:, h, :], GD[:, h, :], (TM, RL_)[h % 2], ALU.mult, after=[d["x", h]])
            d["s2", h] = D()
        pipe(4, [s0, s1, s2])
        cumc, betac = gcol[:, 1, :, :], gcol[:, 0, :, :]
        EC, EL, EX = (LT2[:, x, :].rearrange("p (j h) -> p j h", j=4) for x in range(3))
        for h in range(4):
            vcp(EX[:, :, h], by4(CBh[h])[:, :, 127])
        tt(EL, EX, cumc, ALU.subtract)
        act(EC, cumc, ACT.Exp, after=[D()])
        act(EL, EL, ACT.Exp)
        act(EX, EX, ACT.Exp)
        tt(EC, EC, betac, ALU.mult, after=[A()])
        for h in range(4):
            w3 = lambda ap: bc(ap[:, :, h].unsqueeze(2), [128, 4, 128])
            tt(by4(VT_[:, h, :]), by4(VT_[:, h, :]), w3(betac), ALU.mult)
            tt(by4(GD[:, 8 + h, :]), by4(KT_[:, h, :]), w3(EC), ALU.mult, after=[E()])
            tt(by4(KT_[:, h, :]), by4(KT_[:, h, :]), w3(EL), ALU.mult)
        for h in range(4):
            vcp(by4(XI[:, h, :]), bc(ident.unsqueeze(1), [128, 4, 128]))
            vcp(by4(XT[:, h, :]), bc(ident.unsqueeze(1), [128, 4, 128]))
        mark("gd_inv")
        CTs = [CB, BB]
        P1s = [TM, RL_]
        for h in range(4):
            d["xi", h] = D()

        def v0(t):
            lv, h = t // 4, t % 4
            tt(by4(CTs[t % 2]), by4(LT[:, h, :]), bc(lev[:, lv * 128:(lv + 1) * 128].unsqueeze(1), [128, 4, 128]), ALU.mult,
               after=[d.get(("v1", t - 2))] + (AD() if t < 2 else []))
            d["v0", t] = D()

        def v1(t):
            lv, h = t // 4, t % 4
            b = d["b", t] = bank()
            for t0 in t0s:
                mm(b.t[:, t0], CTs[t % 2][:, t0], XI[:, h, t0], True, True, [d["v0", t], d["xi", h]] + b.free)
            d["v1", t] = E()

        def v2(t):
            act(P1s[t % 2], d["b", t].t[:, :], ACT.Copy, after=[d["v1", t], d.get(("v3", t - 2))] + ([D()] if t < 2 else []))
            d["b", t].free = [A()]
            d["v2", t] = A()

        def v3(t):
            lv, h = t // 4, t % 4
            p1 = P1s[t % 2]
            b = d["x", t] = bank()
            for t0 in t0s:
                mm(b.t[:, t0], p1[:, t0], XT[:, h, t0], True, True, [d["v2", t]] + b.free)
            if lv < 6:
                b2 = d["y", t] = bank()
                for t0 in t0s:
                    mm(b2.t[:, t0], XT[:, h, t0], p1[:, t0], True, True, b2.free)
            d["v3", t] = E()

        def v4(t):
            lv, h = t // 4, t % 4
            if lv < 6:
                tt(XI[:, h, :], XI[:, h, :], d["y", t].t[:, :], ALU.subtract, after=[d["v3", t]])
                d["y", t].free = [D()]
            tt(XT[:, h, :], XT[:, h, :], d["x", t].t[:, :], ALU.subtract, after=[d["v3", t]])
            d["x", t].free = [D()]
            d["xi", h] = D()
        pipe(28, [v0, v1, v2, v3, v4])
        dump(f"xt_{l}", XT, [128, 4, 512])
        mark("gd_chain")
        for h in range(4):
            b = bank()
            for t0 in t0s:
                mm(b.t[:, t0], GD[:, 8 + h, t0], XT[:, h, t0], True, True, AD() + b.free)
            ts(XI[:, h, :], b.t[:, :], -1.0, None, ALU.mult, after=[E()])
            b.free = AD()
        SS = [LT[:, h, 0:128] for h in range(4)]
        VN = [LT[:, h, 128:256] for h in range(4)]
        SQ2 = [LT[:, h, 256:384] for h in range(4)]
        OG = GD[:, 4:8, :]
        gnw = cst("gnw")[:, 128 * l:128 * l + 128]
        SS2 = LT2[:, 3, :].rearrange("p (j h) -> p j h", j=4)
        tks = AD()
        for h in range(4):
            d["S", h] = None

        def c0(t):
            j, h = t // 4, t % 4
            b = d["b", t] = bank()
            mm(b.t[:, 0:128], XT[:, h, t0s[j]], VT_[:, h, t0s[j]], True, j == 0, tks + b.free)
            if j:
                mm(b.t[:, 0:128], XI[:, h, t0s[j]], SS[h], False, True, [d["S", h]])
            d["c0", t] = E()

        def c1(t):
            h = t % 4
            act(VN[h], d["b", t].t[:, 0:128], ACT.Copy, after=[d["c0", t], d.get(("c2", t - 4))] + (tks if t < 4 else []))
            d["b", t].free = [A()]
            d["c1", t] = A()

        def c2(t):
            j, h = t // 4, t % 4
            b = d["o", t] = bank()
            if j:
                mm(b.t[:, 0:128], GD[:, h, t0s[j]], SS[h], True, False, b.free)
            mm(b.t[:, 0:128], scT(h)[:, t0s[j]], VN[h], j == 0, True, [d["c1", t]] + b.free)
            if j < 3:
                mm(b.t[:, 128:256], KT_[:, h, t0s[j]], VN[h], True, True)
            d["c2", t] = E()

        def c3(t):
            j, h = t // 4, t % 4
            b = d["o", t]
            if j == 0:
                vcp(SS[h], b.t[:, 128:256], [d["c2", t]])
            elif j < 3:
                stt(SS[h], SS[h], EX[:, j, h:h + 1], b.t[:, 128:256], ALU.mult, ALU.add, [d["c2", t]])
            d["S", h] = D()
            tt(OG[:, j, h * 128:(h + 1) * 128], b.t[:, 0:128], gnw, ALU.mult, after=[d["c2", t]])
            act(SQ2[h], b.t[:, 0:128], ACT.Square, accum=SS2[:, j, h:h + 1], after=[D()])
            b.free = [A()]
        pipe(16, [c0, c1, c2, c3])
        ts(SS2, SS2, 1.0 / 128, 1e-6, ALU.mult, ALU.add, after=[A()])
        pw(SS2)
        for j in range(4):
            og = OG[:, j, :].rearrange("p (h c) -> p h c", h=4)
            tt(og, og, bc(SS2[:, j, :].unsqueeze(2), [128, 4, 128]), ALU.mult)
            tt(OG[:, j, :], OG[:, j, :], GZ[:, j, :], ALU.mult)
        t0 = AD()
        og_t = to_fm(OG, (H[0][:, 2:6, :], H[1][:, 2:6, :]), 4, after=[D(), E()])
        st["ht"] = (t0, t0) + og_t + (t0, t0)
        low([E(), A(), D(), G()])
        mark(f"wo{l}")
        lin(H, 8, f"wo_{l}", 0, 512, False, res_add(None, 1.0, 0), HT)
        lin(H, 8, f"wo_{l}", 512, 512, False, res_add(None, 1.0, 512), HT)
        dump(f"m_{l}", X[:, :, :], [128, 4, 1024])

    even_mixer()
    mlp_ple(0)
    odd_mixer()
    mlp_ple(1)
    for l in range(2):
        ffn(l, 1)
        hybrid(l)
        ffn(l, 2)
    w, tok, slot = load("nfin", 0, 1, 0, 1024)
    P.flush()
    ar = Arena()
    tmp = ar.take(1024)
    xo = ar.take(4, 1024)
    P.op("act", lambda e: e.activation(SM[:, 200:201], SM[:, 201:202], ACT.Copy), [E(), D()])
    rms_x(tmp, xo)
    for j in range(4):
        tt(xo[:, j, :], xo[:, j, :], w[:, 0, :], ALU.mult, after=[tok, A()])
        P.op("sp", lambda e, W, S, j=j: e.dma_start(W["out"][:, j, :], xo[:, j, :]).then_inc(S["out"], 16), [D()])
    return P, stream


def emit(nc, ctx, P, W, n_out):
    S = {e: ctx.enter_context(nc.semaphore("s_" + e)) for e in ("pe", "act", "dve", "pool")}
    for n in ["c", "x", "pos", "out"] + [f"w{i}" for i in range(NS)]:
        S[n] = ctx.enter_context(nc.semaphore("s_" + n))
    block = ctx.enter_context(nc.Block())

    def run(eng, e):
        for fn, waits, inc in P.ops[e]:
            for s, v in waits:
                eng.wait_ge(S[s], v)
            if e == "sp":
                fn(eng, W, S)
            else:
                i = fn(eng)
                if inc:
                    i.then_inc(S[e], 1)

    @block.sync
    def _(eng):
        run(eng, "sp")
        eng.wait_ge(S["out"], 16 * n_out)

    @block.tensor
    def _(eng):
        run(eng, "pe")

    @block.scalar
    def _(eng):
        run(eng, "act")

    @block.vector
    def _(eng):
        run(eng, "dve")

    @block.gpsimd
    def _(eng):
        run(eng, "pool")


def const_block(I):
    f = np.float32
    C = np.zeros((128, NCB), f)

    def put(name, a, rows=128):
        o, w = COFF[name]
        C[:rows, o:o + w] = a.reshape(rows, w)

    def row(a):
        return np.broadcast_to(np.asarray(a).reshape(1, -1), (128, np.asarray(a).size))

    s = np.arange(128)
    put("ident", np.eye(128, dtype=f))
    lev = np.zeros((128, 8, 128), f)
    for lv in range(7):
        B = 1 << lv
        same = (s[:, None] // (2 * B)) == (s[None, :] // (2 * B))
        lev[:, lv, :] = same & ((s[:, None] // B) % 2 == 0) & ((s[None, :] // B) % 2 == 1)
    lev[:, 7, :] = np.eye(128)
    put("lev", lev)
    put("cmask", np.where(s[None, :] <= s[:, None], 0.0, NEG).astype(f))
    put("tmask", (s[:, None] <= s[None, :]).astype(f))
    put("ones", np.ones((128, 128), f))
    sel = np.zeros((128, 4, 128), f)
    for h in range(4):
        sel[h, h, :] = 1
    put("sel", sel)
    t = np.arange(4)[None, :, None] * 128 + s[:, None, None]
    ok = (np.arange(31) * 16 + 31)[None, None, :] <= t
    put("cmpadd", np.where(ok, 0.0, NEG).astype(f))
    put("cmp01", ok.astype(f))
    inv = [np.float32(10000.0) ** (-np.arange(0, d, 2, dtype=f) / np.float32(d)) for d in (64, 32)]
    put("invf", row(np.concatenate(inv).astype(f)))
    put("aconv", I["e_a_conv"][0].reshape(4, 8, 128).transpose(2, 1, 0))
    put("aib", I["e_a_i_b"][0], 4)
    put("afb", I["e_a_f_b"][0], 4)
    put("anorm", row(I["e_a_norm"][0]))
    cp = I["e_b_cmp_pos"][0].transpose(2, 0, 1)
    put("cpos", np.concatenate([cp, cp], 0))
    put("cw2", I["e_b_cmp_w2"][0].transpose(1, 0, 2))
    put("gb", row(I["e_b_g_b"][0]))
    put("qnorm", I["o_q_norm"][0].reshape(4, 128).T)
    put("kvnorm", row(I["o_kv_norm"][0]))
    put("ikg", row(I["o_ik_g"][0]))
    put("ikb", row(I["o_ik_b"][0]))
    for n, k in (("nf1", "norm_ffn1_2"), ("nmix", "norm_mix_2"), ("nf2", "norm_ffn2_2")):
        put(n, I[k].reshape(2, 8, 128).transpose(2, 0, 1))
    for n, k in (("hlb", "hg_lb_2"), ("rconvb", "rg_conv_b_2"), ("rbr", "rg_br_2"), ("rbi", "rg_bi_2"),
                 ("rlam", "rg_lambda_2")):
        put(n, I[k].reshape(2, 2, 128).transpose(2, 0, 1))
    put("hnw", row(I["hg_norm_w_2"]))
    put("gnw", row(I["gd_norm_w_2"]))
    put("gconv", I["gd_conv_w_2"].reshape(2, 4, 12, 128).transpose(3, 0, 2, 1))
    put("rconv", I["rg_conv_w_2"].reshape(2, 4, 2, 128).transpose(3, 0, 2, 1))
    put("galog", I["gd_a_log_2"].T, 4)
    put("gdt", I["gd_dt_bias_2"].T, 4)
    return C


def matrices(I):
    M = {}
    w = I["e_w_in"][0]
    o = np.cumsum([0, 512, 512, 512, 512, 4, 4, 512, 128, 128, 128, 128, 128, 128, 24])
    c = [w[:, o[i]:o[i + 1]] for i in range(14)]
    aq, ak, av, ao, ai, af, bq, bkc, bvc, bks, bvs, bkw, bvw, bg = c
    bq = bq.reshape(1024, 2, 4, 64).transpose(0, 2, 1, 3).reshape(1024, 512)
    M["e_in"] = np.concatenate([aq, ak, bkc, bvc, bks, bkw, bq, av, ao, bvs, bvw, bg, ai, af], 1)
    M["e_out"] = I["e_w_out"][0]
    M["cw1"] = I["e_b_cmp_w1"][0].reshape(2, 16, 128, 128).transpose(0, 2, 1, 3).reshape(256, 2048)
    rep = lambda a: np.broadcast_to(np.concatenate([x.reshape(-1) for x in a])[None, :], (128, sum(x.size for x in a)))
    for l in range(2):
        M[f"ln1_{l}"] = rep([I["ln1_g"][l], I["ln1_b"][l]])
        M[f"ln2_{l}"] = rep([I["ln2_g"][l], I["ln2_b"][l]])
        M[f"w1_{l}"] = I["mlp_w1"][l]
        M[f"w2_{l}"] = I["mlp_w2"][l]
        M[f"pT_{l}"] = I["p"][l, 0].T
        M[f"pgw_{l}"] = I["ple_gate_w"][l]
        M[f"pw_{l}"] = I["ple_w"][l]
    M["o_in"] = I["o_w_in"][0]
    qb = I["o_w_qb"][0].reshape(512, 8, 192)
    M["o_qb"] = np.concatenate([qb[:, :, :128].reshape(512, 1024), qb[:, :, 128:].reshape(512, 512)], 1)
    M["o_iq"] = I["o_w_iq"][0]
    M["o_uk"] = I["o_w_uk"][0].transpose(2, 1, 0).reshape(128, 2048)
    M["o_uv"] = I["o_w_uv"][0].reshape(256, 1024)
    M["o_out"] = I["o_w_out"][0]
    so = np.cumsum([0, 256, 256, 256, 256, 512, 512, 512, 512, 4, 4, 256, 256])
    for l in range(2):
        for n in ("1", "2"):
            g, u = (I[f"ffn{n}_{k}_2"][l].reshape(1024, 11, 256) for k in ("gate", "up"))
            M[f"fgu{n}_{l}"] = np.concatenate([g, u], 2).reshape(1024, 5632)
            M[f"fd{n}_{l}"] = I[f"ffn{n}_down_2"][l]
        w = I["w_in_2"][l]
        hq, hf, hi, hg, gq, gk, gv, gz, gb, ga, rx, rg = [w[:, so[i]:so[i + 1]] for i in range(12)]
        M[f"win_{l}"] = np.concatenate([hq, hf, gq, gk, gv, rx, rg, hi, hg, gz, gb, ga], 1)
        M[f"wo_{l}"] = I["w_out_2"][l]
        r = np.zeros((128, 4, 128), np.float32)
        for q, k in enumerate(("rg_wr_2", "rg_wi_2")):
            for n in range(4):
                p0 = 64 * (n % 2)
                r[p0:p0 + 64, 2 * q + n // 2, p0:p0 + 64] = I[k][l, n]
        M[f"rgw_{l}"] = r.reshape(128, 512)
    M["nfin"] = rep([I["norm_final_2"]])
    return M


def kernel(**inputs):
    import concourse.bacc as _bacc
    from concourse.bass_utils import run_bass_kernel_spmd as _run

    I = {k: np.asarray(v) for k, v in inputs.items()}
    nc = _bacc.Bacc("TRN2", target_bir_lowering=False, num_devices=1)
    with ExitStack() as ctx:
        P, stream = record(nc, ctx)
        M = matrices(I)
        parts, offs, off = [], [], 0
        for key, k0, nk, c0, ncol in stream:
            a = M[key][k0 * 128:(k0 + nk) * 128, c0:c0 + ncol].reshape(nk, 128, ncol).transpose(1, 0, 2)
            parts.append(a.reshape(-1))
            offs.append((off, nk * ncol))
            off += a.size
        arrays = {"wts": np.concatenate(parts), "cb": const_block(I),
                  "x": np.ascontiguousarray(I["x"][0].reshape(4, 128, 1024).transpose(1, 0, 2)),
                  "pos": np.ascontiguousarray(I["positions"][0].reshape(4, 128).T)}
        W = {}
        for n, a in arrays.items():
            t = nc.dram_tensor("in_" + n, a.shape, mybir.dt.from_np(a.dtype), kind="ExternalInput").ap()
            if n == "wts":
                for i, (o, w) in enumerate(offs):
                    W[i] = t[o:o + 128 * w].rearrange("(p n) -> p n", p=128)
            else:
                W[n] = t
        out = nc.dram_tensor("out_0", (1, 512, 1024), F32, kind="ExternalOutput").ap()
        W["out"] = out[0].rearrange("(j p) n -> p j n", p=128)
        emit(nc, ctx, P, W, 4)
    r = _run(nc, [{"in_" + n: a for n, a in arrays.items()}], core_ids=[0])
    return r.results[0]["out_0"]
```
